# Optimizing a Trainium2 kernel written in Bass

```python
import jax, jax.numpy as jnp
from jax import lax
import numpy as np

D_MODEL = 2048
BATCH = 1
SEQ = 256
DEPTH = 1
DEC_BATCH = 8
DEC_SEQ = 1
PAST_LEN = 1024
PAGE_SIZE = 128

M_HEADS = 4
M_DK = 256
M_DV = 256
M_CHUNK = 64
A_HEADS = 16
A_KV_HEADS = 4
A_HEAD_DIM = 64
A_GROUP = A_HEADS // A_KV_HEADS
WINDOW = 128
A_BLOCK = WINDOW
M_QK_W = M_HEADS * M_DK
M_V_W = M_HEADS * M_DV
A_Q_W = A_HEADS * A_HEAD_DIM
A_KV_W = A_KV_HEADS * A_HEAD_DIM
SPLIT_SIZES = (M_QK_W, M_QK_W, M_V_W, M_V_W, M_HEADS, M_HEADS, A_Q_W, A_KV_W, A_KV_W)
IN_COLS = 2 * M_QK_W + 2 * M_V_W + 2 * M_HEADS + A_Q_W + 2 * A_KV_W
MIX_WIDTH = M_V_W + A_Q_W
N_GROUPS = 4
EXPERTS_PER_GROUP = 8
N_EXPERTS = N_GROUPS * EXPERTS_PER_GROUP
TOP_K = 2
D_EXPERT = 512
MOE_BLOCK = 128
PLE_DIM = 256
EPS = 1e-6

kernel_name = 'hymba_mlstm_swa_hmoe_step'

def rmsnorm(x, g):
    xf = x.astype(jnp.float32)
    r = lax.rsqrt(jnp.mean(xf * xf, axis=-1, keepdims=True) + EPS)
    return (xf * r).astype(x.dtype) * g

def split_in(z):
    offs = np.cumsum(np.array(SPLIT_SIZES))[:-1].tolist()
    return jnp.split(z, offs, axis=-1)

def mlstm_prepare(mq, mk, mv, mi, mf, b_i, b_f):
    B, T = mq.shape[:2]
    f32 = jnp.float32
    q = mq.reshape(B, T, M_HEADS, M_DK).transpose(0, 2, 1, 3).astype(f32)
    k = mk.reshape(B, T, M_HEADS, M_DK).transpose(0, 2, 1, 3).astype(f32) * (M_DK ** -0.5)
    v = mv.reshape(B, T, M_HEADS, M_DV).transpose(0, 2, 1, 3).astype(f32)
    i_pre = (mi.astype(f32) + b_i.astype(f32)).transpose(0, 2, 1)
    logf = jax.nn.log_sigmoid(mf.astype(f32) + b_f.astype(f32)).transpose(0, 2, 1)
    return q, k, v, i_pre, logf

def mlstm_chunk(carry, inp):
    c0, n0, m0 = carry
    q, k, v, i_pre, logf = inp
    L = q.shape[2]
    F = jnp.cumsum(logf, axis=-1)
    a = i_pre - F
    m_t = F + jnp.maximum(m0[..., None], lax.cummax(a, axis=2))
    dec0 = jnp.exp(F + m0[..., None] - m_t)
    causal = jnp.tril(jnp.ones((L, L), dtype=bool))
    log_d = (F - m_t)[..., :, None] + a[..., None, :]
    d = jnp.exp(jnp.where(causal, log_d, -jnp.inf))
    w = jnp.einsum('bhtk,bhsk->bhts', q, k) * d
    num = jnp.einsum('bhts,bhsv->bhtv', w, v) + dec0[..., None] * jnp.einsum('bhvk,bhtk->bhtv', c0, q)
    den = jnp.sum(w, axis=-1) + dec0 * jnp.einsum('bhk,bhtk->bht', n0, q)
    h = num / jnp.maximum(jnp.abs(den), jnp.exp(-m_t))[..., None]
    m_end = m_t[..., -1]
    w_end = jnp.exp(F[..., -1:] + a - m_end[..., None])
    dec_end = jnp.exp(F[..., -1] + m0 - m_end)
    c1 = dec_end[..., None, None] * c0 + jnp.einsum('bhs,bhsv,bhsk->bhvk', w_end, v, k)
    n1 = dec_end[..., None] * n0 + jnp.einsum('bhs,bhsk->bhk', w_end, k)
    return (c1, n1, m_end), h

def mlstm_prompt(q, k, v, i_pre, logf):
    B, H, T, _ = q.shape
    nc = T // M_CHUNK

    def to_chunks(a):
        a = a.reshape((B, H, nc, M_CHUNK) + a.shape[3:])
        return jnp.moveaxis(a, 2, 0)

    f32 = jnp.float32
    carry0 = (jnp.zeros((B, H, M_DV, M_DK), f32), jnp.zeros((B, H, M_DK), f32), jnp.zeros((B, H), f32))
    carry, h = lax.scan(mlstm_chunk, carry0, tuple(to_chunks(a) for a in (q, k, v, i_pre, logf)))
    h = jnp.moveaxis(h, 0, 2).reshape(B, H, T, M_DV)
    return h, carry

def mlstm_out(h, mo, g_mh):
    B, H, T, _ = h.shape
    h = h.transpose(0, 2, 1, 3)
    h = h * lax.rsqrt(jnp.mean(h * h, axis=-1, keepdims=True) + EPS)
    h = h.reshape(B, T, M_V_W).astype(mo.dtype) * g_mh
    return h * jax.nn.sigmoid(mo)

def sink_attention(q, k, v, allowed, sinks):
    s = jnp.einsum('...thgd,...khd->...hgtk', q, k).astype(jnp.float32) * (A_HEAD_DIM ** -0.5)
    s = jnp.where(allowed, s, -jnp.inf)
    sink = sinks.astype(jnp.float32).reshape(A_KV_HEADS, A_GROUP, 1, 1)
    mx = jnp.maximum(jnp.max(s, axis=-1, keepdims=True), sink)
    e = jnp.exp(s - mx)
    p = e / (jnp.sum(e, axis=-1, keepdims=True) + jnp.exp(sink - mx))
    return jnp.einsum('...hgtk,...khd->...thgd', p.astype(v.dtype), v)

def swa_prompt(aq, ak, av, sinks):
    B, T, _ = aq.shape
    nb = T // A_BLOCK
    q = aq.reshape(B, nb, A_BLOCK, A_KV_HEADS, A_GROUP, A_HEAD_DIM)
    k = ak.reshape(B, nb, A_BLOCK, A_KV_HEADS, A_HEAD_DIM)
    v = av.reshape(B, nb, A_BLOCK, A_KV_HEADS, A_HEAD_DIM)
    pad = jnp.zeros_like(k[:, :1])
    k2 = jnp.concatenate([jnp.concatenate([pad, k[:, :-1]], axis=1), k], axis=2)
    v2 = jnp.concatenate([jnp.concatenate([pad, v[:, :-1]], axis=1), v], axis=2)
    blk = jnp.arange(nb)[:, None] * A_BLOCK
    qpos = blk + jnp.arange(A_BLOCK)[None, :]
    kpos = blk - A_BLOCK + jnp.arange(2 * A_BLOCK)[None, :]
    diff = qpos[:, :, None] - kpos[:, None, :]
    allowed = (diff >= 0) & (diff < WINDOW) & (kpos[:, None, :] >= 0)
    o = sink_attention(q, k2, v2, allowed[None, :, None, None], sinks)
    kf = ak.reshape(B, T, A_KV_HEADS, A_HEAD_DIM)
    vf = av.reshape(B, T, A_KV_HEADS, A_HEAD_DIM)
    return o.reshape(B, T, A_Q_W), kf[:, -WINDOW:], vf[:, -WINDOW:]

def swa_sample(aq, ak, av, buf_k, buf_v, sinks):
    B, T, _ = aq.shape
    q = aq.reshape(B, T, A_KV_HEADS, A_GROUP, A_HEAD_DIM)
    k_all = jnp.concatenate([buf_k.astype(ak.dtype), ak.reshape(B, T, A_KV_HEADS, A_HEAD_DIM)], axis=1)
    v_all = jnp.concatenate([buf_v.astype(av.dtype), av.reshape(B, T, A_KV_HEADS, A_HEAD_DIM)], axis=1)
    qpos = WINDOW + jnp.arange(T)
    kpos = jnp.arange(WINDOW + T)
    diff = qpos[:, None] - kpos[None, :]
    allowed = (diff >= 0) & (diff < WINDOW)
    o = sink_attention(q, k_all, v_all, allowed, sinks)
    return o.reshape(B, T, A_Q_W), k_all[:, -WINDOW:], v_all[:, -WINDOW:]

def token_mix(x, g_mix, w_in, b_igate, b_fgate, g_mh, attn_sinks, w_out, state):
    h = rmsnorm(x, g_mix)
    mq, mk, mv, mo, mi, mf, aq, ak, av = split_in(h @ w_in)
    q, k, v, ip, lf = mlstm_prepare(mq, mk, mv, mi, mf, b_igate, b_fgate)
    if state is None:
        h_m, (c, n, m) = mlstm_prompt(q, k, v, ip, lf)
        o_a, kw, vw = swa_prompt(aq, ak, av, attn_sinks)
    else:
        c0, n0, m0, kb, vb = state
        f32 = jnp.float32
        (c, n, m), h_m = mlstm_chunk((c0.astype(f32), n0.astype(f32), m0.astype(f32)), (q, k, v, ip, lf))
        o_a, kw, vw = swa_sample(aq, ak, av, kb, vb, attn_sinks)
    o_m = mlstm_out(h_m, mo, g_mh)
    y = x + jnp.concatenate([o_m, o_a], axis=-1) @ w_out
    dt = x.dtype
    return y, (c.astype(dt), n.astype(dt), m.astype(dt), kw, vw)

def hier_moe(h, w_router_g, b_router_g, w_router_e, b_router_e, w_gate, w_up, w_down):
    B, T, D = h.shape
    hf = h.reshape(B * T, D)
    n_tok = B * T
    f32 = jnp.float32
    hr = hf.astype(f32)
    g_logits = hr @ w_router_g.astype(f32) + b_router_g.astype(f32)
    g_probs = jax.nn.softmax(g_logits, axis=-1)
    g_idx = jnp.argmax(g_logits, axis=-1)
    g_w = jnp.take_along_axis(g_probs, g_idx[:, None], axis=-1)
    e_logits = (hr @ w_router_e.astype(f32) + b_router_e.astype(f32)).reshape(n_tok, N_GROUPS, EXPERTS_PER_GROUP)
    e_logits = jnp.take_along_axis(e_logits, g_idx[:, None, None], axis=1)[:, 0]
    top_l, top_i = lax.top_k(e_logits, TOP_K)
    weights = g_w * jax.nn.softmax(top_l, axis=-1)
    expert = g_idx[:, None] * EXPERTS_PER_GROUP + top_i
    n_assign = n_tok * TOP_K
    e_flat = expert.reshape(n_assign)
    tok_flat = jnp.arange(n_assign) // TOP_K
    order = jnp.argsort(e_flat)
    e_sorted = e_flat[order]
    tok_sorted = tok_flat[order]
    w_sorted = weights.reshape(n_assign)[order]
    counts = jnp.bincount(e_flat, length=N_EXPERTS)
    padded = ((counts + MOE_BLOCK - 1) // MOE_BLOCK) * MOE_BLOCK
    pad_end = jnp.cumsum(padded)
    pad_start = pad_end - padded
    start = jnp.cumsum(counts) - counts
    dest = pad_start[e_sorted] + (jnp.arange(n_assign) - start[e_sorted])
    n_rows = (-(-n_assign // MOE_BLOCK) + N_EXPERTS) * MOE_BLOCK
    n_blocks = n_rows // MOE_BLOCK
    x_pad = jnp.zeros((n_rows, D), h.dtype).at[dest].set(hf[tok_sorted])
    block_expert = jnp.minimum(jnp.searchsorted(pad_end, jnp.arange(n_blocks) * MOE_BLOCK, side='right'), N_EXPERTS - 1)

    def expert_block(args):
        xb, e = args
        return (jax.nn.silu(xb @ w_gate[e]) * (xb @ w_up[e])) @ w_down[e]

    y_pad = lax.map(expert_block, (x_pad.reshape(n_blocks, MOE_BLOCK, D), block_expert)).reshape(n_rows, D)
    y = y_pad[dest] * w_sorted[:, None].astype(h.dtype)
    out = jax.ops.segment_sum(y, tok_sorted, num_segments=n_tok)
    return out.reshape(B, T, D)

def channel_mix(x, p_i, g_ffn, w_router_g, b_router_g, w_router_e, b_router_e, w_gate, w_up, w_down,
                g_ple, w_ple_gate, w_ple_proj):
    x = x + hier_moe(rmsnorm(x, g_ffn), w_router_g, b_router_g, w_router_e, b_router_e, w_gate, w_up, w_down)
    gate = jax.nn.sigmoid(rmsnorm(x, g_ple) @ w_ple_gate)
    return x + gate * (p_i.astype(x.dtype) @ w_ple_proj)

def setup_inputs(seed: int = 0) -> dict:
    key = jax.random.key(seed)
    ks = jax.random.split(key, 32)
    f32 = jnp.float32

    def nrm(k, shape, scale):
        return jax.random.normal(k, shape, f32) * scale

    D = D_MODEL
    return {
        'x_prompt': nrm(ks[0], (BATCH, SEQ, D), 1.0),
        'x_sample': nrm(ks[1], (DEC_BATCH, DEC_SEQ, D), 1.0),
        'p_prompt': nrm(ks[2], (DEPTH, BATCH, SEQ, PLE_DIM), 1.0),
        'p_sample': nrm(ks[3], (DEPTH, DEC_BATCH, DEC_SEQ, PLE_DIM), 1.0),
        'state_mlstm_C': nrm(ks[4], (DEPTH, DEC_BATCH, M_HEADS, M_DV, M_DK), 0.1),
        'state_mlstm_n': nrm(ks[5], (DEPTH, DEC_BATCH, M_HEADS, M_DK), 0.5),
        'state_mlstm_m': nrm(ks[6], (DEPTH, DEC_BATCH, M_HEADS), 1.0),
        'state_swa_k': nrm(ks[7], (DEPTH, DEC_BATCH, WINDOW, A_KV_HEADS, A_HEAD_DIM), 1.0),
        'state_swa_v': nrm(ks[8], (DEPTH, DEC_BATCH, WINDOW, A_KV_HEADS, A_HEAD_DIM), 1.0),
        'g_mix': 1.0 + nrm(ks[9], (DEPTH, D), 0.05),
        'w_in': nrm(ks[10], (DEPTH, D, IN_COLS), D ** -0.5),
        'b_igate': nrm(ks[11], (DEPTH, M_HEADS), 0.1),
        'b_fgate': 3.0 + 3.0 * jax.random.uniform(ks[12], (DEPTH, M_HEADS), f32),
        'g_mh': 1.0 + nrm(ks[13], (DEPTH, M_V_W), 0.05),
        'attn_sinks': nrm(ks[14], (DEPTH, A_HEADS), 0.5),
        'w_out': nrm(ks[15], (DEPTH, MIX_WIDTH, D), MIX_WIDTH ** -0.5),
        'g_ffn': 1.0 + nrm(ks[16], (DEPTH, D), 0.05),
        'w_router_g': nrm(ks[17], (DEPTH, D, N_GROUPS), D ** -0.5),
        'b_router_g': nrm(ks[18], (DEPTH, N_GROUPS), 0.01),
        'w_router_e': nrm(ks[19], (DEPTH, D, N_EXPERTS), D ** -0.5),
        'b_router_e': nrm(ks[20], (DEPTH, N_EXPERTS), 0.01),
        'w_gate': nrm(ks[21], (DEPTH, N_EXPERTS, D, D_EXPERT), D ** -0.5),
        'w_up': nrm(ks[22], (DEPTH, N_EXPERTS, D, D_EXPERT), D ** -0.5),
        'w_down': nrm(ks[23], (DEPTH, N_EXPERTS, D_EXPERT, D), D_EXPERT ** -0.5),
        'g_ple': 1.0 + nrm(ks[24], (DEPTH, D), 0.05),
        'w_ple_gate': nrm(ks[25], (DEPTH, D, D), D ** -0.5),
        'w_ple_proj': nrm(ks[26], (DEPTH, PLE_DIM, D), PLE_DIM ** -0.5),
        'g_final': 1.0 + nrm(ks[27], (D,), 0.05),
    }

def reference(x_prompt, x_sample, p_prompt, p_sample, state_mlstm_C, state_mlstm_n, state_mlstm_m,
              state_swa_k, state_swa_v, g_mix, w_in, b_igate, b_fgate, g_mh, attn_sinks, w_out, g_ffn,
              w_router_g, b_router_g, w_router_e, b_router_e, w_gate, w_up, w_down, g_ple, w_ple_gate,
              w_ple_proj, g_final):
    xp, xs = x_prompt, x_sample
    sp = [[], [], [], [], []]
    ss = [[], [], [], [], []]
    for l in range(DEPTH):
        mix_w = (g_mix[l], w_in[l], b_igate[l], b_fgate[l], g_mh[l], attn_sinks[l], w_out[l])
        ch_w = (g_ffn[l], w_router_g[l], b_router_g[l], w_router_e[l], b_router_e[l], w_gate[l], w_up[l],
                w_down[l], g_ple[l], w_ple_gate[l], w_ple_proj[l])
        xp, st_p = token_mix(xp, *mix_w, None)
        xp = channel_mix(xp, p_prompt[l], *ch_w)
        st_in = (state_mlstm_C[l], state_mlstm_n[l], state_mlstm_m[l], state_swa_k[l], state_swa_v[l])
        xs, st_s = token_mix(xs, *mix_w, st_in)
        xs = channel_mix(xs, p_sample[l], *ch_w)
        for j in range(5):
            sp[j].append(st_p[j])
            ss[j].append(st_s[j])
    y_prompt = rmsnorm(xp, g_final)
    y_sample = rmsnorm(xs, g_final)
    return (y_prompt, y_sample,
            jnp.stack(sp[0]), jnp.stack(sp[1]), jnp.stack(sp[2]), jnp.stack(sp[3]), jnp.stack(sp[4]),
            jnp.stack(ss[0]), jnp.stack(ss[1]), jnp.stack(ss[2]), jnp.stack(ss[3]), jnp.stack(ss[4]))


_drawn_inputs = setup_inputs


def setup_inputs(seed=0):
    import zlib

    import numpy as np

    out = dict(_drawn_inputs(seed))
    spreads = {}
    factors = {'attn_sinks': 4.213, 'b_router_g': 3.329, 'b_router_e': 3.255, 'g_ple': 6.6}
    for name, (base, spread) in spreads.items():
        noise = np.random.default_rng([zlib.crc32(name.encode()), seed]).standard_normal(out[name].shape)
        drawn = base * np.exp(spread * noise) if base else spread * noise
        out[name] = __import__('jax').numpy.asarray(drawn.astype(out[name].dtype))
    for name, factor in factors.items():
        out[name] = (out[name] * factor).astype(out[name].dtype)
    return out
```

```python
from contextlib import ExitStack

import numpy as np

import concourse.bass as bass
from concourse import mybir

F32 = mybir.dt.float32
F32R = mybir.dt.float32r
I32 = mybir.dt.int32
ALU = mybir.AluOpType
ACT = mybir.ActivationFunctionType
AX = mybir.AxisListType.X

P = 128
D = 2048
KD = D // P
SEQ, NS = 256, 8
NT = SEQ + NS
TILES = ((0, P), (P, P), (SEQ, NS))
MH, DK = 4, 256
AH, KV, HD = 16, 4, 64
WIN = 128
NG, NE, EPG = 4, 32, 8
DE = 512
PLE = 256
EPS = 1e-6
GW = 512
CK = 4
NCH = KD // CK
SLOTS = 64
PASSES = -(-NT // SLOTS)
RAW = 6
SPL = 4
ECH = 3 * NCH
NONE = 4096.0
BIG = 1.0e30

AQ0, AK0, AV0 = 0, 8, 10
MQ0, MK0, MV0, MO0 = 12, 20, 28, 36
NPT = 44
C_MQ, C_GATES, C_AQ = 0, 4096, 4104


class Counted:

    def __init__(self, sem):
        self.sem, self.n = sem, 0

    def inc(self, ins, by=1):
        ins.then_inc(self.sem, by)
        self.n += by
        return self.n


def chain(engine, counted):

    def link(ins):
        engine.wait_ge(counted.sem, counted.inc(ins))

    return link


class Core:

    def __init__(self, nc, ctx):
        self.nc, self.ctx = nc, ctx
        self.ps = ctx.enter_context(nc.psum_tensor("ps", [P, 8, 512], F32))
        self.act_chain = Counted(self.sem("act_chain"))
        self.dve_chain = Counted(self.sem("dve_chain"))
        self.pool_chain = Counted(self.sem("pool_chain"))
        self.raw_landed = [self.sem(f"raw_landed{i}") for i in range(RAW)]
        self.raw_free = self.sem("raw_free")
        self.raw_groups = 0
        self.landed_base = 0
        self.proj_done = self.sem("proj_done")
        self.proj_copied = self.sem("proj_copied")
        self.proj_groups = 0
        self.norm_runs = 0
        self.turned, self.added = self.sem("turned"), self.sem("added")
        self.turned_banks = 0
        self.norm_sems = [self.sem(f"norm_{n}") for n in
                          "ss_clear squares mean root rows turned stored copied0 copied1".split()]

    def sem(self, name):
        return self.ctx.enter_context(self.nc.semaphore(name))

    def sb(self, name, shape, dt=F32, ctx=None):
        return (ctx or self.ctx).enter_context(self.nc.sbuf_tensor(name, shape, dt))


def weight_group(w, col):
    return w.rearrange("(k p) c -> p k c", p=P)[:, :, col]


def load_groups(core, sp, w, first_col, count):
    base = core.raw_groups
    with sp.Fori(0, count) as g:
        for c in range(NCH):
            sp.wait_ge(core.raw_free, g * NCH + (base * NCH + c + 1))
            src = weight_group(w, bass.ds(g * GW + first_col, GW))[:, c * CK:(c + 1) * CK, :]
            dst = core.raw[:, c, :].rearrange("p (k c) -> p k c", k=CK)
            sp.dma_start(dst, src).then_inc(core.raw_landed[c], 16)


def project_groups(core, pe, xT, count):
    nc, ps = core.nc, core.ps
    base, done = core.raw_groups, core.proj_groups
    with pe.Fori(0, count) as g:
        pe.wait_ge(core.proj_copied, g * 2 + (done * 2 + 2))
        for c in range(NCH):
            pe.wait_ge(core.raw_landed[c], g * 16 + ((base - core.landed_base) * 16 + 16))
            for k in range(CK):
                for j in range(4):
                    last = nc.tensor.matmul(ps[:, j, 0:NT], core.raw[:, c, k * GW + j * P:k * GW + (j + 1) * P],
                                            xT[:, c * CK + k, :], start=(c == 0 and k == 0),
                                            stop=(c == NCH - 1 and k == CK - 1))
            last.then_inc(core.raw_free, 1)
        pe.wait_ge(core.raw_free, g * NCH + (base * NCH + 2 * NCH))
        pe.sem_inc(core.proj_done, 1)


def constants(core, w):
    nc = core.nc
    core.ident = core.sb("ident", [P, P])
    core.ones = core.sb("ones", [P, P])
    core.upper = core.sb("upper", [P, P])
    core.gcols = core.sb("gcols", [P, 56])
    core.eps = core.sb("eps", [P, 1])
    core.grows = core.sb("grows", [56, P])
    core.consts_ready = core.sem("consts_ready")
    core.grows_landed = core.sem("grows_landed")

    with nc.Block() as block:
        @block.gpsimd
        def _(pool):
            link = chain(pool, core.pool_chain)
            link(nc.gpsimd.memset(core.ident[:], 0.0))
            link(nc.gpsimd.memset(core.ones[:], 1.0))
            link(nc.gpsimd.memset(core.eps[:], EPS))
            link(nc.gpsimd.affine_select(out=core.ident[:], in_=core.ident[:], compare_op=ALU.not_equal,
                                         fill=1.0, base=0, pattern=[[-1, P]], channel_multiplier=1))
            link(nc.gpsimd.affine_select(out=core.upper[:], in_=core.ones[:], compare_op=ALU.is_gt,
                                         fill=0.0, base=0, pattern=[[1, P]], channel_multiplier=-1))
            pool.sem_inc(core.consts_ready, 1)

        @block.sync
        def _(sp):
            at = 0
            for name, n in (("g_mix", 16), ("g_mh", 8), ("g_ffn", 16), ("g_ple", 16)):
                sp.dma_start(core.grows[at:at + n, :], w[name].rearrange("l (k p) -> (l k) p", p=P)
                             ).then_inc(core.grows_landed, 16)
                at += n
            for t, (t0, n) in enumerate(TILES):
                src = w["x_prompt"][0, t0:t0 + n, :] if t < 2 else w["x_sample"].rearrange("b s d -> (b s) d")
                sp.dma_start(core.x_res[0:n, t, :], src).then_inc(core.x_landed, 16)
            sp.sem_inc(core.raw_free, NCH)
            sp.wait_ge(core.x_landed, 48)

        @block.vector
        def _(dve):
            dve.wait_ge(core.gcols_turned, 1)
            nc.vector.tensor_copy(core.gcols[:], core.ps[:, 0, 0:56]).then_inc(core.gcols_ready, 1)
            dve.sem_inc(core.proj_copied, 2)

        @block.tensor
        def _(pe):
            pe.wait_ge(core.consts_ready, 1)
            pe.wait_ge(core.grows_landed, 64)
            nc.tensor.transpose(core.ps[:, 0, 0:56], core.grows[:], core.ident[0:56, 0:56]
                                ).then_inc(core.gcols_turned, 1)


def norm_stage(core, xn, xT, ctx, gain_cols=None, gain_row=None, rows_out=None):
    nc, ps = core.nc, core.ps
    ss = core.sb(f"norm{core.norm_runs}_ss", [P, 3], F32, ctx)
    u = core.norm_runs
    core.norm_runs += 1
    ss_clear, squares, mean_ready, root_ready, rows_ready, turned, stored = core.norm_sems[:7]
    copied = core.norm_sems[7:9]

    def take(engine, k):
        engine.wait_ge(turned, u * KD + k + 1)
        src, dst = ps[:, k % 8, 0:NT], xT[:, k, :]
        if k % 2 == 0:
            scale = gain_cols[:, k:k + 1] if gain_cols is not None else 1.0
            nc.scalar.activation(dst, src, ACT.Copy, scale=scale).then_inc(copied[0], 1)
        elif gain_cols is not None:
            nc.vector.tensor_scalar(dst, src, gain_cols[:, k:k + 1], None, ALU.mult).then_inc(copied[1], 1)
        else:
            nc.vector.tensor_copy(dst, src).then_inc(copied[1], 1)

    with nc.Block() as block:
        @block.scalar
        def _(act):
            act.wait_ge(ss_clear, u + 1)
            for t, (_, n) in enumerate(TILES):
                nc.scalar.activation(xn[0:n, t, :], core.x_res[0:n, t, :], ACT.Square,
                                     accum_out=ss[0:n, t:t + 1]).then_inc(squares, 1)
            act.wait_ge(mean_ready, u + 1)
            nc.scalar.activation(ss[:], ss[:], ACT.Sqrt).then_inc(root_ready, 1)
            for k in range(0, KD, 2):
                take(act, k)

        @block.vector
        def _(dve):
            link = chain(dve, core.dve_chain)
            nc.vector.memset(ss[:], 1.0).then_inc(ss_clear, 1)
            dve.wait_ge(squares, u * 3 + 3)
            nc.vector.tensor_scalar(ss[:], ss[:], 1.0 / D, EPS, ALU.mult, ALU.add).then_inc(mean_ready, 1)
            dve.wait_ge(root_ready, u + 1)
            link(nc.vector.reciprocal(ss[:], ss[:]))
            for t, (_, n) in enumerate(TILES):
                if gain_row is None:
                    nc.vector.tensor_scalar(xn[0:n, t, :], core.x_res[0:n, t, :], ss[0:n, t:t + 1], None,
                                            ALU.mult).then_inc(rows_ready, 1)
                else:
                    nc.vector.scalar_tensor_tensor(xn[0:n, t, :], core.x_res[0:n, t, :], ss[0:n, t:t + 1],
                                                   gain_row[0:n, :], ALU.mult, ALU.mult).then_inc(rows_ready, 1)
            for k in range(1, KD, 2):
                take(dve, k)

        @block.tensor
        def _(pe):
            pe.wait_ge(rows_ready, u * 3 + 3)
            for k in range(KD):
                if k >= 8:
                    pe.wait_ge(copied[k % 2], u * (KD // 2) + (k - 8) // 2 + 1)
                for t, (t0, n) in enumerate(TILES):
                    last = nc.tensor.transpose(ps[:, k % 8, t0:t0 + n], xn[0:n, t, k * P:(k + 1) * P],
                                               core.ident[0:n, 0:n])
                last.then_inc(turned, 1)

        if rows_out is not None:
            @block.sync
            def _(sp):
                sp.wait_ge(rows_ready, u * 3 + 3)
                for t, (t0, n) in enumerate(TILES):
                    sp.dma_start(rows_out[t0:t0 + n, :], xn[0:n, t, :]).then_inc(stored, 16)
                sp.wait_ge(stored, 48)


def mix_project(core, w, hT, pT, gates):
    nc, ps = core.nc, core.ps
    wi = w["w_in"][0]
    wg8 = core.wg8
    gates_landed = core.sem("gates_landed")
    gates_done = core.sem("gates_done")
    gates_copied = core.sem("gates_copied")
    parts = ((C_AQ, AQ0, 3), (C_MQ, MQ0, 8))
    start_groups, start_proj = core.raw_groups, core.proj_groups

    with nc.Block() as block:
        def reset():
            core.raw_groups, core.proj_groups = start_groups, start_proj

        def through(fn):
            reset()
            for col, tile, count in parts:
                fn(col, tile, count)
                core.raw_groups += count
                core.proj_groups += count

        @block.sync
        def _(sp):
            sp.dma_start(wg8[:], wi.rearrange("(k p) c -> p k c", p=P)[:, :, C_GATES:C_GATES + 2 * MH]
                         ).then_inc(gates_landed, 16)
            through(lambda col, tile, count: load_groups(core, sp, wi, col, count))

        @block.tensor
        def _(pe):
            pe.wait_ge(gates_landed, 16)
            for b in range(2):
                for k in range(KD):
                    last = nc.tensor.matmul(ps[0:MH, 4 + b, 0:NT], wg8[:, k, b * MH:(b + 1) * MH], hT[:, k, :],
                                            start=(k == 0), stop=(k == KD - 1))
            last.then_inc(gates_done, 1)
            through(lambda col, tile, count: project_groups(core, pe, hT, count))

        def copies(engine, copy, banks):
            def part(col, tile, count):
                done = core.proj_groups
                with engine.Fori(0, count) as g:
                    engine.wait_ge(core.proj_done, g + (done + 1))
                    copy(pT[:, bass.ds(g * 4 + (tile + banks), 2), :], ps[:, banks:banks + 2, 0:NT]
                         ).then_inc(core.proj_copied, 1)
            through(part)

        @block.scalar
        def _(act):
            copies(act, lambda o, i: nc.scalar.activation(o, i, ACT.Copy), 0)

        @block.vector
        def _(dve):
            dve.wait_ge(gates_done, 1)
            nc.vector.tensor_copy(gates[:], ps[0:MH, 4:6, 0:NT]).then_inc(gates_copied, 1)
            copies(dve, lambda o, i: nc.vector.tensor_copy(o, i), 2)


def attention(core, w, out, pT, mixT, ctx):
    nc, ps = core.nc, core.ps
    S = lambda name, shape, dt=F32: core.sb(name, shape, dt, ctx)
    kswp = S("kswp", [P, 2, NT])
    avtok = S("avtok", [P, 2, 256])
    aktok = S("aktok", [P, 256])
    new_kv = S("new_kv", [NS, 2, 256])
    mask = S("mask", [P, 256])
    sinks = S("sinks", [P, AH])
    sink16 = S("sink16", [AH, 1])
    spread = S("spread", [AH, P])
    sm = S("sm", [P, 2, 4, 256])
    small = S("small", [P, 2, 6, 4])
    prT = S("prT", [P, 8, P])
    kv = S("kv", [P, 2, NS, 256])
    kT = S("kT", [P, 2, 2 * NS, P])
    sT = S("sT", [P, P])
    sq = S("sq", [P, P])
    st = S("st", [P, 8])

    names = ("a_const a_swap a_rows a_rowsT a_sinks a_win a_new a_stored a_scores a_shift a_exp "
             "a_prob a_turn a_turned a_pv a_mixed s_keysT s_kcopy s_scores s_sT s_turn s_prob s_back "
             "s_pT s_pv a_bias a_bias2 s_straight").split()
    q = {n: core.sem(n) for n in names}

    def span(b):
        return 128 * (b + 1)

    with nc.Block() as block:
        @block.gpsimd
        def _(pool):
            link = chain(pool, core.pool_chain)
            link(nc.gpsimd.memset(mask[:], 0.0))
            link(nc.gpsimd.affine_select(out=mask[:], in_=mask[:], compare_op=ALU.is_ge, fill=-BIG,
                                         base=P, pattern=[[-1, 256]], channel_multiplier=1))
            link(nc.gpsimd.affine_select(out=mask[:], in_=mask[:], compare_op=ALU.is_gt, fill=-BIG,
                                         base=0, pattern=[[1, 256]], channel_multiplier=-1))
            link(nc.gpsimd.memset(spread[:], 0.0))
            link(nc.gpsimd.affine_select(out=spread[:].rearrange("p (b h) -> p b h", b=NS),
                                         in_=spread[:].rearrange("p (b h) -> p b h", b=NS),
                                         compare_op=ALU.not_equal, fill=1.0, base=0,
                                         pattern=[[0, NS], [1, AH]], channel_multiplier=-1))
            pool.sem_inc(q["a_const"], 1)

        @block.sync
        def _(sp):
            sp.dma_start(sinks[:], w["attn_sinks"].to_broadcast([P, AH])).then_inc(q["a_sinks"], 16)
            sp.dma_start(sink16[:], w["attn_sinks"].rearrange("l h -> h l")).then_inc(q["a_sinks"], 16)
            for i, name in enumerate(("state_swa_k", "state_swa_v")):
                rows = w[name][0].rearrange("b s h d -> s b (h d)")
                for a, b in ((0, 112), (112, 127)):
                    sp.dma_start(kv[a:b, i, :, :], rows[a + 1:b + 1]).then_inc(q["a_win"], 16)
            sp.wait_ge(q["a_rows"], 2)
            for i in range(2):
                sp.dma_start(kv[127:128, i, :, :], new_kv[:, i, :]).then_inc(q["a_new"], 16)
            sp.dma_start(out["prompt_k"][0, 0].rearrange("s h d -> s (h d)"), aktok[:]).then_inc(q["a_stored"], 16)
            sp.dma_start(out["prompt_v"][0, 0].rearrange("s h d -> s (h d)"), avtok[:, 1, :]).then_inc(q["a_stored"], 16)
            sp.wait_ge(q["a_win"], 64)
            sp.wait_ge(q["a_new"], 32)
            for i, name in enumerate(("sample_k", "sample_v")):
                sp.dma_start(out[name][0].rearrange("b s h d -> s b (h d)"), kv[:, i, :, :]).then_inc(q["a_stored"], 16)
            sp.wait_ge(q["a_stored"], 64)

        @block.tensor
        def _(pe):
            for i in range(2):
                for b in range(2):
                    nc.tensor.transpose(ps[:, 7, b * 256 + i * P:b * 256 + (i + 1) * P],
                                        pT[:, AV0 + i, b * P:(b + 1) * P], core.ident[:])
                nc.tensor.transpose(ps[:, 6, i * P:(i + 1) * P], pT[:, AK0 + i, P:SEQ], core.ident[:])
                nc.tensor.transpose(ps[0:NS, 6, 256 + i * P:256 + (i + 1) * P], pT[:, AK0 + i, SEQ:NT], core.ident[:])
                last = nc.tensor.transpose(ps[0:NS, 5, i * P:(i + 1) * P], pT[:, AV0 + i, SEQ:NT], core.ident[:])
            last.then_inc(q["a_rowsT"], 1)
            pe.wait_ge(q["a_swap"], 2)

            def scores(u):
                g, b = divmod(u, 2)
                if u >= 2:
                    pe.wait_ge(q["a_shift"], 2 * u - 2)
                for i in range(4):
                    h = 4 * g + i
                    lo = (h % 2) * HD
                    keys = pT[lo:lo + HD, AK0 + g // 2, 0:span(b)] if h % 2 == g % 2 else kswp[lo:lo + HD, g // 2, 0:span(b)]
                    last = nc.tensor.matmul(ps[:, 2 * (u % 2) + i % 2, (i // 2) * 256:(i // 2) * 256 + span(b)],
                                            pT[lo:lo + HD, AQ0 + h // 2, b * P:(b + 1) * P], keys,
                                            start=True, stop=True)
                last.then_inc(q["a_scores"], 1)

            def turn(u):
                b = u % 2
                pe.wait_ge(q["a_prob"], u + 1)
                if u == 0:
                    pe.wait_ge(q["a_rows"], 2)
                if u >= 1:
                    pe.wait_ge(q["a_turned"], u)
                for i in range(4):
                    for kb in range(b + 1):
                        n = i * 2 + kb
                        last = nc.tensor.transpose(ps[:, 4 + n // 4, (n % 4) * P:(n % 4 + 1) * P],
                                                   sm[:, u % 2, i, kb * P:(kb + 1) * P], core.ident[:])
                last.then_inc(q["a_turn"], 1)

            def values(u):
                g, b = divmod(u, 2)
                pe.wait_ge(q["a_turned"], u + 1)
                if u >= 2:
                    pe.wait_ge(q["a_mixed"], u - 1)
                for i in range(4):
                    lo = (i % 2) * HD
                    for kb in range(b + 1):
                        last = nc.tensor.matmul(ps[lo:lo + HD, 6 + u % 2, (i // 2) * P:(i // 2 + 1) * P],
                                                avtok[:, kb, g * HD:(g + 1) * HD], prT[:, i * 2 + kb, :],
                                                start=(kb == 0), stop=(kb == b))
                last.then_inc(q["a_pv"], 1)

            scores(0)
            for u in range(8):
                if u + 1 < 8:
                    scores(u + 1)
                turn(u)
                values(u)

            pe.wait_ge(q["a_win"], 64)
            pe.wait_ge(q["a_new"], 32)
            pe.wait_ge(q["a_shift"], 16)
            for n in range(2 * NS):
                last = nc.tensor.transpose(ps[:, n // 4, (n % 4) * P:(n % 4 + 1) * P],
                                           kv[:, 0, n // 2, (n % 2) * P:(n % 2 + 1) * P], core.ident[:])
                if n % 4 == 3:
                    last.then_inc(q["s_keysT"], 1)
            pe.wait_ge(q["a_const"], 1)
            pe.wait_ge(q["a_sinks"], 32)
            pe.wait_ge(q["a_turned"], 8)
            nc.tensor.matmul(ps[:, 5, 256:257], spread[:], sink16[:], start=True, stop=True)
            pe.wait_ge(q["s_kcopy"], 8)
            for b in range(NS):
                for g in range(KV):
                    for par in range(2):
                        lo = par * HD
                        keys = kT[lo:lo + HD, int(par != g % 2), 2 * b + g // 2, :]
                        c = b * (AH // 2) + 2 * g
                        last = nc.tensor.matmul(ps[:, par, c:c + 2], keys,
                                                pT[lo:lo + HD, AQ0 + 2 * g:AQ0 + 2 * g + 2, SEQ + b],
                                                start=True, stop=True)
            last.then_inc(q["s_scores"], 1)
            pe.wait_ge(q["s_sT"], 1)
            nc.tensor.transpose(ps[:, 5, 0:P], sT[:], core.ident[:]).then_inc(q["s_turn"], 1)
            pe.wait_ge(q["s_prob"], 1)
            nc.tensor.transpose(ps[:, 5, 128:256], sq[:], core.ident[:]).then_inc(q["s_back"], 1)
            pe.wait_ge(q["s_pT"], 1)
            pe.wait_ge(q["a_mixed"], 8)
            for b in range(NS):
                for g in range(KV):
                    last = nc.tensor.matmul(ps[0:HD, 6, b * AH + 4 * g:b * AH + 4 * g + 4],
                                            kv[:, 1, b, g * HD:(g + 1) * HD], sT[:, b * AH + 4 * g:b * AH + 4 * g + 4],
                                            start=True, stop=True)
            last.then_inc(q["s_pv"], 1)

        @block.scalar
        def _(act):
            act.wait_ge(q["a_rowsT"], 1)
            nc.scalar.activation(avtok[:], ps[:, 7, :].rearrange("p (b c) -> p b c", b=2), ACT.Copy
                                 ).then_inc(q["a_rows"], 1)

            def turned(u):
                b = u % 2
                act.wait_ge(q["a_turn"], u + 1)
                if u >= 1:
                    act.wait_ge(q["a_pv"], u)
                src = ps[:, 4:6, :].rearrange("p a (i k c) -> p (a i) k c", k=2, c=P)[:, :, 0:b + 1, :]
                dst = prT[:].rearrange("p (i k) c -> p i k c", k=2)[:, :, 0:b + 1, :]
                nc.scalar.activation(dst, src, ACT.Copy).then_inc(q["a_turned"], 1)

            def mixed(u):
                g, b = divmod(u, 2)
                act.wait_ge(q["a_pv"], u + 1)
                nc.scalar.activation(mixT[:, 8 + 2 * g:10 + 2 * g, b * P:(b + 1) * P],
                                     ps[:, 6 + u % 2, 0:256].rearrange("p (i c) -> p i c", i=2), ACT.Copy
                                     ).then_inc(q["a_mixed"], 1)

            for u in range(8):
                b = u % 2
                act.wait_ge(q["a_bias"], u + 1)
                for i in range(4):
                    nc.scalar.activation(sm[:, u % 2, i, 0:span(b)], sm[:, u % 2, i, 0:span(b)], ACT.Exp,
                                         bias=small[:, u % 2, 1, i:i + 1], accum_out=small[:, u % 2, 3, i:i + 1])
                nc.scalar.activation(small[:, u % 2, 2, :], small[:, u % 2, 2, :], ACT.Exp).then_inc(q["a_exp"], 1)
                turned(u)
                mixed(u)
            link = chain(act, core.act_chain)
            for n in range(4):
                act.wait_ge(q["s_keysT"], n + 1)
                src = ps[:, n, :].rearrange("p (i c) -> p i c", i=4)
                nc.scalar.activation(kT[:, 0, 4 * n:4 * n + 4, :], src, ACT.Copy).then_inc(q["s_straight"], 1)
                nc.scalar.activation(kT[0:HD, 1, 4 * n:4 * n + 4, :], src[HD:P], ACT.Copy).then_inc(q["s_kcopy"], 1)
            act.wait_ge(q["s_scores"], 1)
            nc.scalar.activation(sT[:].rearrange("p (c a) -> p a c", a=2), ps[:, 0:2, 0:P // 2], ACT.Copy,
                                 scale=HD ** -0.5).then_inc(q["s_sT"], 1)
            act.wait_ge(q["a_bias2"], 1)
            link(nc.scalar.activation(sq[:], ps[:, 5, 0:P], ACT.Exp, bias=st[:, 1:2], accum_out=st[:, 3:4]))
            nc.scalar.activation(st[:, 2:3], st[:, 2:3], ACT.Exp).then_inc(q["a_exp"], 1)
            act.wait_ge(q["s_back"], 1)
            nc.scalar.activation(sT[:], ps[:, 5, 128:256], ACT.Copy).then_inc(q["s_pT"], 1)
            act.wait_ge(q["s_pv"], 1)
            for par in range(2):
                src = ps[0:HD, 6, 0:P].rearrange("p (b j q) -> p q j b", b=NS, q=2)[:, par]
                link(nc.scalar.activation(mixT[par * HD:(par + 1) * HD, 8:16, SEQ:NT], src, ACT.Copy))

        @block.vector
        def _(dve):
            link = chain(dve, core.dve_chain)
            nc.vector.tensor_copy(kswp[0:HD], pT[HD:P, AK0:AK0 + 2, :]).then_inc(q["a_swap"], 1)
            nc.vector.tensor_copy(kswp[HD:P], pT[0:HD, AK0:AK0 + 2, :]).then_inc(q["a_swap"], 1)
            dve.wait_ge(q["a_rowsT"], 1)
            link(nc.vector.tensor_copy(aktok[:], ps[:, 6, 0:256]))
            link(nc.vector.tensor_copy(new_kv[:, 0, :], ps[0:NS, 6, 256:512]))
            nc.vector.tensor_copy(new_kv[:, 1, :], ps[0:NS, 5, 0:256]).then_inc(q["a_rows"], 1)
            dve.wait_ge(q["a_const"], 1)
            dve.wait_ge(q["a_sinks"], 32)
            for u in range(8):
                g, b = divmod(u, 2)
                s, m = sm[:, u % 2, :, 0:span(b)], small[:, u % 2]
                dve.wait_ge(q["a_scores"], u + 1)
                if u >= 2:
                    dve.wait_ge(q["a_turn"], u - 1)
                msk = mask[:, 256 - span(b):256].rearrange("p (o c) -> p o c", o=1).to_broadcast([P, 2, span(b)])
                for a in range(2):
                    src = ps[:, 2 * (u % 2) + a, :].rearrange("p (i c) -> p i c", i=2)[:, :, 0:span(b)]
                    nc.vector.scalar_tensor_tensor(sm[:, u % 2, a::2, 0:span(b)], src, HD ** -0.5, msk, ALU.mult, ALU.add
                                                   ).then_inc(q["a_shift"], 1)
                dve.wait_ge(q["a_shift"], 2 * u + 2)
                link(nc.vector.tensor_reduce(m[:, 0, :], s, AX, ALU.max))
                link(nc.vector.tensor_tensor(m[:, 0, :], m[:, 0, :], sinks[:, 4 * g:4 * g + 4], ALU.max))
                link(nc.vector.tensor_tensor(m[:, 2, :], sinks[:, 4 * g:4 * g + 4], m[:, 0, :], ALU.subtract))
                nc.vector.tensor_scalar(m[:, 1, :], m[:, 0, :], -1.0, None, ALU.mult).then_inc(q["a_bias"], 1)
                dve.wait_ge(q["a_exp"], u + 1)
                link(nc.vector.tensor_tensor(m[:, 4, :], m[:, 3, :], m[:, 2, :], ALU.add))
                link(nc.vector.reciprocal(m[:, 5, :], m[:, 4, :]))
                nc.vector.tensor_tensor(s, s, m[:, 5, :].rearrange("p (i o) -> p i o", o=1).to_broadcast([P, 4, span(b)]),
                                        ALU.mult).then_inc(q["a_prob"], 1)
            for n in range(4):
                dve.wait_ge(q["s_straight"], n + 1)
                nc.vector.tensor_copy(kT[HD:P, 1, 4 * n:4 * n + 4, :], kT[0:HD, 0, 4 * n:4 * n + 4, :]).then_inc(q["s_kcopy"], 1)
            dve.wait_ge(q["s_turn"], 1)
            link(nc.vector.tensor_reduce(st[:, 0:1], ps[:, 5, 0:P], AX, ALU.max))
            link(nc.vector.tensor_tensor(st[:, 0:1], st[:, 0:1], ps[:, 5, 256:257], ALU.max))
            link(nc.vector.tensor_tensor(st[:, 2:3], ps[:, 5, 256:257], st[:, 0:1], ALU.subtract))
            nc.vector.tensor_scalar(st[:, 1:2], st[:, 0:1], -1.0, None, ALU.mult).then_inc(q["a_bias2"], 1)
            dve.wait_ge(q["a_exp"], 9)
            link(nc.vector.tensor_tensor(st[:, 4:5], st[:, 3:4], st[:, 2:3], ALU.add))
            link(nc.vector.reciprocal(st[:, 5:6], st[:, 4:5]))
            nc.vector.tensor_scalar(sq[:], sq[:], st[:, 5:6], None, ALU.mult).then_inc(q["s_prob"], 1)


def mlstm(core, w, out, pT, mixT, gates, ctx):
    nc, ps = core.nc, core.ps
    S = lambda name, shape, dt=F32: core.sb(name, shape, dt, ctx)
    ktok = S("ktok", [P, 2, 4 * DK])
    vaug = S("vaug", [P, 2, MH, DK + 1])
    skq = S("skq", [NS, 2, 4 * DK])
    bi, bf = S("bi", [MH, 1]), S("bf", [MH, 1])
    lf = S("lf", [MH, NT])
    t1, t2 = S("t1", [MH, NT]), S("t2", [MH, NT])
    fsum, amax = S("fsum", [MH, SEQ]), S("amax", [MH, SEQ])
    arow = S("arow", [MH, 3, SEQ])
    cols = S("cols", [P, 3, 2, MH])
    mend = S("mend", [MH, 2])
    sel = S("sel", [NS, NS, P])
    causal = S("causal", [P, 256])
    et = S("et", [P, 2, 384])
    wt = S("wt", [P, 2, 384])
    hh = core.raw[:, 3, :].rearrange("p (b h k) -> p b h k", b=2, h=MH)
    vw = S("vw", [P, 2, DK])
    col = S("col", [P, 6, 8])
    cout = S("cout", [P, 2, 2, DK])
    nout = S("nout", [1, MH, DK])
    sg = S("sg", [NS, 10, MH])
    n0, n1 = S("n0", [NS, MH, DK]), S("n1", [NS, MH, DK])
    diag = S("diag", [NS, 3, NS, MH])
    tab = S("tab", [P, 3, NS, MH])
    vd = S("vd", [P, 8, NS])
    num = S("num", [P, 8, NS])
    nsq = S("nsq", [P, 8, NS])
    cst = core.raw[:, 4:6, :]
    junk, prod = wt[:, 0, 0:DK], et[:, 0, 0:DK]

    names = ("m_small m_const m_rowsT m_rows m_lf1 m_lf2 m_arow m_colsT m_cols m_en m_mb m_e1 m_e2 m_st m_wt "
             "m_num m_den m_root m_hh m_hT m_mix m_vw m_c m_cout m_cst0 m_cst1 m_nn m_sig m_state m_sT m_sg1 "
             "m_sg2 m_diag m_tabT m_tab m_kq m_cdec m_cnew m_num2 m_sqs m_ssum m_root2 "
             "m_stored m_cstored m_nrec").split()
    q = {n: core.sem(n) for n in names}

    with nc.Block() as block:
        @block.gpsimd
        def _(pool):
            link = chain(pool, core.pool_chain)
            link(nc.gpsimd.memset(vaug[:, :, :, DK:DK + 1], 1.0))
            link(nc.gpsimd.memset(sel[:], 0.0))
            link(nc.gpsimd.affine_select(out=sel[:], in_=sel[:], compare_op=ALU.not_equal, fill=1.0,
                                         base=0, pattern=[[1, NS], [0, P]], channel_multiplier=-1))
            link(nc.gpsimd.memset(causal[:], 0.0))
            link(nc.gpsimd.affine_select(out=causal[:], in_=causal[:], compare_op=ALU.is_ge, fill=-BIG,
                                         base=0, pattern=[[1, 256]], channel_multiplier=-1))
            pool.sem_inc(q["m_const"], 1)

        @block.sync
        def _(sp):
            sp.dma_start(bi[:], w["b_igate"].rearrange("l h -> h l")).then_inc(q["m_small"], 16)
            sp.dma_start(bf[:], w["b_fgate"].rearrange("l h -> h l")).then_inc(q["m_small"], 16)
            sp.dma_start(sg[:, 0, :], w["state_mlstm_m"][0]).then_inc(q["m_small"], 16)
            sp.dma_start(n0[:], w["state_mlstm_n"][0]).then_inc(q["m_small"], 16)

            def state(ap, b):
                return ap[0, b].rearrange("h (v p) k -> p (h v) k", p=P)

            def slot(b):
                return cst[:, b % 2, :].rearrange("p (t k) -> p t k", k=DK)

            def load(b):
                sp.dma_start(slot(b), state(w["state_mlstm_C"], b)).then_inc(q["m_state"], 16)

            load(0)
            for h in range(MH):
                sp.wait_ge(q["m_cout"], h + 1)
                sp.dma_start(out["prompt_C"][0, 0, h].rearrange("(v p) k -> p v k", p=P), cout[:, h % 2]
                             ).then_inc(q[f"m_cst{h % 2}"], 16)
            sp.wait_ge(q["m_nn"], 2)
            sp.dma_start(out["prompt_n"][0], nout[:]).then_inc(q["m_stored"], 16)
            sp.dma_start(out["prompt_m"].rearrange("l b h -> h (l b)"), mend[:, 1:2]).then_inc(q["m_stored"], 16)
            sp.wait_ge(q["m_nrec"], 1)
            sp.dma_start(out["sample_n"][0], n1[:]).then_inc(q["m_stored"], 16)
            sp.dma_start(out["sample_m"][0], sg[:, 5, :]).then_inc(q["m_stored"], 16)
            for b in range(NS):
                if b + 1 < NS:
                    if b >= 1:
                        sp.wait_ge(q["m_cstored"], 16 * b)
                        sp.wait_ge(q["m_num2"], 8 * b)
                    sp.wait_ge(q["m_state"], 16 * (b + 1))
                    load(b + 1)
                sp.wait_ge(q["m_cnew"], 8 * (b + 1))
                sp.dma_start(state(out["sample_C"], b), slot(b)).then_inc(q["m_cstored"], 16)
            for i in range(2):
                sp.wait_ge(q[f"m_cst{i}"], 16 * (MH // 2))
            sp.wait_ge(q["m_stored"], 64)
            sp.wait_ge(q["m_cstored"], 16 * NS)

        jobs = [(MK0, 0, t) for t in range(3)] + [(MK0, 4, t) for t in range(3)]
        jobs += [(MV0, 0, t) for t in range(2)] + [(MV0, 4, t) for t in range(2)]
        jobs += [(MQ0, 0, 2), (MQ0, 4, 2)]

        @block.tensor
        def _(pe):
            for n, (tile, off, t) in enumerate(jobs):
                t0, rows = TILES[t]
                if n >= 4:
                    pe.wait_ge(q["m_rows"], n - 3)
                for i in range(4):
                    last = nc.tensor.transpose(ps[0:rows, n % 4, i * P:(i + 1) * P],
                                               pT[:, tile + off + i, t0:t0 + rows], core.ident[:])
                last.then_inc(q["m_rowsT"], 1)
            pe.wait_ge(q["m_arow"], 3)
            for kind in range(3):
                for b in range(2):
                    c = (kind * 2 + b) * MH
                    last = nc.tensor.transpose(ps[:, 4, c:c + MH], arow[:, kind, b * P:(b + 1) * P],
                                               core.ident[0:MH, 0:MH])
            last.then_inc(q["m_colsT"], 1)
            nc.tensor.transpose(ps[0:NS, 5, 0:MH], t1[:, SEQ:NT], core.ident[0:MH, 0:MH])
            nc.tensor.transpose(ps[0:NS, 5, MH:2 * MH], lf[:, SEQ:NT], core.ident[0:MH, 0:MH]).then_inc(q["m_sT"], 1)
            pe.wait_ge(q["m_const"], 1)
            pe.wait_ge(q["m_rows"], len(jobs))

            def scores(h):
                if h >= 2:
                    pe.wait_ge(q["m_e1"], h - 1)
                nc.tensor.matmul(ps[:, h % 2, 0:SEQ], sel[0:MH, h, :], amax[:], start=True, stop=True
                                 ).then_inc(q["m_mb"], 1)
                if h >= 2:
                    pe.wait_ge(q["m_wt"], h - 1)
                for s in range(2):
                    o = ps[:, 2 + h % 2, 0:256] if s == 0 else ps[:, 2 + h % 2, 256:384]
                    for j in range(2):
                        last = nc.tensor.matmul(o, pT[:, MK0 + 2 * h + j, s * P:(s + 1) * P],
                                                pT[:, MQ0 + 2 * h + j, s * P:SEQ], start=(j == 0), stop=(j == 1))
                last.then_inc(q["m_st"], 1)

            def values(h):
                pe.wait_ge(q["m_wt"], h + 1)
                if h >= 1:
                    pe.wait_ge(q["m_den"], 2 * h)
                for t in range(2):
                    for s in range(t + 1):
                        lhs = wt[:, h % 2, t * P:(t + 1) * P] if s == 0 else wt[:, h % 2, 256:384]
                        last = nc.tensor.matmul(ps[:, 6 + t, 0:DK + 1], lhs, vaug[:, s, h, :],
                                                start=(s == 0), stop=(s == t))
                last.then_inc(q["m_num"], 1)

            scores(0)
            for h in range(MH):
                if h + 1 < MH:
                    scores(h + 1)
                values(h)
            pe.wait_ge(q["m_cols"], 1)
            pe.wait_ge(q["m_sg1"], 1)
            for h in range(MH):
                if h >= 2:
                    pe.wait_ge(q["m_cout"], h - 1)
                for b in range(2):
                    pe.wait_ge(q["m_vw"], 2 * h + b + 1)
                    for v in range(2):
                        last = nc.tensor.matmul(ps[:, 4 + h % 2, v * DK:(v + 1) * DK], vw[:, b, v * P:(v + 1) * P],
                                                ktok[:, b, h * DK:(h + 1) * DK], start=(b == 0 and v == 0),
                                                stop=(b == 1), skip_group_check=True)
                    if b == 1:
                        last.then_inc(q["m_c"], 1)
                for b in range(2):
                    last = nc.tensor.matmul(ps[0:1, 2 + h // 2, (h % 2) * DK:(h % 2 + 1) * DK], cols[:, 2, b, h:h + 1],
                                            ktok[:, b, h * DK:(h + 1) * DK], start=(b == 0), stop=(b == 1))
                if h % 2:
                    last.then_inc(q["m_hT"], 1)
            pe.wait_ge(q["m_diag"], 1)
            pe.wait_ge(q["m_cout"], MH)
            nc.tensor.matmul(ps[:, 4, 0:96], core.ones[0:NS, :], diag[:].rearrange("p a b h -> p (a b h)"),
                             start=True, stop=True).then_inc(q["m_tabT"], 1)
            pe.wait_ge(q["m_hh"], 1)
            for j in range(8):
                if j >= 2:
                    pe.wait_ge(q["m_mix"], j - 1)
                for b in range(2):
                    last = nc.tensor.transpose(ps[:, 6 + j % 2, b * P:(b + 1) * P],
                                               hh[:, b, j // 2, (j % 2) * P:(j % 2 + 1) * P], core.ident[:])
                last.then_inc(q["m_hT"], 1)
            pe.wait_ge(q["m_nn"], 2)
            for b in range(NS):
                if b >= 1:
                    pe.wait_ge(q["m_num2"], 8 * b)
                for kq in range(2):
                    for i in range(2):
                        last = nc.tensor.matmul(ps[:, 2 * kq + i, :], sel[:, b, :], skq[:, kq, i * 512:(i + 1) * 512],
                                                start=True, stop=True)
                last.then_inc(q["m_kq"], 1)
            pe.wait_ge(q["m_sqs"], 1)
            pe.wait_ge(q["m_tab"], 1)
            v4 = nsq[:].rearrange("p (h v) b -> p v h b", v=2)
            for v in range(2):
                last = nc.tensor.matmul(ps[:, 5, 0:32], core.ones[:], v4[:, v], start=(v == 0), stop=(v == 1))
            last.then_inc(q["m_ssum"], 1)

        @block.scalar
        def _(act):
            link = chain(act, core.act_chain)
            for n, (tile, off, t) in enumerate(jobs):
                act.wait_ge(q["m_rowsT"], n + 1)
                rows = TILES[t][1]
                src = ps[0:rows, n % 4, :]
                if t == 2:
                    dst = skq[:, int(tile == MQ0), off * P:off * P + 512]
                elif tile == MK0:
                    dst = ktok[:, t, off * P:off * P + 512]
                else:
                    dst = vaug[:, t, off // 2:off // 2 + 2, 0:DK]
                    src = src.rearrange("p (h c) -> p h c", h=2)
                nc.scalar.activation(dst, src, ACT.Copy).then_inc(q["m_rows"], 1)
            act.wait_ge(q["m_lf1"], 1)
            link(nc.scalar.activation(t2[:], t2[:], ACT.Exp, scale=-1.0))
            nc.scalar.activation(t2[:], t2[:], ACT.Ln, bias=1.0).then_inc(q["m_lf2"], 1)
            act.wait_ge(q["m_arow"], 2)
            nc.scalar.activation(arow[:, 2, :], arow[:, 2, :], ACT.Exp).then_inc(q["m_en"], 1)
            act.wait_ge(q["m_cols"], 1)
            nc.scalar.activation(col[:, 0, :], cols[:, 1].rearrange("p b h -> p (b h)"), ACT.Exp).then_inc(q["m_en"], 1)
            for h in range(MH):
                act.wait_ge(q["m_e1"], h + 1)
                for s in range(2):
                    o = et[:, h % 2, 0:256] if s == 0 else et[:, h % 2, 256:384]
                    ins = nc.scalar.activation(o, o, ACT.Exp, bias=cols[:, 0, s, h:h + 1])
                ins.then_inc(q["m_e2"], 1)
            act.wait_ge(q["m_sg1"], 1)
            nc.scalar.activation(sg[:, 6:9, :], sg[:, 6:9, :], ACT.Exp).then_inc(q["m_sg2"], 1)
            act.wait_ge(q["m_den"], 8)
            for b in range(2):
                for h in range(MH):
                    link(nc.scalar.activation(junk, hh[:, b, h, :], ACT.Square, accum_out=col[:, 3, b * MH + h:b * MH + h + 1]))
            nc.scalar.activation(col[:, 4, :], col[:, 3, :], ACT.Sqrt, scale=1.0 / DK, bias=core.eps[:]).then_inc(q["m_root"], 1)
            for j in range(2):
                act.wait_ge(q["m_hT"], j + 1)
                link(nc.scalar.activation(nout[:, 2 * j:2 * j + 2, :], ps[0:1, 2 + j, :].rearrange("p (h c) -> p h c", h=2),
                                     ACT.Copy))
                act.sem_inc(q["m_nn"], 1)
            nc.scalar.activation(pT[:, MO0:MO0 + 8, :], pT[:, MO0:MO0 + 8, :], ACT.Sigmoid).then_inc(q["m_sig"], 1)
            act.wait_ge(q["m_tab"], 1)
            for b in range(NS):
                act.wait_ge(q["m_state"], 16 * (b + 1))
                for h in range(MH):
                    c = cst[:, b % 2, h * 512:(h + 1) * 512]
                    nc.scalar.activation(c, c, ACT.Copy, scale=tab[:, 0, b, h:h + 1]).then_inc(q["m_cdec"], 1)
            act.wait_ge(q["m_ssum"], 1)
            nc.scalar.activation(vd[:, 0:4, :], ps[:, 5, 0:32].rearrange("p (h b) -> p h b", h=MH), ACT.Sqrt,
                                 scale=1.0 / DK, bias=core.eps[:]).then_inc(q["m_root2"], 1)

        @block.vector
        def _(dve):
            link = chain(dve, core.dve_chain)
            V = nc.vector
            dve.wait_ge(q["m_small"], 64)
            link(V.tensor_scalar(t1[:], gates[:, 1, :], bf[:], -1.0, ALU.add, ALU.mult))
            V.scalar_tensor_tensor(t2[:], t1[:], -1.0, t1[:], ALU.mult, ALU.max).then_inc(q["m_lf1"], 1)
            dve.wait_ge(q["m_lf2"], 1)
            link(V.scalar_tensor_tensor(lf[:], t1[:], 0.0, t2[:], ALU.max, ALU.add))
            link(V.tensor_scalar(lf[:], lf[:], -1.0, None, ALU.mult))
            link(V.tensor_scalar(t1[:], gates[:, 0, :], bi[:], None, ALU.add))
            dve.wait_ge(q["m_const"], 1)
            link(V.tensor_tensor_scan(fsum[:], core.ones[0:MH, 0:1].to_broadcast([MH, SEQ]), lf[:, 0:SEQ], 0.0, ALU.mult, ALU.add))
            link(V.tensor_tensor(arow[:, 0, :], t1[:, 0:SEQ], fsum[:], ALU.subtract))
            link(V.tensor_tensor_scan(amax[:], arow[:, 0, :], arow[:, 0, :], 0.0, ALU.max, ALU.max))
            V.scalar_tensor_tensor(arow[:, 1, :], fsum[:], -1.0, amax[:], ALU.mult, ALU.subtract).then_inc(q["m_arow"], 1)
            link(V.tensor_copy(mend[:, 0:1], amax[:, SEQ - 1:SEQ]))
            link(V.tensor_tensor(mend[:, 1:2], mend[:, 0:1], fsum[:, SEQ - 1:SEQ], ALU.add))
            V.tensor_scalar(arow[:, 2, :], arow[:, 0, :], mend[:, 0:1], None, ALU.subtract).then_inc(q["m_arow"], 1)
            dve.wait_ge(q["m_en"], 1)
            V.tensor_scalar(arow[:, 2, :], arow[:, 2, :], DK ** -0.5, None, ALU.mult).then_inc(q["m_arow"], 1)
            dve.wait_ge(q["m_colsT"], 1)
            V.tensor_copy(cols[:].rearrange("p a b h -> p (a b h)"), ps[:, 4, 0:24]).then_inc(q["m_cols"], 1)
            dve.wait_ge(q["m_sT"], 1)
            link(V.tensor_copy(sg[:, 1:3, :], ps[0:NS, 5, 0:8].rearrange("p (a h) -> p a h", a=2)))
            link(V.tensor_tensor(sg[:, 3, :], sg[:, 1, :], sg[:, 2, :], ALU.subtract))
            link(V.tensor_tensor(sg[:, 4, :], sg[:, 0, :], sg[:, 3, :], ALU.max))
            link(V.tensor_tensor(sg[:, 5, :], sg[:, 2, :], sg[:, 4, :], ALU.add))
            link(V.tensor_tensor(sg[:, 6, :], sg[:, 0, :], sg[:, 4, :], ALU.subtract))
            link(V.tensor_tensor(sg[:, 7, :], sg[:, 3, :], sg[:, 4, :], ALU.subtract))
            V.tensor_scalar(sg[:, 8, :], sg[:, 5, :], -1.0, None, ALU.mult).then_inc(q["m_sg1"], 1)
            for h in range(MH):
                dve.wait_ge(q["m_mb"], h + 1)
                if h >= 2:
                    dve.wait_ge(q["m_wt"], h - 1)
                link(V.scalar_tensor_tensor(et[:, h % 2, 0:256], ps[:, h % 2, 0:256], -1.0, causal[:], ALU.mult, ALU.add))
                V.scalar_tensor_tensor(et[:, h % 2, 256:384], ps[:, h % 2, P:256], -1.0, causal[:, 0:P],
                                       ALU.mult, ALU.add).then_inc(q["m_e1"], 1)
                dve.wait_ge(q["m_e2"], h + 1)
                dve.wait_ge(q["m_st"], h + 1)
                if h >= 2:
                    dve.wait_ge(q["m_num"], h - 1)
                V.scalar_tensor_tensor(wt[:, h % 2], ps[:, 2 + h % 2, 0:384], DK ** -0.5, et[:, h % 2],
                                       ALU.mult, ALU.mult).then_inc(q["m_wt"], 1)
                dve.wait_ge(q["m_num"], h + 1)
                dve.wait_ge(q["m_en"], 2)
                for b in range(2):
                    i = b * MH + h
                    den, rec = col[:, 1, i:i + 1], col[:, 2, i:i + 1]
                    link(V.tensor_copy(rec, ps[:, 6 + b, DK:DK + 1]))
                    link(V.scalar_tensor_tensor(den, rec, -1.0, rec, ALU.mult, ALU.max))
                    link(V.tensor_tensor(den, den, col[:, 0, i:i + 1], ALU.max))
                    link(V.reciprocal(rec, den))
                    link(V.tensor_scalar(hh[:, b, h, :], ps[:, 6 + b, 0:DK], rec, None, ALU.mult))
                    dve.sem_inc(q["m_den"], 1)
            for h in range(MH):
                for b in range(2):
                    if h >= 1:
                        dve.wait_ge(q["m_c"], h)
                    V.tensor_scalar(vw[:, b, :], vaug[:, b, h, 0:DK], cols[:, 2, b, h:h + 1], None, ALU.mult
                                    ).then_inc(q["m_vw"], 1)
                if h >= 2:
                    dve.wait_ge(q[f"m_cst{h % 2}"], 16 * (h // 2))
                dve.wait_ge(q["m_c"], h + 1)
                V.tensor_copy(cout[:, h % 2], ps[:, 4 + h % 2, :].rearrange("p (v k) -> p v k", v=2)).then_inc(q["m_cout"], 1)
            dve.wait_ge(q["m_root"], 1)
            link(V.reciprocal(col[:, 5, :], col[:, 4, :]))
            for b in range(2):
                for h in range(MH):
                    link(V.tensor_scalar(hh[:, b, h, :], hh[:, b, h, :], col[:, 5, b * MH + h:b * MH + h + 1], None, ALU.mult))
            dve.sem_inc(q["m_hh"], 1)
            dve.wait_ge(q["m_sg2"], 1)
            link(V.tensor_scalar(sg[:, 7, :], sg[:, 7, :], DK ** -0.5, None, ALU.mult))
            wide = lambda i: sg[:, i, :].rearrange("p (h o) -> p h o", o=1).to_broadcast([NS, MH, DK])
            kk, qq = (skq[:, i, :].rearrange("p (h k) -> p h k", h=MH) for i in range(2))
            dve.wait_ge(q["m_rows"], len(jobs))
            link(V.tensor_tensor(n0[:], n0[:], wide(6), ALU.mult))
            link(V.tensor_tensor(n1[:], kk, wide(7), ALU.mult))
            link(V.tensor_tensor(n1[:], n1[:], n0[:], ALU.add))
            dve.sem_inc(q["m_nrec"], 1)
            link(V.tensor_tensor(n0[:], n1[:], qq, ALU.mult))
            link(V.tensor_reduce(sg[:, 9, :], n0[:], AX, ALU.add))
            link(V.scalar_tensor_tensor(sg[:, 9, :], sg[:, 9, :], -1.0, sg[:, 9, :], ALU.mult, ALU.max))
            link(V.tensor_tensor(sg[:, 9, :], sg[:, 9, :], sg[:, 8, :], ALU.max))
            link(V.reciprocal(sg[:, 9, :], sg[:, 9, :]))
            eye = core.ident[0:NS, 0:NS].rearrange("p (b o) -> p b o", o=1).to_broadcast([NS, NS, MH])
            for i, row in enumerate((6, 7, 9)):
                link(V.tensor_tensor(diag[:, i], eye, sg[:, row, :].rearrange("p (o h) -> p o h", o=1).to_broadcast([NS, NS, MH]),
                                     ALU.mult))
            dve.sem_inc(q["m_diag"], 1)
            dve.wait_ge(q["m_tabT"], 1)
            V.tensor_copy(tab[:].rearrange("p a b h -> p (a b h)"), ps[:, 4, 0:96]).then_inc(q["m_tab"], 1)
            dve.wait_ge(q["m_tab"], 1)
            by_head = lambda i: tab[:, i].rearrange("p b h -> p h b")
            for v in range(2):
                link(V.tensor_tensor(vd[:].rearrange("p (h v) b -> p v h b", v=2)[:, v],
                                     pT[:, MV0:MV0 + 8, SEQ:NT].rearrange("p (h v) b -> p v h b", v=2)[:, v],
                                     by_head(1), ALU.mult))
            dve.wait_ge(q["m_sig"], 1)
            for j in range(8):
                dve.wait_ge(q["m_hT"], 2 + j + 1)
                V.scalar_tensor_tensor(mixT[:, j, 0:SEQ], ps[:, 6 + j % 2, 0:SEQ], core.gcols[:, 16 + j:17 + j],
                                       pT[:, MO0 + j, 0:SEQ], ALU.mult, ALU.mult).then_inc(q["m_mix"], 1)
            for b in range(NS):
                dve.wait_ge(q["m_kq"], b + 1)
                for t in range(8):
                    h = t // 2
                    c = cst[:, b % 2, t * DK:(t + 1) * DK]
                    if t % 2 == 0:
                        dve.wait_ge(q["m_cdec"], b * MH + h + 1)
                    V.scalar_tensor_tensor(c, ps[:, h // 2, (h % 2) * DK:(h % 2 + 1) * DK], vd[:, t, b:b + 1], c,
                                           ALU.mult, ALU.add).then_inc(q["m_cnew"], 1)
                for t in range(8):
                    h = t // 2
                    c = cst[:, b % 2, t * DK:(t + 1) * DK]
                    dve.wait_ge(q["m_cnew"], b * 8 + t + 1)
                    if b or t:
                        dve.wait_ge(q["m_num2"], b * 8 + t)
                    V.tensor_tensor_reduce(prod, c, ps[:, 2 + h // 2, (h % 2) * DK:(h % 2 + 1) * DK], 1.0, 0.0,
                                           ALU.mult, ALU.add, num[:, t, b:b + 1]).then_inc(q["m_num2"], 1)
            dve.wait_ge(q["m_num2"], 8 * NS)
            for v in range(2):
                o = num[:].rearrange("p (h v) b -> p v h b", v=2)[:, v]
                link(V.tensor_tensor(o, o, by_head(2), ALU.mult))
            V.tensor_tensor(nsq[:], num[:], num[:], ALU.mult).then_inc(q["m_sqs"], 1)
            dve.wait_ge(q["m_root2"], 1)
            link(V.reciprocal(vd[:, 0:4, :], vd[:, 0:4, :]))
            for v in range(2):
                o = num[:].rearrange("p (h v) b -> p v h b", v=2)[:, v]
                link(V.tensor_tensor(o, o, vd[:, 0:4, :], ALU.mult))
            link(V.tensor_tensor(num[:], num[:], core.gcols[:, 16:24].rearrange("p (j o) -> p j o", o=1).to_broadcast([P, 8, NS]),
                                 ALU.mult))
            link(V.tensor_tensor(mixT[:, 0:8, SEQ:NT], num[:], pT[:, MO0:MO0 + 8, SEQ:NT], ALU.mult))


def out_project(core, w, mixT, oT):
    nc, ps = core.nc, core.ps
    wo = w["w_out"][0]
    with nc.Block() as block:
        @block.sync
        def _(sp):
            load_groups(core, sp, wo, 0, 4)

        @block.tensor
        def _(pe):
            project_groups(core, pe, mixT, 4)
            pe.wait_ge(core.proj_copied, 2 * (core.proj_groups + 4) + 2)
            turn_back(core, pe, oT)

        @block.scalar
        def _(act):
            base = core.proj_groups
            with act.Fori(0, 4) as g:
                act.wait_ge(core.proj_done, g + (base + 1))
                nc.scalar.activation(oT[:, bass.ds(g * 4, 2), :], ps[:, 0:2, 0:NT], ACT.Copy).then_inc(core.proj_copied, 1)

        @block.vector
        def _(dve):
            base = core.proj_groups
            with dve.Fori(0, 4) as g:
                dve.wait_ge(core.proj_done, g + (base + 1))
                nc.vector.tensor_copy(oT[:, bass.ds(g * 4 + 2, 2), :], ps[:, 2:4, 0:NT]).then_inc(core.proj_copied, 1)
            add_turned(core, dve)
    core.turned_banks += 12
    core.raw_groups += 4
    core.proj_groups += 4


def turn_back(core, pe, oT):
    nc, ps = core.nc, core.ps
    base, n = core.turned_banks, 0
    for t, (t0, rows) in enumerate(TILES):
        for j in range(4):
            if n >= 4:
                pe.wait_ge(core.added, base + n - 3)
            for i in range(4):
                last = nc.tensor.transpose(ps[0:rows, 4 + n % 4, i * P:(i + 1) * P], oT[:, 4 * j + i, t0:t0 + rows],
                                           core.ident[:])
            last.then_inc(core.turned, 1)
            n += 1


def add_turned(core, dve):
    nc, ps = core.nc, core.ps
    base, n = core.turned_banks, 0
    for t, (t0, rows) in enumerate(TILES):
        for j in range(4):
            dve.wait_ge(core.turned, base + n + 1)
            x = core.x_res[0:rows, t, j * 512:(j + 1) * 512]
            nc.vector.tensor_tensor(x, x, ps[0:rows, 4 + n % 4, :], ALU.add).then_inc(core.added, 1)
            n += 1


def router(core, w, xT, rt, ctx):
    nc, ps = core.nc, core.ps
    S = lambda name, shape, dt=F32: core.sb(name, shape, dt, ctx)
    NL = NG + NE
    wr = S("wr", [P, KD, NL])
    br = S("br", [1, NL])
    lg = S("lg", [P, 3, NL])
    a, b4 = S("ra", [P, 3, NG]), S("rb", [P, 3, NG])
    el, e1, e2 = S("el", [P, 3, NE]), S("e1", [P, 3, NE]), S("e2", [P, 3, NE])
    c = S("rc", [P, 10, 3])
    down4, down32 = S("down4", [P, NG]), S("down32", [P, NE])
    valid = S("valid", [P, 3])
    both = S("both", [P, 3, NE])
    names = "r_loaded r_const r_logits r_exp1 r_exp2 r_in1 r_in2 r_rank r_ranked".split()
    q = {n: core.sem(n) for n in names}
    with nc.Block() as block:
        @block.gpsimd
        def _(pool):
            link = chain(pool, core.pool_chain)
            link(nc.gpsimd.iota(down4[:], pattern=[[-1, NG]], base=NG, channel_multiplier=0, allow_small_or_imprecise_dtypes=True))
            link(nc.gpsimd.iota(down32[:], pattern=[[-1, NE]], base=NE, channel_multiplier=0, allow_small_or_imprecise_dtypes=True))
            link(nc.gpsimd.memset(valid[:], 1.0))
            link(nc.gpsimd.affine_select(out=valid[:, 2:3], in_=valid[:, 2:3], compare_op=ALU.is_gt, fill=0.0,
                                         base=NS, pattern=[[0, 1]], channel_multiplier=-1))
            link(nc.gpsimd.memset(lg[:, 2, :], 0.0))
            link(nc.gpsimd.iota(rt["slot"][:], pattern=[[1, SLOTS]], base=0, channel_multiplier=0, allow_small_or_imprecise_dtypes=True))
            link(nc.gpsimd.iota(rt["ids"][:, :, :, 0], pattern=[[P, 3], [0, NE]], base=1, channel_multiplier=1, allow_small_or_imprecise_dtypes=True))
            link(nc.gpsimd.iota(rt["ids"][:, :, :, 1], pattern=[[2 * P, 3], [0, NE]], base=1, channel_multiplier=2, allow_small_or_imprecise_dtypes=True))
            link(nc.gpsimd.iota(rt["level"][:], pattern=[[SLOTS, PASSES]], base=0, channel_multiplier=0, allow_small_or_imprecise_dtypes=True))
            pool.sem_inc(q["r_const"], 1)

        @block.sync
        def _(sp):
            sp.dma_start(wr[:, :, 0:NG], w["w_router_g"][0].rearrange("(k p) c -> p k c", p=P)).then_inc(q["r_loaded"], 16)
            sp.dma_start(wr[:, :, NG:NL], w["w_router_e"][0].rearrange("(k p) c -> p k c", p=P)).then_inc(q["r_loaded"], 16)
            sp.dma_start(br[:, 0:NG], w["b_router_g"]).then_inc(q["r_loaded"], 16)
            sp.dma_start(br[:, NG:NL], w["b_router_e"]).then_inc(q["r_loaded"], 16)

        @block.tensor
        def _(pe):
            pe.wait_ge(q["r_loaded"], 64)
            for t, (t0, n) in enumerate(TILES):
                for k in range(KD):
                    nc.tensor.matmul(ps[0:n, t, 0:NL], xT[:, k, t0:t0 + n], wr[:, k, :], start=(k == 0), stop=False)
                nc.tensor.matmul(ps[0:n, t, 0:NL], core.ones[0:1, 0:n], br[:], start=False, stop=True).then_inc(q["r_logits"], 1)
            pe.wait_ge(q["r_rank"], 1)
            for t in range(3):
                nc.tensor.matmul(ps[:, 3, t * NE:(t + 1) * NE], core.upper[:], both[:, t, :], start=True, stop=(t == 0))
                for s in range(t):
                    nc.tensor.matmul(ps[:, 3, t * NE:(t + 1) * NE], core.ones[:], both[:, s, :], start=False, stop=(s == t - 1))
            for t in range(3):
                last = nc.tensor.matmul(ps[:, 4, 0:NE], core.ones[:], both[:, t, :], start=(t == 0), stop=(t == 2))
            last.then_inc(q["r_ranked"], 1)

        @block.scalar
        def _(act):
            act.wait_ge(q["r_in1"], 1)
            nc.scalar.activation(a[:], a[:], ACT.Exp).then_inc(q["r_exp1"], 1)
            act.wait_ge(q["r_in2"], 1)
            nc.scalar.activation(c[:, 5, :], c[:, 5, :], ACT.Exp).then_inc(q["r_exp2"], 1)

        @block.vector
        def _(dve):
            link = chain(dve, core.dve_chain)
            V = nc.vector
            wide = lambda row, n: row.rearrange("p (t o) -> p t o", o=1).to_broadcast([P, 3, n])
            over = lambda row, n: row.rearrange("p (o e) -> p o e", o=1).to_broadcast([P, 3, n])
            dve.wait_ge(q["r_const"], 1)
            dve.wait_ge(q["r_logits"], 3)
            link(V.tensor_copy(lg[:, 0:2, :], ps[:, 0:2, 0:NL]))
            link(V.tensor_copy(lg[0:NS, 2, :], ps[0:NS, 2, 0:NL]))
            gl, le = lg[:, :, 0:NG], lg[:, :, NG:NL]

            def first_max(src, n, top, onehot, tmp, down):
                link(V.tensor_reduce(top, src, AX, ALU.max))
                link(V.tensor_tensor(tmp, src, wide(top, n), ALU.is_equal))
                link(V.tensor_tensor(tmp, tmp, over(down[:], n), ALU.mult))
                link(V.tensor_reduce(c[:, 9, :], tmp, AX, ALU.max))
                link(V.tensor_tensor(onehot, tmp, wide(c[:, 9, :], n), ALU.is_equal))

            first_max(gl, NG, c[:, 0, :], b4[:], a[:], down4)
            V.tensor_tensor(a[:], gl, wide(c[:, 0, :], NG), ALU.subtract).then_inc(q["r_in1"], 1)
            dve.wait_ge(q["r_exp1"], 1)
            link(V.tensor_reduce(c[:, 1, :], a[:], AX, ALU.add))
            link(V.reciprocal(c[:, 2, :], c[:, 1, :]))
            link(V.tensor_scalar(b4[:], b4[:], 1.0, BIG, ALU.subtract, ALU.mult))
            for t in range(3):
                link(V.tensor_tensor(el[:, t, :].rearrange("p (g e) -> p g e", g=NG), le[:, t, :].rearrange("p (g e) -> p g e", g=NG),
                                     b4[:, t, :].rearrange("p (g o) -> p g o", o=1).to_broadcast([P, NG, EPG]), ALU.add))
            first_max(el[:], NE, c[:, 3, :], e1[:], both[:], down32)
            link(V.scalar_tensor_tensor(el[:], e1[:], -2.0 * BIG, el[:], ALU.mult, ALU.add))
            first_max(el[:], NE, c[:, 4, :], e2[:], both[:], down32)
            V.tensor_tensor(c[:, 5, :], c[:, 4, :], c[:, 3, :], ALU.subtract).then_inc(q["r_in2"], 1)
            dve.wait_ge(q["r_exp2"], 1)
            link(V.tensor_scalar(c[:, 6, :], c[:, 5, :], 1.0, None, ALU.add))
            link(V.reciprocal(c[:, 7, :], c[:, 6, :]))
            link(V.tensor_tensor(rt["wt"][:, 0, :], c[:, 7, :], c[:, 2, :], ALU.mult))
            link(V.tensor_tensor(rt["wt"][:, 1, :], rt["wt"][:, 0, :], c[:, 5, :], ALU.mult))
            link(V.tensor_tensor(both[:], e1[:], e2[:], ALU.add))
            link(V.tensor_tensor(both[:], both[:], wide(valid[:], NE), ALU.mult))
            dve.sem_inc(q["r_rank"], 1)
            link(V.tensor_tensor(rt["ids"][:, :, :, 1], rt["ids"][:, :, :, 1], e2[:], ALU.add))
            dve.wait_ge(q["r_ranked"], 1)
            link(V.tensor_tensor(el[:], ps[:, 3, 0:3 * NE].rearrange("p (t e) -> p t e", t=3), both[:], ALU.mult))
            link(V.tensor_scalar(both[:], both[:], 1.0, 1.0e6, ALU.subtract, ALU.mult))
            link(V.tensor_tensor(rt["rank"][:], el[:], both[:], ALU.add))
            link(V.tensor_reduce(c[:, 8, 0:1], ps[:, 4, 0:NE], AX, ALU.max))
            link(V.tensor_tensor(rt["need"][:], c[:, 8, 0:1].to_broadcast([P, PASSES]), rt["level"][:], ALU.is_gt))


def experts(core, w, rt, rows, ydram, ctx):
    nc, ps, raw = core.nc, core.ps, core.raw
    S = lambda name, shape, dt=F32: core.sb(name, shape, dt, ctx)
    hi, lo = S("w_hi", [P, SPL, 2048], F32R), S("w_lo", [P, SPL, 2048], F32R)
    xs = S("x_split", [P, KD, 2 * SLOTS], F32R)
    hs = S("h_split", [P, 4, 2 * SLOTS], F32R)
    xe = S("xe", [SLOTS, D])
    gu = S("gu", [P, 2, DE])
    sig, hid = S("sig", [P, 4, SLOTS]), S("hid", [P, 4, SLOTS])
    yl, ysum = S("yl", [SLOTS, D]), S("ysum", [SLOTS, D])
    fold = S("fold", [P, SLOTS])
    hot = S("hot", [P, NE, SLOTS])
    rel = S("rel", [P, 3, NE])
    tabs = S("tabs", [SLOTS, NE, 2])
    gat, sca = S("gat", [SLOTS, NE + 1], I32), S("sca", [SLOTS, NE + 1], I32)
    gi, si = S("gi", [SLOTS, 1], I32), S("si", [SLOTS, 1], I32)
    flag = S("flag", [1, PASSES], I32)
    names = ("w_hi_ready w_lo_ready w_used rel_ready hot_ready hot_used tabs_step tabs_ready "
             "gather_idx gathered x_turned x_hi x_lo gu_copied gu_folded sig_ready h_step h_ready "
             "y_low y_sum scatter_idx y_stored pass_done pool_tick pe_tick").split()
    q = {n: core.sem(n) for n in names}
    landed = core.raw_landed
    lbase = [16 * core.raw_groups] * NCH + [0] * (RAW - NCH)
    wg = w["w_gate"][0].rearrange("e (k p) c -> e p k c", p=P)
    wu = w["w_up"][0].rearrange("e (k p) c -> e p k c", p=P)
    wd = w["w_down"][0].rearrange("e (k p) c -> e p k c", p=P)
    XB, GB, YB = 3, 2, 4

    with nc.Block() as block:
        @block.gpsimd
        def _(pool):
            link = chain(pool, core.pool_chain)
            link(nc.gpsimd.memset(xe[:], 0.0))
            link(nc.gpsimd.tensor_copy(fold[0:SLOTS, :], core.ident[0:SLOTS, 0:SLOTS]))
            link(nc.gpsimd.tensor_copy(fold[SLOTS:P, :], core.ident[SLOTS:P, SLOTS:P]))
            link(nc.gpsimd.memset(gat[:, NE:NE + 1], int(NONE)))
            link(nc.gpsimd.memset(sca[:, 0:1], int(NONE)))
            pool.sem_inc(q["pass_done"], 1)

        @block.vector
        def _(dve):
            link = chain(dve, core.dve_chain)
            link(nc.vector.tensor_copy(flag[:], rt["need"][0:1, :]))
            link(nc.vector.memset(ps[:, YB:YB + 4, :], 0.0))
            dve.sem_inc(q["x_lo"], 1)

        @block.tensor
        def _(pe):
            pe.sem_inc(q["w_used"], SPL)
            pe.sem_inc(q["x_turned"], 2)
            pe.sem_inc(q["hot_used"], 1)

        @block.sync
        def _(sp):
            sp.sem_inc(q["w_lo_ready"], RAW)

    def passes(engine, body):
        with engine.Fori(0, PASSES) as p:
            need = engine.value_load(flag[0:1, bass.ds(p, 1)], min_val=0, max_val=1)
            with engine.If(need > 0):
                body(p)

    with nc.Block() as block:
        @block.sync
        def _(sp):
            def body(p):
                with sp.Fori(0, NE) as e:
                    it = p * NE + e
                    for c in range(ECH):
                        sp.wait_ge(q["w_lo_ready"], it * ECH + (c + 1))
                        if c < 2 * NCH:
                            k = (c % NCH) * CK
                            src = (wg, wu)[c // NCH][bass.ds(e, 1), :, k:k + CK, :].rearrange("o p k c -> (o p) k c")
                            dst = raw[:, c % RAW, :].rearrange("p (k c) -> p k c", k=CK)
                        else:
                            src = wd[bass.ds(e, 1), :, c - 2 * NCH, :].rearrange("o p c -> (o p) c")
                            dst = raw[:, c % RAW, :]
                        sp.dma_start(dst, src).then_inc(landed[c % RAW], 16)
            passes(sp, body)

        @block.scalar
        def _(act):
            def x_high(half, ix):
                act.wait_ge(q["x_turned"], ix * 2 + (half + 3))
                nc.scalar.activation(xs[:, half * 8:half * 8 + 8, 0:SLOTS],
                                     ps[:, XB, :].rearrange("p (k s) -> p k s", k=8), ACT.Copy).then_inc(q["x_hi"], 1)

            def y_low():
                nc.scalar.activation(yl[:].rearrange("p (a c) -> p a c", a=4), ps[SLOTS:P, YB:YB + 4, :], ACT.Copy
                                     ).then_inc(q["y_low"], 1)

            def body(p):
                x_high(0, p * (NE + 1))
                x_high(1, p * (NE + 1))
                with act.Fori(0, NE) as e:
                    it = p * NE + e
                    ix = p * (NE + 1) + e
                    for c in range(ECH):
                        act.wait_ge(landed[c % RAW], it * (16 * ECH // RAW) + (lbase[c % RAW] + 16 * (c // RAW + 1)))
                        act.wait_ge(q["w_used"], it * ECH + (c + 1))
                        nc.scalar.activation(hi[:, c % SPL, :], raw[:, c % RAW, :], ACT.Copy).then_inc(q["w_hi_ready"], 1)
                        if c == SPL - 1:
                            y_low()
                        if c == NCH + SPL - 1:
                            nc.scalar.activation(gu[:, 0, :], ps[:, 0, :], ACT.Copy).then_inc(q["gu_copied"], 1)
                    nc.scalar.activation(gu[:, 1, :], ps[:, 1, :], ACT.Copy).then_inc(q["gu_copied"], 1)
                    x_high(0, ix + 1)
                    act.wait_ge(q["gu_folded"], it + 1)
                    nc.scalar.activation(sig[:], ps[:, GB, 0:256].rearrange("p (k s) -> p k s", k=4), ACT.Sigmoid
                                         ).then_inc(q["sig_ready"], 1)
                    x_high(1, ix + 1)
                act.wait_ge(q["w_used"], p * (NE * ECH) + (NE * ECH + SPL))
                y_low()
            passes(act, body)

        @block.vector
        def _(dve):
            V = nc.vector

            def x_low(half, ix):
                dve.wait_ge(q["x_hi"], ix * 2 + (half + 1))
                V.tensor_tensor(xs[:, half * 8:half * 8 + 8, SLOTS:2 * SLOTS],
                                ps[:, XB, :].rearrange("p (k s) -> p k s", k=8),
                                xs[:, half * 8:half * 8 + 8, 0:SLOTS].bitcast(F32), ALU.subtract).then_inc(q["x_lo"], 1)

            def y_add(iy):
                dve.wait_ge(q["y_low"], iy + 1)
                dve.wait_ge(q["y_stored"], iy * 16)
                V.tensor_tensor(ysum[:].rearrange("p (a c) -> p a c", a=4), ps[0:SLOTS, YB:YB + 4, :],
                                yl[:].rearrange("p (a c) -> p a c", a=4), ALU.add).then_inc(q["y_sum"], 1)

            def body(p):
                dve.wait_ge(q["pass_done"], p + 1)
                V.tensor_scalar(rel[:], rt["rank"][:], rt["level"][:, bass.ds(p, 1)], None, ALU.subtract
                                ).then_inc(q["rel_ready"], 1)
                dve.wait_ge(q["rel_ready"], p + 1)
                for t in range(3):
                    dve.wait_ge(q["hot_used"], p * 3 + (t + 1))
                    V.tensor_tensor(hot[:], rt["slot"][:].rearrange("p (o s) -> p o s", o=1).to_broadcast([P, NE, SLOTS]),
                                    rel[:, t, :].rearrange("p (e o) -> p e o", o=1).to_broadcast([P, NE, SLOTS]),
                                    ALU.is_equal).then_inc(q["hot_ready"], 1)
                dve.wait_ge(q["hot_used"], p * 3 + 4)
                t2 = ps[0:SLOTS, GB, 0:2 * NE].rearrange("p (e i) -> p e i", i=2)
                V.tensor_scalar(tabs[:], t2, 0.0, NONE, ALU.is_equal, ALU.mult).then_inc(q["tabs_step"], 1)
                dve.wait_ge(q["tabs_step"], p + 1)
                V.scalar_tensor_tensor(gat[:, 0:NE], t2[:, :, 0], -1.0, tabs[:, :, 0], ALU.add, ALU.add
                                       ).then_inc(q["tabs_ready"], 1)
                V.scalar_tensor_tensor(sca[:, 1:NE + 1], t2[:, :, 1], -1.0, tabs[:, :, 1], ALU.add, ALU.add
                                       ).then_inc(q["tabs_ready"], 1)
                x_low(0, p * (NE + 1))
                x_low(1, p * (NE + 1))
                with dve.Fori(0, NE) as e:
                    it = p * NE + e
                    ix = p * (NE + 1) + e
                    for c in range(ECH):
                        dve.wait_ge(q["w_hi_ready"], it * ECH + (c + 1))
                        V.tensor_tensor(lo[:, c % SPL, :], raw[:, c % RAW, :], hi[:, c % SPL, :].bitcast(F32),
                                        ALU.subtract).then_inc(q["w_lo_ready"], 1)
                        if c == SPL - 1:
                            y_add(ix)
                    x_low(0, ix + 1)
                    g3 = ps[:, GB, 0:256].rearrange("p (k s) -> p k s", k=4)
                    u3 = ps[:, GB, 256:512].rearrange("p (k s) -> p k s", k=4)
                    dve.wait_ge(q["sig_ready"], it + 1)
                    V.tensor_tensor(hid[:], g3, sig[:], ALU.mult).then_inc(q["h_step"], 1)
                    dve.wait_ge(q["h_step"], it * 3 + 1)
                    V.tensor_tensor(hid[:], u3, hid[:], ALU.mult).then_inc(q["h_step"], 1)
                    dve.wait_ge(q["h_step"], it * 3 + 2)
                    V.tensor_copy(hs[:, :, 0:SLOTS], hid[:]).then_inc(q["h_step"], 1)
                    dve.wait_ge(q["h_step"], it * 3 + 3)
                    V.tensor_tensor(hs[:, :, SLOTS:2 * SLOTS], hid[:], hs[:, :, 0:SLOTS].bitcast(F32), ALU.subtract
                                    ).then_inc(q["h_ready"], 1)
                    x_low(1, ix + 1)
                y_add(p * (NE + 1) + NE)
            passes(dve, body)

        @block.tensor
        def _(pe):
            def x_turn(half, ix):
                pe.wait_ge(q["gathered"], ix * 16 + 16)
                pe.wait_ge(q["x_lo"], ix * 2 + (half + 1))
                pe.sem_inc(q["pe_tick"], 1)
                for k in range(8):
                    kk = half * 8 + k
                    last = nc.tensor.transpose(ps[:, XB, k * SLOTS:(k + 1) * SLOTS], xe[:, kk * P:(kk + 1) * P],
                                               core.ident[0:SLOTS, 0:SLOTS])
                last.then_inc(q["x_turned"], 1)

            def body(p):
                for t in range(3):
                    pe.wait_ge(q["hot_ready"], p * 3 + (t + 1))
                    for e in range(NE):
                        last = nc.tensor.matmul(ps[0:SLOTS, GB, 2 * e:2 * e + 2], hot[:, e, :], rt["ids"][:, t, e, :],
                                                start=(t == 0 and e == 0), stop=(t == 2), skip_group_check=True)
                    last.then_inc(q["hot_used"], 1)
                x_turn(0, p * (NE + 1))
                x_turn(1, p * (NE + 1))
                with pe.Fori(0, NE) as e:
                    it = p * NE + e
                    ix = p * (NE + 1) + e
                    pe.wait_ge(q["x_lo"], ix * 2 + 3)
                    for c in range(2 * NCH):
                        pe.wait_ge(q["w_lo_ready"], it * ECH + (c + 1 + RAW))
                        for k in range(CK):
                            for part in (hi, lo):
                                kk = (c % NCH) * CK + k
                                last = nc.tensor.matmul(ps[:, c // NCH, :], xs[:, kk, :],
                                                        part[:, c % SPL, k * GW:(k + 1) * GW],
                                                        start=(kk == 0 and part is hi), stop=(kk == KD - 1 and part is lo))
                        last.then_inc(q["w_used"], 1)
                    x_turn(0, ix + 1)
                    for i in range(2):
                        pe.wait_ge(q["gu_copied"], it * 2 + (i + 1))
                        for j in range(4):
                            last = nc.tensor.matmul(ps[:, GB, i * 256 + j * SLOTS:i * 256 + (j + 1) * SLOTS],
                                                    gu[:, i, j * P:(j + 1) * P], fold[:], start=True, stop=True)
                    last.then_inc(q["gu_folded"], 1)
                    pe.wait_ge(q["h_ready"], it + 1)
                    pe.wait_ge(q["y_sum"], ix + 1)
                    for j in range(4):
                        c = 2 * NCH + j
                        pe.wait_ge(q["w_lo_ready"], it * ECH + (c + 1 + RAW))
                        for part in (hi, lo):
                            for a in range(4):
                                last = nc.tensor.matmul(ps[:, YB + a, :], hs[:, j, :], part[:, c % SPL, a * GW:(a + 1) * GW],
                                                        start=(j == 0 and part is hi), stop=(j == 3 and part is lo))
                        last.then_inc(q["w_used"], 1)
                        if j == 0:
                            x_turn(1, ix + 1)
            passes(pe, body)

        @block.gpsimd
        def _(pool):
            def wait(sem, value):
                pool.wait_ge(sem, value)
                pool.sem_inc(q["pool_tick"], 1)

            def gather(column, ix):
                wait(q["x_turned"], ix * 2 + 2)
                nc.gpsimd.tensor_copy(gi[:], gat[:, column]).then_inc(q["gather_idx"], 1)
                wait(q["gather_idx"], ix + 1)
                pool.indirect_dma_start(out=xe[:], out_offset=None, in_=rows,
                                        in_offset=bass.IndirectOffsetOnAxis(ap=gi[:, 0:1], axis=0),
                                        bounds_check=NT - 1, oob_is_err=False).then_inc(q["gathered"], 16)

            def scatter(column, iy):
                wait(q["y_stored"], iy * 16)
                nc.gpsimd.tensor_copy(si[:], sca[:, column]).then_inc(q["scatter_idx"], 1)
                wait(q["scatter_idx"], iy + 1)
                wait(q["y_sum"], iy + 1)
                pool.indirect_dma_start(out=ydram, out_offset=bass.IndirectOffsetOnAxis(ap=si[:, 0:1], axis=0),
                                        in_=ysum[:], in_offset=None,
                                        bounds_check=2 * NT - 1, oob_is_err=False).then_inc(q["y_stored"], 16)

            def body(p):
                wait(q["tabs_ready"], p * 2 + 2)
                gather(slice(0, 1), p * (NE + 1))
                with pool.Fori(0, NE) as e:
                    ix = p * (NE + 1) + e
                    gather(bass.ds(e + 1, 1), ix + 1)
                    scatter(bass.ds(e, 1), ix)
                scatter(slice(NE, NE + 1), p * (NE + 1) + NE)
                wait(q["y_stored"], p * (16 * (NE + 1)) + 16 * (NE + 1))
                pool.sem_inc(q["pass_done"], 1)
            passes(pool, body)


def combine(core, rt, ydram, ctx):
    nc = core.nc
    yb = core.sb("yb", [P, 3, 2 * D], F32, ctx)
    landed = [core.sem(f"c_landed{t}") for t in range(3)]
    y2 = ydram.rearrange("(t i) d -> t (i d)", i=2)
    with nc.Block() as block:
        @block.sync
        def _(sp):
            for t, (t0, n) in enumerate(TILES):
                sp.dma_start(yb[0:n, t, :], y2[t0:t0 + n, :]).then_inc(landed[t], 16)

        @block.vector
        def _(dve):
            link = chain(dve, core.dve_chain)
            for t, (t0, n) in enumerate(TILES):
                dve.wait_ge(landed[t], 16)
                x = core.x_res[0:n, t, :]
                for i in range(2):
                    link(nc.vector.scalar_tensor_tensor(x, yb[0:n, t, i * D:(i + 1) * D], rt["wt"][0:n, i, t:t + 1], x,
                                                        ALU.mult, ALU.add))


def ple(core, w, xT, ctx):
    nc, ps = core.nc, core.ps
    S = lambda name, shape, dt=F32: core.sb(name, shape, dt, ctx)
    pin, pinT = S("pin", [P, 3, PLE]), S("pinT", [P, 2, NT])
    wp = S("wp", [P, 2, D])
    pp, gate = S("pp", [P, KD, NT]), S("ple_gate", [P, KD, NT])
    names = "e_loaded e_turned e_inT e_pp e_ppc e_mul".split()
    q = {n: core.sem(n) for n in names}
    with nc.Block() as block:
        @block.sync
        def _(sp):
            for t, (t0, n) in enumerate(TILES):
                src = w["p_prompt"][0, 0, t0:t0 + n, :] if t < 2 else w["p_sample"][0].rearrange("b s d -> (b s) d")
                sp.dma_start(pin[0:n, t, :], src).then_inc(q["e_loaded"], 16)
            sp.dma_start(wp[:], w["w_ple_proj"][0].rearrange("(k p) c -> p k c", p=P)).then_inc(q["e_loaded"], 16)
            load_groups(core, sp, w["w_ple_gate"][0], 0, 4)

        @block.tensor
        def _(pe):
            pe.wait_ge(q["e_loaded"], 64)
            for k in range(2):
                for t, (t0, n) in enumerate(TILES):
                    last = nc.tensor.transpose(ps[:, 4 + k, t0:t0 + n], pin[0:n, t, k * P:(k + 1) * P], core.ident[0:n, 0:n])
            last.then_inc(q["e_turned"], 1)
            pe.wait_ge(q["e_inT"], 1)
            for j in range(KD):
                if j >= 4:
                    pe.wait_ge(q["e_ppc"], j - 3)
                for k in range(2):
                    last = nc.tensor.matmul(ps[:, 4 + j % 4, 0:NT], wp[:, k, j * P:(j + 1) * P], pinT[:, k, :],
                                            start=(k == 0), stop=(k == 1))
                last.then_inc(q["e_pp"], 1)
            project_groups(core, pe, xT, 4)
            pe.wait_ge(q["e_mul"], 4)
            turn_back(core, pe, gate)

        @block.scalar
        def _(act):
            base = core.proj_groups
            with act.Fori(0, 4) as g:
                act.wait_ge(core.proj_done, g + (base + 1))
                nc.scalar.activation(gate[:, bass.ds(g * 4, 4), :], ps[:, 0:4, 0:NT], ACT.Sigmoid).then_inc(core.proj_copied, 2)

        @block.vector
        def _(dve):
            dve.wait_ge(q["e_turned"], 1)
            nc.vector.tensor_copy(pinT[:], ps[:, 4:6, 0:NT]).then_inc(q["e_inT"], 1)
            for j in range(KD):
                dve.wait_ge(q["e_pp"], j + 1)
                nc.vector.tensor_copy(pp[:, j, :], ps[:, 4 + j % 4, 0:NT]).then_inc(q["e_ppc"], 1)
            dve.wait_ge(q["e_ppc"], KD)
            base = core.proj_groups
            with dve.Fori(0, 4) as g:
                dve.wait_ge(core.proj_copied, g * 2 + (2 * base + 4))
                o = gate[:, bass.ds(g * 4, 4), :]
                nc.vector.tensor_tensor(o, o, pp[:, bass.ds(g * 4, 4), :], ALU.mult).then_inc(q["e_mul"], 1)
            add_turned(core, dve)
    core.raw_groups += 4
    core.proj_groups += 4


def final_norm(core, gain_row, out_p, out_s, ctx):
    nc = core.nc
    y = core.sb("y", [P, 3, D], F32, ctx)
    ss = core.sb("f_ss", [P, 3], F32, ctx)
    u = core.norm_runs
    ss_clear, squares, mean_ready, root_ready, rows_ready = core.norm_sems[:5]
    stored = core.sem("f_stored")
    with nc.Block() as block:
        @block.scalar
        def _(act):
            act.wait_ge(ss_clear, u + 1)
            for t, (_, n) in enumerate(TILES):
                nc.scalar.activation(y[0:n, t, :], core.x_res[0:n, t, :], ACT.Square,
                                     accum_out=ss[0:n, t:t + 1]).then_inc(squares, 1)
            act.wait_ge(mean_ready, u + 1)
            nc.scalar.activation(ss[:], ss[:], ACT.Sqrt).then_inc(root_ready, 1)

        @block.vector
        def _(dve):
            link = chain(dve, core.dve_chain)
            nc.vector.memset(ss[:], 1.0).then_inc(ss_clear, 1)
            dve.wait_ge(squares, u * 3 + 3)
            nc.vector.tensor_scalar(ss[:], ss[:], 1.0 / D, EPS, ALU.mult, ALU.add).then_inc(mean_ready, 1)
            dve.wait_ge(root_ready, u + 1)
            link(nc.vector.reciprocal(ss[:], ss[:]))
            for t, (_, n) in enumerate(TILES):
                nc.vector.scalar_tensor_tensor(y[0:n, t, :], core.x_res[0:n, t, :], ss[0:n, t:t + 1], gain_row[0:n, :],
                                               ALU.mult, ALU.mult).then_inc(rows_ready, 1)

        @block.sync
        def _(sp):
            for t, (t0, n) in enumerate(TILES):
                sp.wait_ge(rows_ready, u * 3 + t + 1)
                dst = out_p[0, t0:t0 + n, :] if t < 2 else out_s.rearrange("b s d -> (b s) d")
                sp.dma_start(dst, y[0:n, t, :]).then_inc(stored, 16)
            sp.wait_ge(stored, 48)


def load_row(core, dst, src, name):
    landed = core.sem(name)
    with core.nc.Block() as block:
        @block.sync
        def _(sp):
            sp.dma_start(dst, src.to_broadcast([P, D])).then_inc(landed, 16)
            sp.wait_ge(landed, 16)


def build(nc, w, out):
    with ExitStack() as ctx:
        core = Core(nc, ctx)
        core.x_res = core.sb("x_res", [P, 3, D])
        core.raw = core.sb("raw", [P, RAW, 2048])
        core.x_landed = core.sem("x_landed")
        core.gcols_turned = core.sem("gcols_turned")
        core.gcols_ready = core.sem("gcols_ready")
        rows = nc.dram_tensor("ffn_rows", (NT, D), F32, kind="Internal").ap()
        ydram = nc.dram_tensor("expert_rows", (2 * NT, D), F32, kind="Internal").ap()
        constants(core, w)

        with ExitStack() as mix:
            pT = core.sb("pT", [P, NPT, NT], F32, mix)
            gates = core.sb("gates", [MH, 2, NT], F32, mix)
            with ExitStack() as s:
                hT = core.sb("hT", [P, KD, NT], F32, s)
                core.wg8 = core.sb("wg8", [P, KD, 2 * MH], F32, s)
                with ExitStack() as s2:
                    xn = core.sb("xn", [P, 3, D], F32, s2)
                    norm_stage(core, xn, hT, s2, gain_cols=core.gcols[:, 0:16])
                mix_project(core, w, hT, pT, gates)
            mixT = core.sb("mixT", [P, KD, NT], F32, mix)
            with ExitStack() as s:
                attention(core, w, out, pT, mixT, s)
            with ExitStack() as s:
                mlstm(core, w, out, pT, mixT, gates, s)
            with ExitStack() as s:
                oT = core.sb("oT", [P, KD, NT], F32, s)
                out_project(core, w, mixT, oT)

        with ExitStack() as moe:
            rt = {"slot": core.sb("slot", [P, SLOTS], F32), "ids": core.sb("ids", [P, 3, NE, 2], F32),
                  "level": core.sb("level", [P, PASSES], F32), "wt": core.sb("wt_tok", [P, 2, 3], F32),
                  "rank": core.sb("rank", [P, 3, NE], F32), "need": core.sb("need", [P, PASSES], F32)}
            with ExitStack() as s:
                grow = core.sb("g_ffn_row", [P, D], F32, s)
                load_row(core, grow[:], w["g_ffn"], "g_ffn_landed")
                xn = core.sb("xn2", [P, 3, D], F32, s)
                xT = core.sb("xT2", [P, KD, NT], F32, s)
                norm_stage(core, xn, xT, s, gain_row=grow, rows_out=rows)
                router(core, w, xT, rt, s)
            with ExitStack() as s:
                experts(core, w, rt, rows, ydram, s)
            with ExitStack() as s:
                combine(core, rt, ydram, s)

        with ExitStack() as s:
            xn = core.sb("xn3", [P, 3, D], F32, s)
            xT = core.sb("xT3", [P, KD, NT], F32, s)
            norm_stage(core, xn, xT, s, gain_cols=core.gcols[:, 40:56])
            core.raw_landed = [core.sem(f"ple_landed{i}") for i in range(NCH)]
            core.landed_base = core.raw_groups
            ple(core, w, xT, s)
        with ExitStack() as s:
            grow = core.sb("g_final_row", [P, D], F32, s)
            load_row(core, grow[:], w["g_final"].rearrange("(o d) -> o d", o=1), "g_final_landed")
            final_norm(core, grow, out["y_prompt"], out["y_sample"], s)


_INS = ("x_prompt x_sample p_prompt p_sample state_mlstm_C state_mlstm_n state_mlstm_m state_swa_k state_swa_v "
        "g_mix w_in b_igate b_fgate g_mh attn_sinks w_out g_ffn w_router_g b_router_g w_router_e b_router_e "
        "w_gate w_up w_down g_ple w_ple_gate w_ple_proj g_final").split()
_STATE = {"C": (MH, DK, DK), "n": (MH, DK), "m": (MH,), "k": (WIN, KV, HD), "v": (WIN, KV, HD)}
_OUTS = {"y_prompt": (1, SEQ, D), "y_sample": (NS, 1, D),
         **{f"prompt_{n}": (1, 1, *s) for n, s in _STATE.items()},
         **{f"sample_{n}": (1, NS, *s) for n, s in _STATE.items()}}


def kernel(**inputs):
    import concourse.bacc as bacc
    from concourse.bass_utils import run_bass_kernel_spmd

    nc = bacc.Bacc("TRN2", target_bir_lowering=False, num_devices=1)
    arrays, w, out = {}, {}, {}
    for name in _INS:
        a = np.ascontiguousarray(inputs[name])
        arrays[f"in_{name}"] = a
        w[name] = nc.dram_tensor(f"in_{name}", a.shape, mybir.dt.from_np(a.dtype), kind="ExternalInput").ap()
    for name, shape in _OUTS.items():
        out[name] = nc.dram_tensor(f"out_{name}", shape, F32, kind="ExternalOutput").ap()
    build(nc, w, out)
    r = run_bass_kernel_spmd(nc, [arrays], core_ids=[0])
    return tuple(r.results[0][f"out_{name}"] for name in _OUTS)
```

```python
from contextlib import ExitStack

import numpy as np

import concourse.bass as bass
from concourse import mybir

F32 = mybir.dt.float32
F32R = mybir.dt.float32r
I32 = mybir.dt.int32
ALU = mybir.AluOpType
ACT = mybir.ActivationFunctionType
AX = mybir.AxisListType.X

P = 128
D = 2048
KD = D // P
SEQ, NS = 256, 8
NT = SEQ + NS
TILES = ((0, P), (P, P), (SEQ, NS))
MH, DK = 4, 256
AH, KV, HD = 16, 4, 64
WIN = 128
NG, NE, EPG = 4, 32, 8
DE = 512
PLE = 256
EPS = 1e-6
GW = 512
CK = 4
NCH = KD // CK
SLOTS = 32
PASSES = -(-NT // SLOTS)
RAW = 6
LEAD = 6
SPL = 3
ECH = 3 * NCH
NONE = 4096.0
BIG = 1.0e30

AQ0, AK0, AV0 = 0, 8, 10
MQ0, MK0, MV0, MO0 = 12, 20, 28, 36
NPT = 44
C_MQ, C_GATES, C_AQ = 0, 4096, 4104


class Counted:

    def __init__(self, sem):
        self.sem, self.n = sem, 0

    def inc(self, ins, by=1):
        ins.then_inc(self.sem, by)
        self.n += by
        return self.n


def chain(engine, counted):

    def link(ins):
        engine.wait_ge(counted.sem, counted.inc(ins))

    return link


class Core:

    def __init__(self, nc, ctx):
        self.nc, self.ctx = nc, ctx
        self.ps = ctx.enter_context(nc.psum_tensor("ps", [P, 8, 512], F32))
        self.act_chain = Counted(self.sem("act_chain"))
        self.dve_chain = Counted(self.sem("dve_chain"))
        self.pool_chain = Counted(self.sem("pool_chain"))
        self.raw_landed = [self.sem(f"raw_landed{i}") for i in range(RAW)]
        self.raw_free = self.sem("raw_free")
        self.raw_groups = 0
        self.landed_base = 0
        self.proj_done = self.sem("proj_done")
        self.proj_copied = self.sem("proj_copied")
        self.proj_groups = 0
        self.norm_runs = 0
        self.turned, self.added = self.sem("turned"), self.sem("added")
        self.turned_banks = 0
        self.norm_sems = [self.sem(f"norm_{n}") for n in
                          "ss_clear squares mean root rows turned stored copied0 copied1".split()]

    def sem(self, name):
        return self.ctx.enter_context(self.nc.semaphore(name))

    def sb(self, name, shape, dt=F32, ctx=None):
        return (ctx or self.ctx).enter_context(self.nc.sbuf_tensor(name, shape, dt))


def weight_group(w, col):
    return w.rearrange("(k p) c -> p k c", p=P)[:, :, col]


def load_groups(core, sp, w, first_col, count):
    base = core.raw_groups
    with sp.Fori(0, count) as g:
        for c in range(NCH):
            sp.wait_ge(core.raw_free, g * NCH + (base * NCH + c + 1))
            src = weight_group(w, bass.ds(g * GW + first_col, GW))[:, c * CK:(c + 1) * CK, :]
            dst = core.raw[:, c, :].rearrange("p (k c) -> p k c", k=CK)
            sp.dma_start(dst, src).then_inc(core.raw_landed[c], 16)


def project_groups(core, pe, xT, count):
    nc, ps = core.nc, core.ps
    base, done = core.raw_groups, core.proj_groups
    with pe.Fori(0, count) as g:
        pe.wait_ge(core.proj_copied, g * 2 + (done * 2 + 2))
        for c in range(NCH):
            pe.wait_ge(core.raw_landed[c], g * 16 + ((base - core.landed_base) * 16 + 16))
            for k in range(CK):
                for j in range(4):
                    last = nc.tensor.matmul(ps[:, j, 0:NT], core.raw[:, c, k * GW + j * P:k * GW + (j + 1) * P],
                                            xT[:, c * CK + k, :], start=(c == 0 and k == 0),
                                            stop=(c == NCH - 1 and k == CK - 1))
            last.then_inc(core.raw_free, 1)
        pe.wait_ge(core.raw_free, g * NCH + (base * NCH + 2 * NCH))
        pe.sem_inc(core.proj_done, 1)


def constants(core, w):
    nc = core.nc
    core.ident = core.sb("ident", [P, P])
    core.ones = core.sb("ones", [P, P])
    core.upper = core.sb("upper", [P, P])
    core.gcols = core.sb("gcols", [P, 56])
    core.eps = core.sb("eps", [P, 1])
    core.grows = core.sb("grows", [56, P])
    core.consts_ready = core.sem("consts_ready")
    core.grows_landed = core.sem("grows_landed")

    with nc.Block() as block:
        @block.gpsimd
        def _(pool):
            link = chain(pool, core.pool_chain)
            link(nc.gpsimd.memset(core.ident[:], 0.0))
            link(nc.gpsimd.memset(core.ones[:], 1.0))
            link(nc.gpsimd.memset(core.eps[:], EPS))
            link(nc.gpsimd.affine_select(out=core.ident[:], in_=core.ident[:], compare_op=ALU.not_equal,
                                         fill=1.0, base=0, pattern=[[-1, P]], channel_multiplier=1))
            link(nc.gpsimd.affine_select(out=core.upper[:], in_=core.ones[:], compare_op=ALU.is_gt,
                                         fill=0.0, base=0, pattern=[[1, P]], channel_multiplier=-1))
            pool.sem_inc(core.consts_ready, 1)

        @block.sync
        def _(sp):
            at = 0
            for name, n in (("g_mix", 16), ("g_mh", 8), ("g_ffn", 16), ("g_ple", 16)):
                sp.dma_start(core.grows[at:at + n, :], w[name].rearrange("l (k p) -> (l k) p", p=P)
                             ).then_inc(core.grows_landed, 16)
                at += n
            for t, (t0, n) in enumerate(TILES):
                src = w["x_prompt"][0, t0:t0 + n, :] if t < 2 else w["x_sample"].rearrange("b s d -> (b s) d")
                sp.dma_start(core.x_res[0:n, t, :], src).then_inc(core.x_landed, 16)
            sp.sem_inc(core.raw_free, NCH)
            sp.wait_ge(core.x_landed, 48)

        @block.vector
        def _(dve):
            dve.wait_ge(core.gcols_turned, 1)
            nc.vector.tensor_copy(core.gcols[:], core.ps[:, 0, 0:56]).then_inc(core.gcols_ready, 1)
            dve.sem_inc(core.proj_copied, 2)

        @block.tensor
        def _(pe):
            pe.wait_ge(core.consts_ready, 1)
            pe.wait_ge(core.grows_landed, 64)
            nc.tensor.transpose(core.ps[:, 0, 0:56], core.grows[:], core.ident[0:56, 0:56]
                                ).then_inc(core.gcols_turned, 1)


def norm_stage(core, xn, xT, ctx, gain_cols=None, gain_row=None, rows_out=None):
    nc, ps = core.nc, core.ps
    ss = core.sb(f"norm{core.norm_runs}_ss", [P, 3], F32, ctx)
    u = core.norm_runs
    core.norm_runs += 1
    ss_clear, squares, mean_ready, root_ready, rows_ready, turned, stored = core.norm_sems[:7]
    copied = core.norm_sems[7:9]

    def take(engine, k):
        engine.wait_ge(turned, u * KD + k + 1)
        src, dst = ps[:, k % 8, 0:NT], xT[:, k, :]
        if k % 2 == 0:
            scale = gain_cols[:, k:k + 1] if gain_cols is not None else 1.0
            nc.scalar.activation(dst, src, ACT.Copy, scale=scale).then_inc(copied[0], 1)
        elif gain_cols is not None:
            nc.vector.tensor_scalar(dst, src, gain_cols[:, k:k + 1], None, ALU.mult).then_inc(copied[1], 1)
        else:
            nc.vector.tensor_copy(dst, src).then_inc(copied[1], 1)

    with nc.Block() as block:
        @block.scalar
        def _(act):
            act.wait_ge(ss_clear, u + 1)
            for t, (_, n) in enumerate(TILES):
                nc.scalar.activation(xn[0:n, t, :], core.x_res[0:n, t, :], ACT.Square,
                                     accum_out=ss[0:n, t:t + 1]).then_inc(squares, 1)
            act.wait_ge(mean_ready, u + 1)
            nc.scalar.activation(ss[:], ss[:], ACT.Sqrt).then_inc(root_ready, 1)
            for k in range(0, KD, 2):
                take(act, k)

        @block.vector
        def _(dve):
            link = chain(dve, core.dve_chain)
            nc.vector.memset(ss[:], 1.0).then_inc(ss_clear, 1)
            dve.wait_ge(squares, u * 3 + 3)
            nc.vector.tensor_scalar(ss[:], ss[:], 1.0 / D, EPS, ALU.mult, ALU.add).then_inc(mean_ready, 1)
            dve.wait_ge(root_ready, u + 1)
            link(nc.vector.reciprocal(ss[:], ss[:]))
            for t, (_, n) in enumerate(TILES):
                if gain_row is None:
                    nc.vector.tensor_scalar(xn[0:n, t, :], core.x_res[0:n, t, :], ss[0:n, t:t + 1], None,
                                            ALU.mult).then_inc(rows_ready, 1)
                else:
                    nc.vector.scalar_tensor_tensor(xn[0:n, t, :], core.x_res[0:n, t, :], ss[0:n, t:t + 1],
                                                   gain_row[0:n, :], ALU.mult, ALU.mult).then_inc(rows_ready, 1)
            for k in range(1, KD, 2):
                take(dve, k)

        @block.tensor
        def _(pe):
            pe.wait_ge(rows_ready, u * 3 + 3)
            for k in range(KD):
                if k >= 8:
                    pe.wait_ge(copied[k % 2], u * (KD // 2) + (k - 8) // 2 + 1)
                for t, (t0, n) in enumerate(TILES):
                    last = nc.tensor.transpose(ps[:, k % 8, t0:t0 + n], xn[0:n, t, k * P:(k + 1) * P],
                                               core.ident[0:n, 0:n])
                last.then_inc(turned, 1)

        if rows_out is not None:
            @block.sync
            def _(sp):
                sp.wait_ge(rows_ready, u * 3 + 3)
                for t, (t0, n) in enumerate(TILES):
                    sp.dma_start(rows_out[t0:t0 + n, :], xn[0:n, t, :]).then_inc(stored, 16)
                sp.wait_ge(stored, 48)


def mix_project(core, w, hT, pT, gates):
    nc, ps = core.nc, core.ps
    wi = w["w_in"][0]
    wg8 = core.wg8
    gates_landed = core.sem("gates_landed")
    gates_done = core.sem("gates_done")
    gates_copied = core.sem("gates_copied")
    parts = ((C_AQ, AQ0, 3), (C_MQ, MQ0, 8))
    start_groups, start_proj = core.raw_groups, core.proj_groups

    with nc.Block() as block:
        def reset():
            core.raw_groups, core.proj_groups = start_groups, start_proj

        def through(fn):
            reset()
            for col, tile, count in parts:
                fn(col, tile, count)
                core.raw_groups += count
                core.proj_groups += count

        @block.sync
        def _(sp):
            sp.dma_start(wg8[:], wi.rearrange("(k p) c -> p k c", p=P)[:, :, C_GATES:C_GATES + 2 * MH]
                         ).then_inc(gates_landed, 16)
            through(lambda col, tile, count: load_groups(core, sp, wi, col, count))

        @block.tensor
        def _(pe):
            pe.wait_ge(gates_landed, 16)
            for b in range(2):
                for k in range(KD):
                    last = nc.tensor.matmul(ps[0:MH, 4 + b, 0:NT], wg8[:, k, b * MH:(b + 1) * MH], hT[:, k, :],
                                            start=(k == 0), stop=(k == KD - 1))
            last.then_inc(gates_done, 1)
            through(lambda col, tile, count: project_groups(core, pe, hT, count))

        def copies(engine, copy, banks):
            def part(col, tile, count):
                done = core.proj_groups
                with engine.Fori(0, count) as g:
                    engine.wait_ge(core.proj_done, g + (done + 1))
                    copy(pT[:, bass.ds(g * 4 + (tile + banks), 2), :], ps[:, banks:banks + 2, 0:NT]
                         ).then_inc(core.proj_copied, 1)
            through(part)

        @block.scalar
        def _(act):
            copies(act, lambda o, i: nc.scalar.activation(o, i, ACT.Copy), 0)

        @block.vector
        def _(dve):
            dve.wait_ge(gates_done, 1)
            nc.vector.tensor_copy(gates[:], ps[0:MH, 4:6, 0:NT]).then_inc(gates_copied, 1)
            copies(dve, lambda o, i: nc.vector.tensor_copy(o, i), 2)


def attention(core, w, out, pT, mixT, ctx):
    nc, ps = core.nc, core.ps
    S = lambda name, shape, dt=F32: core.sb(name, shape, dt, ctx)
    kswp = S("kswp", [P, 2, NT])
    avtok = S("avtok", [P, 2, 256])
    aktok = S("aktok", [P, 256])
    new_kv = S("new_kv", [NS, 2, 256])
    mask = S("mask", [P, 256])
    sinks = S("sinks", [P, AH])
    sink16 = S("sink16", [AH, 1])
    spread = S("spread", [AH, P])
    sm = S("sm", [P, 2, 4, 256])
    small = S("small", [P, 2, 6, 4])
    prT = S("prT", [P, 8, P])
    kv = S("kv", [P, 2, NS, 256])
    kT = S("kT", [P, 2, 2 * NS, P])
    sT = S("sT", [P, P])
    sq = S("sq", [P, P])
    st = S("st", [P, 8])

    names = ("a_const a_swap a_rows a_rowsT a_sinks a_win a_new a_stored a_scores a_shift a_exp "
             "a_prob a_turn a_turned a_pv a_mixed s_keysT s_kcopy s_scores s_sT s_turn s_prob s_back "
             "s_pT s_pv a_bias a_bias2 s_straight").split()
    q = {n: core.sem(n) for n in names}

    def span(b):
        return 128 * (b + 1)

    with nc.Block() as block:
        @block.gpsimd
        def _(pool):
            link = chain(pool, core.pool_chain)
            link(nc.gpsimd.memset(mask[:], 0.0))
            link(nc.gpsimd.affine_select(out=mask[:], in_=mask[:], compare_op=ALU.is_ge, fill=-BIG,
                                         base=P, pattern=[[-1, 256]], channel_multiplier=1))
            link(nc.gpsimd.affine_select(out=mask[:], in_=mask[:], compare_op=ALU.is_gt, fill=-BIG,
                                         base=0, pattern=[[1, 256]], channel_multiplier=-1))
            link(nc.gpsimd.memset(spread[:], 0.0))
            link(nc.gpsimd.affine_select(out=spread[:].rearrange("p (b h) -> p b h", b=NS),
                                         in_=spread[:].rearrange("p (b h) -> p b h", b=NS),
                                         compare_op=ALU.not_equal, fill=1.0, base=0,
                                         pattern=[[0, NS], [1, AH]], channel_multiplier=-1))
            pool.sem_inc(q["a_const"], 1)

        @block.sync
        def _(sp):
            sp.dma_start(sinks[:], w["attn_sinks"].to_broadcast([P, AH])).then_inc(q["a_sinks"], 16)
            sp.dma_start(sink16[:], w["attn_sinks"].rearrange("l h -> h l")).then_inc(q["a_sinks"], 16)
            for i, name in enumerate(("state_swa_k", "state_swa_v")):
                rows = w[name][0].rearrange("b s h d -> s b (h d)")
                for a, b in ((0, 112), (112, 127)):
                    sp.dma_start(kv[a:b, i, :, :], rows[a + 1:b + 1]).then_inc(q["a_win"], 16)
            sp.wait_ge(q["a_rows"], 2)
            for i in range(2):
                sp.dma_start(kv[127:128, i, :, :], new_kv[:, i, :]).then_inc(q["a_new"], 16)
            sp.dma_start(out["prompt_k"][0, 0].rearrange("s h d -> s (h d)"), aktok[:]).then_inc(q["a_stored"], 16)
            sp.dma_start(out["prompt_v"][0, 0].rearrange("s h d -> s (h d)"), avtok[:, 1, :]).then_inc(q["a_stored"], 16)
            sp.wait_ge(q["a_win"], 64)
            sp.wait_ge(q["a_new"], 32)
            for i, name in enumerate(("sample_k", "sample_v")):
                sp.dma_start(out[name][0].rearrange("b s h d -> s b (h d)"), kv[:, i, :, :]).then_inc(q["a_stored"], 16)
            sp.wait_ge(q["a_stored"], 64)

        @block.tensor
        def _(pe):
            for i in range(2):
                for b in range(2):
                    nc.tensor.transpose(ps[:, 7, b * 256 + i * P:b * 256 + (i + 1) * P],
                                        pT[:, AV0 + i, b * P:(b + 1) * P], core.ident[:])
                nc.tensor.transpose(ps[:, 6, i * P:(i + 1) * P], pT[:, AK0 + i, P:SEQ], core.ident[:])
                nc.tensor.transpose(ps[0:NS, 6, 256 + i * P:256 + (i + 1) * P], pT[:, AK0 + i, SEQ:NT], core.ident[:])
                last = nc.tensor.transpose(ps[0:NS, 5, i * P:(i + 1) * P], pT[:, AV0 + i, SEQ:NT], core.ident[:])
            last.then_inc(q["a_rowsT"], 1)
            pe.wait_ge(q["a_swap"], 2)

            def scores(u):
                g, b = divmod(u, 2)
                if u >= 2:
                    pe.wait_ge(q["a_shift"], 2 * u - 2)
                for i in range(4):
                    h = 4 * g + i
                    lo = (h % 2) * HD
                    keys = pT[lo:lo + HD, AK0 + g // 2, 0:span(b)] if h % 2 == g % 2 else kswp[lo:lo + HD, g // 2, 0:span(b)]
                    last = nc.tensor.matmul(ps[:, 2 * (u % 2) + i % 2, (i // 2) * 256:(i // 2) * 256 + span(b)],
                                            pT[lo:lo + HD, AQ0 + h // 2, b * P:(b + 1) * P], keys,
                                            start=True, stop=True)
                last.then_inc(q["a_scores"], 1)

            def turn(u):
                b = u % 2
                pe.wait_ge(q["a_prob"], u + 1)
                if u == 0:
                    pe.wait_ge(q["a_rows"], 2)
                if u >= 1:
                    pe.wait_ge(q["a_turned"], u)
                for i in range(4):
                    for kb in range(b + 1):
                        n = i * 2 + kb
                        last = nc.tensor.transpose(ps[:, 4 + n // 4, (n % 4) * P:(n % 4 + 1) * P],
                                                   sm[:, u % 2, i, kb * P:(kb + 1) * P], core.ident[:])
                last.then_inc(q["a_turn"], 1)

            def values(u):
                g, b = divmod(u, 2)
                pe.wait_ge(q["a_turned"], u + 1)
                if u >= 2:
                    pe.wait_ge(q["a_mixed"], u - 1)
                for i in range(4):
                    lo = (i % 2) * HD
                    for kb in range(b + 1):
                        last = nc.tensor.matmul(ps[lo:lo + HD, 6 + u % 2, (i // 2) * P:(i // 2 + 1) * P],
                                                avtok[:, kb, g * HD:(g + 1) * HD], prT[:, i * 2 + kb, :],
                                                start=(kb == 0), stop=(kb == b))
                last.then_inc(q["a_pv"], 1)

            scores(0)
            for u in range(8):
                if u + 1 < 8:
                    scores(u + 1)
                turn(u)
                values(u)

            pe.wait_ge(q["a_win"], 64)
            pe.wait_ge(q["a_new"], 32)
            pe.wait_ge(q["a_shift"], 16)
            for n in range(2 * NS):
                last = nc.tensor.transpose(ps[:, n // 4, (n % 4) * P:(n % 4 + 1) * P],
                                           kv[:, 0, n // 2, (n % 2) * P:(n % 2 + 1) * P], core.ident[:])
                if n % 4 == 3:
                    last.then_inc(q["s_keysT"], 1)
            pe.wait_ge(q["a_const"], 1)
            pe.wait_ge(q["a_sinks"], 32)
            pe.wait_ge(q["a_turned"], 8)
            nc.tensor.matmul(ps[:, 5, 256:257], spread[:], sink16[:], start=True, stop=True)
            pe.wait_ge(q["s_kcopy"], 8)
            for b in range(NS):
                for g in range(KV):
                    for par in range(2):
                        lo = par * HD
                        keys = kT[lo:lo + HD, int(par != g % 2), 2 * b + g // 2, :]
                        c = b * (AH // 2) + 2 * g
                        last = nc.tensor.matmul(ps[:, par, c:c + 2], keys,
                                                pT[lo:lo + HD, AQ0 + 2 * g:AQ0 + 2 * g + 2, SEQ + b],
                                                start=True, stop=True)
            last.then_inc(q["s_scores"], 1)
            pe.wait_ge(q["s_sT"], 1)
            nc.tensor.transpose(ps[:, 5, 0:P], sT[:], core.ident[:]).then_inc(q["s_turn"], 1)
            pe.wait_ge(q["s_prob"], 1)
            nc.tensor.transpose(ps[:, 5, 128:256], sq[:], core.ident[:]).then_inc(q["s_back"], 1)
            pe.wait_ge(q["s_pT"], 1)
            pe.wait_ge(q["a_mixed"], 8)
            for b in range(NS):
                for g in range(KV):
                    last = nc.tensor.matmul(ps[0:HD, 6, b * AH + 4 * g:b * AH + 4 * g + 4],
                                            kv[:, 1, b, g * HD:(g + 1) * HD], sT[:, b * AH + 4 * g:b * AH + 4 * g + 4],
                                            start=True, stop=True)
            last.then_inc(q["s_pv"], 1)

        @block.scalar
        def _(act):
            act.wait_ge(q["a_rowsT"], 1)
            nc.scalar.activation(avtok[:], ps[:, 7, :].rearrange("p (b c) -> p b c", b=2), ACT.Copy
                                 ).then_inc(q["a_rows"], 1)

            def turned(u):
                b = u % 2
                act.wait_ge(q["a_turn"], u + 1)
                if u >= 1:
                    act.wait_ge(q["a_pv"], u)
                src = ps[:, 4:6, :].rearrange("p a (i k c) -> p (a i) k c", k=2, c=P)[:, :, 0:b + 1, :]
                dst = prT[:].rearrange("p (i k) c -> p i k c", k=2)[:, :, 0:b + 1, :]
                nc.scalar.activation(dst, src, ACT.Copy).then_inc(q["a_turned"], 1)

            def mixed(u):
                g, b = divmod(u, 2)
                act.wait_ge(q["a_pv"], u + 1)
                nc.scalar.activation(mixT[:, 8 + 2 * g:10 + 2 * g, b * P:(b + 1) * P],
                                     ps[:, 6 + u % 2, 0:256].rearrange("p (i c) -> p i c", i=2), ACT.Copy
                                     ).then_inc(q["a_mixed"], 1)

            for u in range(8):
                b = u % 2
                act.wait_ge(q["a_bias"], u + 1)
                for i in range(4):
                    nc.scalar.activation(sm[:, u % 2, i, 0:span(b)], sm[:, u % 2, i, 0:span(b)], ACT.Exp,
                                         bias=small[:, u % 2, 1, i:i + 1], accum_out=small[:, u % 2, 3, i:i + 1])
                nc.scalar.activation(small[:, u % 2, 2, :], small[:, u % 2, 2, :], ACT.Exp).then_inc(q["a_exp"], 1)
                turned(u)
                mixed(u)
            link = chain(act, core.act_chain)
            for n in range(4):
                act.wait_ge(q["s_keysT"], n + 1)
                src = ps[:, n, :].rearrange("p (i c) -> p i c", i=4)
                nc.scalar.activation(kT[:, 0, 4 * n:4 * n + 4, :], src, ACT.Copy).then_inc(q["s_straight"], 1)
                nc.scalar.activation(kT[0:HD, 1, 4 * n:4 * n + 4, :], src[HD:P], ACT.Copy).then_inc(q["s_kcopy"], 1)
            act.wait_ge(q["s_scores"], 1)
            nc.scalar.activation(sT[:].rearrange("p (c a) -> p a c", a=2), ps[:, 0:2, 0:P // 2], ACT.Copy,
                                 scale=HD ** -0.5).then_inc(q["s_sT"], 1)
            act.wait_ge(q["a_bias2"], 1)
            link(nc.scalar.activation(sq[:], ps[:, 5, 0:P], ACT.Exp, bias=st[:, 1:2], accum_out=st[:, 3:4]))
            nc.scalar.activation(st[:, 2:3], st[:, 2:3], ACT.Exp).then_inc(q["a_exp"], 1)
            act.wait_ge(q["s_back"], 1)
            nc.scalar.activation(sT[:], ps[:, 5, 128:256], ACT.Copy).then_inc(q["s_pT"], 1)
            act.wait_ge(q["s_pv"], 1)
            for par in range(2):
                src = ps[0:HD, 6, 0:P].rearrange("p (b j q) -> p q j b", b=NS, q=2)[:, par]
                link(nc.scalar.activation(mixT[par * HD:(par + 1) * HD, 8:16, SEQ:NT], src, ACT.Copy))

        @block.vector
        def _(dve):
            link = chain(dve, core.dve_chain)
            nc.vector.tensor_copy(kswp[0:HD], pT[HD:P, AK0:AK0 + 2, :]).then_inc(q["a_swap"], 1)
            nc.vector.tensor_copy(kswp[HD:P], pT[0:HD, AK0:AK0 + 2, :]).then_inc(q["a_swap"], 1)
            dve.wait_ge(q["a_rowsT"], 1)
            link(nc.vector.tensor_copy(aktok[:], ps[:, 6, 0:256]))
            link(nc.vector.tensor_copy(new_kv[:, 0, :], ps[0:NS, 6, 256:512]))
            nc.vector.tensor_copy(new_kv[:, 1, :], ps[0:NS, 5, 0:256]).then_inc(q["a_rows"], 1)
            dve.wait_ge(q["a_const"], 1)
            dve.wait_ge(q["a_sinks"], 32)
            for u in range(8):
                g, b = divmod(u, 2)
                s, m = sm[:, u % 2, :, 0:span(b)], small[:, u % 2]
                dve.wait_ge(q["a_scores"], u + 1)
                if u >= 2:
                    dve.wait_ge(q["a_turn"], u - 1)
                msk = mask[:, 256 - span(b):256].rearrange("p (o c) -> p o c", o=1).to_broadcast([P, 2, span(b)])
                for a in range(2):
                    src = ps[:, 2 * (u % 2) + a, :].rearrange("p (i c) -> p i c", i=2)[:, :, 0:span(b)]
                    nc.vector.scalar_tensor_tensor(sm[:, u % 2, a::2, 0:span(b)], src, HD ** -0.5, msk, ALU.mult, ALU.add
                                                   ).then_inc(q["a_shift"], 1)
                dve.wait_ge(q["a_shift"], 2 * u + 2)
                link(nc.vector.tensor_reduce(m[:, 0, :], s, AX, ALU.max))
                link(nc.vector.tensor_tensor(m[:, 0, :], m[:, 0, :], sinks[:, 4 * g:4 * g + 4], ALU.max))
                link(nc.vector.tensor_tensor(m[:, 2, :], sinks[:, 4 * g:4 * g + 4], m[:, 0, :], ALU.subtract))
                nc.vector.tensor_scalar(m[:, 1, :], m[:, 0, :], -1.0, None, ALU.mult).then_inc(q["a_bias"], 1)
                dve.wait_ge(q["a_exp"], u + 1)
                link(nc.vector.tensor_tensor(m[:, 4, :], m[:, 3, :], m[:, 2, :], ALU.add))
                link(nc.vector.reciprocal(m[:, 5, :], m[:, 4, :]))
                nc.vector.tensor_tensor(s, s, m[:, 5, :].rearrange("p (i o) -> p i o", o=1).to_broadcast([P, 4, span(b)]),
                                        ALU.mult).then_inc(q["a_prob"], 1)
            for n in range(4):
                dve.wait_ge(q["s_straight"], n + 1)
                nc.vector.tensor_copy(kT[HD:P, 1, 4 * n:4 * n + 4, :], kT[0:HD, 0, 4 * n:4 * n + 4, :]).then_inc(q["s_kcopy"], 1)
            dve.wait_ge(q["s_turn"], 1)
            link(nc.vector.tensor_reduce(st[:, 0:1], ps[:, 5, 0:P], AX, ALU.max))
            link(nc.vector.tensor_tensor(st[:, 0:1], st[:, 0:1], ps[:, 5, 256:257], ALU.max))
            link(nc.vector.tensor_tensor(st[:, 2:3], ps[:, 5, 256:257], st[:, 0:1], ALU.subtract))
            nc.vector.tensor_scalar(st[:, 1:2], st[:, 0:1], -1.0, None, ALU.mult).then_inc(q["a_bias2"], 1)
            dve.wait_ge(q["a_exp"], 9)
            link(nc.vector.tensor_tensor(st[:, 4:5], st[:, 3:4], st[:, 2:3], ALU.add))
            link(nc.vector.reciprocal(st[:, 5:6], st[:, 4:5]))
            nc.vector.tensor_scalar(sq[:], sq[:], st[:, 5:6], None, ALU.mult).then_inc(q["s_prob"], 1)


def mlstm(core, w, out, pT, mixT, gates, ctx):
    nc, ps = core.nc, core.ps
    S = lambda name, shape, dt=F32: core.sb(name, shape, dt, ctx)
    ktok = S("ktok", [P, 2, 4 * DK])
    vaug = S("vaug", [P, 2, MH, DK + 1])
    skq = S("skq", [NS, 2, 4 * DK])
    bi, bf = S("bi", [MH, 1]), S("bf", [MH, 1])
    lf = S("lf", [MH, NT])
    t1, t2 = S("t1", [MH, NT]), S("t2", [MH, NT])
    fsum, amax = S("fsum", [MH, SEQ]), S("amax", [MH, SEQ])
    arow = S("arow", [MH, 3, SEQ])
    cols = S("cols", [P, 3, 2, MH])
    mend = S("mend", [MH, 2])
    sel = S("sel", [NS, NS, P])
    causal = S("causal", [P, 256])
    et = S("et", [P, 2, 384])
    wt = S("wt", [P, 2, 384])
    hh = core.raw[:, NCH, :].rearrange("p (b h k) -> p b h k", b=2, h=MH)
    vw = S("vw", [P, 2, DK])
    col = S("col", [P, 6, 8])
    cout = S("cout", [P, 2, 2, DK])
    nout = S("nout", [1, MH, DK])
    sg = S("sg", [NS, 10, MH])
    n0, n1 = S("n0", [NS, MH, DK]), S("n1", [NS, MH, DK])
    diag = S("diag", [NS, 3, NS, MH])
    tab = S("tab", [P, 3, NS, MH])
    vd = S("vd", [P, 8, NS])
    num = S("num", [P, 8, NS])
    nsq = S("nsq", [P, 8, NS])
    cst = core.raw[:, 0:NCH, :]
    landed_before = 16 * (core.raw_groups - core.landed_base)
    junk, prod = wt[:, 0, 0:DK], et[:, 0, 0:DK]

    names = ("m_small m_const m_rowsT m_rows m_lf1 m_lf2 m_arow m_colsT m_cols m_en m_mb m_e1 m_e2 m_st m_wt "
             "m_num m_den m_root m_hh m_hT m_mix m_vw m_c m_cout m_cst0 m_cst1 m_nn m_sig m_sT m_sg1 "
             "m_sg2 m_diag m_tabT m_tab m_kq m_cdec m_cnew m_num2 m_sqs m_ssum m_root2 "
             "m_stored m_cstored m_nrec").split()
    q = {n: core.sem(n) for n in names}

    with nc.Block() as block:
        @block.gpsimd
        def _(pool):
            link = chain(pool, core.pool_chain)
            link(nc.gpsimd.memset(vaug[:, :, :, DK:DK + 1], 1.0))
            link(nc.gpsimd.memset(sel[:], 0.0))
            link(nc.gpsimd.affine_select(out=sel[:], in_=sel[:], compare_op=ALU.not_equal, fill=1.0,
                                         base=0, pattern=[[1, NS], [0, P]], channel_multiplier=-1))
            link(nc.gpsimd.memset(causal[:], 0.0))
            link(nc.gpsimd.affine_select(out=causal[:], in_=causal[:], compare_op=ALU.is_ge, fill=-BIG,
                                         base=0, pattern=[[1, 256]], channel_multiplier=-1))
            pool.sem_inc(q["m_const"], 1)

        @block.sync
        def _(sp):
            sp.dma_start(bi[:], w["b_igate"].rearrange("l h -> h l")).then_inc(q["m_small"], 16)
            sp.dma_start(bf[:], w["b_fgate"].rearrange("l h -> h l")).then_inc(q["m_small"], 16)
            sp.dma_start(sg[:, 0, :], w["state_mlstm_m"][0]).then_inc(q["m_small"], 16)
            sp.dma_start(n0[:], w["state_mlstm_n"][0]).then_inc(q["m_small"], 16)

            def state(ap, b):
                return ap[0, b].rearrange("h (v p) k -> p (h v) k", p=P)

            def slot(b):
                return cst[:, b % NCH, :].rearrange("p (t k) -> p t k", k=DK)

            def load(b):
                sp.dma_start(slot(b), state(w["state_mlstm_C"], b)).then_inc(core.raw_landed[b % NCH], 16)

            for b in range(NCH):
                load(b)
            for h in range(MH):
                sp.wait_ge(q["m_cout"], h + 1)
                sp.dma_start(out["prompt_C"][0, 0, h].rearrange("(v p) k -> p v k", p=P), cout[:, h % 2]
                             ).then_inc(q[f"m_cst{h % 2}"], 16)
            sp.wait_ge(q["m_nn"], 2)
            sp.dma_start(out["prompt_n"][0], nout[:]).then_inc(q["m_stored"], 16)
            sp.dma_start(out["prompt_m"].rearrange("l b h -> h (l b)"), mend[:, 1:2]).then_inc(q["m_stored"], 16)
            sp.wait_ge(q["m_nrec"], 1)
            sp.dma_start(out["sample_n"][0], n1[:]).then_inc(q["m_stored"], 16)
            sp.dma_start(out["sample_m"][0], sg[:, 5, :]).then_inc(q["m_stored"], 16)
            for b in range(NS):
                if b >= 1 and b - 1 + NCH < NS:
                    sp.wait_ge(q["m_cstored"], 16 * b)
                    sp.wait_ge(q["m_num2"], 8 * b)
                    load(b - 1 + NCH)
                sp.wait_ge(q["m_cnew"], 8 * (b + 1))
                sp.dma_start(state(out["sample_C"], b), slot(b)).then_inc(q["m_cstored"], 16)
            for i in range(2):
                sp.wait_ge(q[f"m_cst{i}"], 16 * (MH // 2))
            sp.wait_ge(q["m_stored"], 64)
            sp.wait_ge(q["m_cstored"], 16 * NS)

        jobs = [(MK0, 0, t) for t in range(3)] + [(MK0, 4, t) for t in range(3)]
        jobs += [(MV0, 0, t) for t in range(2)] + [(MV0, 4, t) for t in range(2)]
        jobs += [(MQ0, 0, 2), (MQ0, 4, 2)]

        @block.tensor
        def _(pe):
            for n, (tile, off, t) in enumerate(jobs):
                t0, rows = TILES[t]
                if n >= 4:
                    pe.wait_ge(q["m_rows"], n - 3)
                for i in range(4):
                    last = nc.tensor.transpose(ps[0:rows, n % 4, i * P:(i + 1) * P],
                                               pT[:, tile + off + i, t0:t0 + rows], core.ident[:])
                last.then_inc(q["m_rowsT"], 1)
            pe.wait_ge(q["m_arow"], 3)
            for kind in range(3):
                for b in range(2):
                    c = (kind * 2 + b) * MH
                    last = nc.tensor.transpose(ps[:, 4, c:c + MH], arow[:, kind, b * P:(b + 1) * P],
                                               core.ident[0:MH, 0:MH])
            last.then_inc(q["m_colsT"], 1)
            nc.tensor.transpose(ps[0:NS, 5, 0:MH], t1[:, SEQ:NT], core.ident[0:MH, 0:MH])
            nc.tensor.transpose(ps[0:NS, 5, MH:2 * MH], lf[:, SEQ:NT], core.ident[0:MH, 0:MH]).then_inc(q["m_sT"], 1)
            pe.wait_ge(q["m_const"], 1)
            pe.wait_ge(q["m_rows"], len(jobs))

            def scores(h):
                if h >= 2:
                    pe.wait_ge(q["m_e1"], h - 1)
                nc.tensor.matmul(ps[:, h % 2, 0:SEQ], sel[0:MH, h, :], amax[:], start=True, stop=True
                                 ).then_inc(q["m_mb"], 1)
                if h >= 2:
                    pe.wait_ge(q["m_wt"], h - 1)
                for s in range(2):
                    o = ps[:, 2 + h % 2, 0:256] if s == 0 else ps[:, 2 + h % 2, 256:384]
                    for j in range(2):
                        last = nc.tensor.matmul(o, pT[:, MK0 + 2 * h + j, s * P:(s + 1) * P],
                                                pT[:, MQ0 + 2 * h + j, s * P:SEQ], start=(j == 0), stop=(j == 1))
                last.then_inc(q["m_st"], 1)

            def values(h):
                pe.wait_ge(q["m_wt"], h + 1)
                if h >= 1:
                    pe.wait_ge(q["m_den"], 2 * h)
                for t in range(2):
                    for s in range(t + 1):
                        lhs = wt[:, h % 2, t * P:(t + 1) * P] if s == 0 else wt[:, h % 2, 256:384]
                        last = nc.tensor.matmul(ps[:, 6 + t, 0:DK + 1], lhs, vaug[:, s, h, :],
                                                start=(s == 0), stop=(s == t))
                last.then_inc(q["m_num"], 1)

            scores(0)
            for h in range(MH):
                if h + 1 < MH:
                    scores(h + 1)
                values(h)
            pe.wait_ge(q["m_cols"], 1)
            pe.wait_ge(q["m_sg1"], 1)
            for h in range(MH):
                if h >= 2:
                    pe.wait_ge(q["m_cout"], h - 1)
                for b in range(2):
                    pe.wait_ge(q["m_vw"], 2 * h + b + 1)
                    for v in range(2):
                        last = nc.tensor.matmul(ps[:, 4 + h % 2, v * DK:(v + 1) * DK], vw[:, b, v * P:(v + 1) * P],
                                                ktok[:, b, h * DK:(h + 1) * DK], start=(b == 0 and v == 0),
                                                stop=(b == 1), skip_group_check=True)
                    if b == 1:
                        last.then_inc(q["m_c"], 1)
                for b in range(2):
                    last = nc.tensor.matmul(ps[0:1, 2 + h // 2, (h % 2) * DK:(h % 2 + 1) * DK], cols[:, 2, b, h:h + 1],
                                            ktok[:, b, h * DK:(h + 1) * DK], start=(b == 0), stop=(b == 1))
                if h % 2:
                    last.then_inc(q["m_hT"], 1)
            pe.wait_ge(q["m_diag"], 1)
            pe.wait_ge(q["m_cout"], MH)
            nc.tensor.matmul(ps[:, 4, 0:96], core.ones[0:NS, :], diag[:].rearrange("p a b h -> p (a b h)"),
                             start=True, stop=True).then_inc(q["m_tabT"], 1)
            pe.wait_ge(q["m_hh"], 1)
            for j in range(8):
                if j >= 2:
                    pe.wait_ge(q["m_mix"], j - 1)
                for b in range(2):
                    last = nc.tensor.transpose(ps[:, 6 + j % 2, b * P:(b + 1) * P],
                                               hh[:, b, j // 2, (j % 2) * P:(j % 2 + 1) * P], core.ident[:])
                last.then_inc(q["m_hT"], 1)
            pe.wait_ge(q["m_nn"], 2)
            for b in range(NS):
                if b == 1:
                    pe.wait_ge(q["m_mix"], 8)
                    pe.wait_ge(q["m_tab"], 1)
                if b >= 2:
                    pe.wait_ge(q["m_num2"], 8 * (b - 1))
                for kq in range(2):
                    for i in range(2):
                        last = nc.tensor.matmul(ps[:, 4 * (b % 2) + 2 * kq + i, :], sel[:, b, :], skq[:, kq, i * 512:(i + 1) * 512],
                                                start=True, stop=True)
                last.then_inc(q["m_kq"], 1)
            pe.wait_ge(q["m_sqs"], 1)
            v4 = nsq[:].rearrange("p (h v) b -> p v h b", v=2)
            for v in range(2):
                last = nc.tensor.matmul(ps[:, 5, 0:32], core.ones[:], v4[:, v], start=(v == 0), stop=(v == 1))
            last.then_inc(q["m_ssum"], 1)

        @block.scalar
        def _(act):
            link = chain(act, core.act_chain)
            for n, (tile, off, t) in enumerate(jobs):
                act.wait_ge(q["m_rowsT"], n + 1)
                rows = TILES[t][1]
                src = ps[0:rows, n % 4, :]
                if t == 2:
                    dst = skq[:, int(tile == MQ0), off * P:off * P + 512]
                elif tile == MK0:
                    dst = ktok[:, t, off * P:off * P + 512]
                else:
                    dst = vaug[:, t, off // 2:off // 2 + 2, 0:DK]
                    src = src.rearrange("p (h c) -> p h c", h=2)
                nc.scalar.activation(dst, src, ACT.Copy).then_inc(q["m_rows"], 1)
            act.wait_ge(q["m_lf1"], 1)
            link(nc.scalar.activation(t2[:], t2[:], ACT.Exp, scale=-1.0))
            nc.scalar.activation(t2[:], t2[:], ACT.Ln, bias=1.0).then_inc(q["m_lf2"], 1)
            act.wait_ge(q["m_arow"], 2)
            nc.scalar.activation(arow[:, 2, :], arow[:, 2, :], ACT.Exp).then_inc(q["m_en"], 1)
            act.wait_ge(q["m_cols"], 1)
            nc.scalar.activation(col[:, 0, :], cols[:, 1].rearrange("p b h -> p (b h)"), ACT.Exp).then_inc(q["m_en"], 1)
            for h in range(MH):
                act.wait_ge(q["m_e1"], h + 1)
                for s in range(2):
                    o = et[:, h % 2, 0:256] if s == 0 else et[:, h % 2, 256:384]
                    ins = nc.scalar.activation(o, o, ACT.Exp, bias=cols[:, 0, s, h:h + 1])
                ins.then_inc(q["m_e2"], 1)
            act.wait_ge(q["m_sg1"], 1)
            nc.scalar.activation(sg[:, 6:9, :], sg[:, 6:9, :], ACT.Exp).then_inc(q["m_sg2"], 1)
            act.wait_ge(q["m_den"], 8)
            for b in range(2):
                for h in range(MH):
                    link(nc.scalar.activation(junk, hh[:, b, h, :], ACT.Square, accum_out=col[:, 3, b * MH + h:b * MH + h + 1]))
            nc.scalar.activation(col[:, 4, :], col[:, 3, :], ACT.Sqrt, scale=1.0 / DK, bias=core.eps[:]).then_inc(q["m_root"], 1)
            for j in range(2):
                act.wait_ge(q["m_hT"], j + 1)
                link(nc.scalar.activation(nout[:, 2 * j:2 * j + 2, :], ps[0:1, 2 + j, :].rearrange("p (h c) -> p h c", h=2),
                                     ACT.Copy))
                act.sem_inc(q["m_nn"], 1)
            nc.scalar.activation(pT[:, MO0:MO0 + 8, :], pT[:, MO0:MO0 + 8, :], ACT.Sigmoid).then_inc(q["m_sig"], 1)
            act.wait_ge(q["m_tab"], 1)
            for b in range(NS):
                act.wait_ge(core.raw_landed[b % NCH], landed_before + 16 * (b // NCH + 1))
                for h in range(MH):
                    c = cst[:, b % NCH, h * 512:(h + 1) * 512]
                    nc.scalar.activation(c, c, ACT.Copy, scale=tab[:, 0, b, h:h + 1]).then_inc(q["m_cdec"], 1)
            act.wait_ge(q["m_ssum"], 1)
            nc.scalar.activation(vd[:, 0:4, :], ps[:, 5, 0:32].rearrange("p (h b) -> p h b", h=MH), ACT.Sqrt,
                                 scale=1.0 / DK, bias=core.eps[:]).then_inc(q["m_root2"], 1)

        @block.vector
        def _(dve):
            link = chain(dve, core.dve_chain)
            V = nc.vector
            dve.wait_ge(q["m_small"], 64)
            link(V.tensor_scalar(t1[:], gates[:, 1, :], bf[:], -1.0, ALU.add, ALU.mult))
            V.scalar_tensor_tensor(t2[:], t1[:], -1.0, t1[:], ALU.mult, ALU.max).then_inc(q["m_lf1"], 1)
            dve.wait_ge(q["m_lf2"], 1)
            link(V.scalar_tensor_tensor(lf[:], t1[:], 0.0, t2[:], ALU.max, ALU.add))
            link(V.tensor_scalar(lf[:], lf[:], -1.0, None, ALU.mult))
            link(V.tensor_scalar(t1[:], gates[:, 0, :], bi[:], None, ALU.add))
            dve.wait_ge(q["m_const"], 1)
            link(V.tensor_tensor_scan(fsum[:], core.ones[0:MH, 0:1].to_broadcast([MH, SEQ]), lf[:, 0:SEQ], 0.0, ALU.mult, ALU.add))
            link(V.tensor_tensor(arow[:, 0, :], t1[:, 0:SEQ], fsum[:], ALU.subtract))
            link(V.tensor_tensor_scan(amax[:], arow[:, 0, :], arow[:, 0, :], 0.0, ALU.max, ALU.max))
            V.scalar_tensor_tensor(arow[:, 1, :], fsum[:], -1.0, amax[:], ALU.mult, ALU.subtract).then_inc(q["m_arow"], 1)
            link(V.tensor_copy(mend[:, 0:1], amax[:, SEQ - 1:SEQ]))
            link(V.tensor_tensor(mend[:, 1:2], mend[:, 0:1], fsum[:, SEQ - 1:SEQ], ALU.add))
            V.tensor_scalar(arow[:, 2, :], arow[:, 0, :], mend[:, 0:1], None, ALU.subtract).then_inc(q["m_arow"], 1)
            dve.wait_ge(q["m_en"], 1)
            V.tensor_scalar(arow[:, 2, :], arow[:, 2, :], DK ** -0.5, None, ALU.mult).then_inc(q["m_arow"], 1)
            dve.wait_ge(q["m_colsT"], 1)
            V.tensor_copy(cols[:].rearrange("p a b h -> p (a b h)"), ps[:, 4, 0:24]).then_inc(q["m_cols"], 1)
            dve.wait_ge(q["m_sT"], 1)
            link(V.tensor_copy(sg[:, 1:3, :], ps[0:NS, 5, 0:8].rearrange("p (a h) -> p a h", a=2)))
            link(V.tensor_tensor(sg[:, 3, :], sg[:, 1, :], sg[:, 2, :], ALU.subtract))
            link(V.tensor_tensor(sg[:, 4, :], sg[:, 0, :], sg[:, 3, :], ALU.max))
            link(V.tensor_tensor(sg[:, 5, :], sg[:, 2, :], sg[:, 4, :], ALU.add))
            link(V.tensor_tensor(sg[:, 6, :], sg[:, 0, :], sg[:, 4, :], ALU.subtract))
            link(V.tensor_tensor(sg[:, 7, :], sg[:, 3, :], sg[:, 4, :], ALU.subtract))
            V.tensor_scalar(sg[:, 8, :], sg[:, 5, :], -1.0, None, ALU.mult).then_inc(q["m_sg1"], 1)
            for h in range(MH):
                dve.wait_ge(q["m_mb"], h + 1)
                if h >= 2:
                    dve.wait_ge(q["m_wt"], h - 1)
                link(V.scalar_tensor_tensor(et[:, h % 2, 0:256], ps[:, h % 2, 0:256], -1.0, causal[:], ALU.mult, ALU.add))
                V.scalar_tensor_tensor(et[:, h % 2, 256:384], ps[:, h % 2, P:256], -1.0, causal[:, 0:P],
                                       ALU.mult, ALU.add).then_inc(q["m_e1"], 1)
                dve.wait_ge(q["m_e2"], h + 1)
                dve.wait_ge(q["m_st"], h + 1)
                if h >= 2:
                    dve.wait_ge(q["m_num"], h - 1)
                V.scalar_tensor_tensor(wt[:, h % 2], ps[:, 2 + h % 2, 0:384], DK ** -0.5, et[:, h % 2],
                                       ALU.mult, ALU.mult).then_inc(q["m_wt"], 1)
                dve.wait_ge(q["m_num"], h + 1)
                dve.wait_ge(q["m_en"], 2)
                for b in range(2):
                    i = b * MH + h
                    den, rec = col[:, 1, i:i + 1], col[:, 2, i:i + 1]
                    link(V.tensor_copy(rec, ps[:, 6 + b, DK:DK + 1]))
                    link(V.scalar_tensor_tensor(den, rec, -1.0, rec, ALU.mult, ALU.max))
                    link(V.tensor_tensor(den, den, col[:, 0, i:i + 1], ALU.max))
                    link(V.reciprocal(rec, den))
                    link(V.tensor_scalar(hh[:, b, h, :], ps[:, 6 + b, 0:DK], rec, None, ALU.mult))
                    dve.sem_inc(q["m_den"], 1)
            for h in range(MH):
                for b in range(2):
                    if h >= 1:
                        dve.wait_ge(q["m_c"], h)
                    V.tensor_scalar(vw[:, b, :], vaug[:, b, h, 0:DK], cols[:, 2, b, h:h + 1], None, ALU.mult
                                    ).then_inc(q["m_vw"], 1)
                if h >= 2:
                    dve.wait_ge(q[f"m_cst{h % 2}"], 16 * (h // 2))
                dve.wait_ge(q["m_c"], h + 1)
                V.tensor_copy(cout[:, h % 2], ps[:, 4 + h % 2, :].rearrange("p (v k) -> p v k", v=2)).then_inc(q["m_cout"], 1)
            dve.wait_ge(q["m_root"], 1)
            link(V.reciprocal(col[:, 5, :], col[:, 4, :]))
            for b in range(2):
                for h in range(MH):
                    link(V.tensor_scalar(hh[:, b, h, :], hh[:, b, h, :], col[:, 5, b * MH + h:b * MH + h + 1], None, ALU.mult))
            dve.sem_inc(q["m_hh"], 1)
            dve.wait_ge(q["m_sg2"], 1)
            link(V.tensor_scalar(sg[:, 7, :], sg[:, 7, :], DK ** -0.5, None, ALU.mult))
            wide = lambda i: sg[:, i, :].rearrange("p (h o) -> p h o", o=1).to_broadcast([NS, MH, DK])
            kk, qq = (skq[:, i, :].rearrange("p (h k) -> p h k", h=MH) for i in range(2))
            dve.wait_ge(q["m_rows"], len(jobs))
            link(V.tensor_tensor(n0[:], n0[:], wide(6), ALU.mult))
            link(V.tensor_tensor(n1[:], kk, wide(7), ALU.mult))
            link(V.tensor_tensor(n1[:], n1[:], n0[:], ALU.add))
            dve.sem_inc(q["m_nrec"], 1)
            link(V.tensor_tensor(n0[:], n1[:], qq, ALU.mult))
            link(V.tensor_reduce(sg[:, 9, :], n0[:], AX, ALU.add))
            link(V.scalar_tensor_tensor(sg[:, 9, :], sg[:, 9, :], -1.0, sg[:, 9, :], ALU.mult, ALU.max))
            link(V.tensor_tensor(sg[:, 9, :], sg[:, 9, :], sg[:, 8, :], ALU.max))
            link(V.reciprocal(sg[:, 9, :], sg[:, 9, :]))
            eye = core.ident[0:NS, 0:NS].rearrange("p (b o) -> p b o", o=1).to_broadcast([NS, NS, MH])
            for i, row in enumerate((6, 7, 9)):
                link(V.tensor_tensor(diag[:, i], eye, sg[:, row, :].rearrange("p (o h) -> p o h", o=1).to_broadcast([NS, NS, MH]),
                                     ALU.mult))
            dve.sem_inc(q["m_diag"], 1)
            dve.wait_ge(q["m_tabT"], 1)
            V.tensor_copy(tab[:].rearrange("p a b h -> p (a b h)"), ps[:, 4, 0:96]).then_inc(q["m_tab"], 1)
            dve.wait_ge(q["m_tab"], 1)
            by_head = lambda i: tab[:, i].rearrange("p b h -> p h b")
            for v in range(2):
                link(V.tensor_tensor(vd[:].rearrange("p (h v) b -> p v h b", v=2)[:, v],
                                     pT[:, MV0:MV0 + 8, SEQ:NT].rearrange("p (h v) b -> p v h b", v=2)[:, v],
                                     by_head(1), ALU.mult))
            dve.wait_ge(q["m_sig"], 1)
            for j in range(8):
                dve.wait_ge(q["m_hT"], 2 + j + 1)
                V.scalar_tensor_tensor(mixT[:, j, 0:SEQ], ps[:, 6 + j % 2, 0:SEQ], core.gcols[:, 16 + j:17 + j],
                                       pT[:, MO0 + j, 0:SEQ], ALU.mult, ALU.mult).then_inc(q["m_mix"], 1)
            for b in range(NS):
                dve.wait_ge(q["m_kq"], b + 1)
                for t in range(8):
                    h = t // 2
                    c = cst[:, b % NCH, t * DK:(t + 1) * DK]
                    if t % 2 == 0:
                        dve.wait_ge(q["m_cdec"], b * MH + h + 1)
                    V.scalar_tensor_tensor(c, ps[:, 4 * (b % 2) + h // 2, (h % 2) * DK:(h % 2 + 1) * DK], vd[:, t, b:b + 1], c,
                                           ALU.mult, ALU.add).then_inc(q["m_cnew"], 1)
                for t in range(8):
                    h = t // 2
                    c = cst[:, b % NCH, t * DK:(t + 1) * DK]
                    dve.wait_ge(q["m_cnew"], b * 8 + t + 1)
                    if b or t:
                        dve.wait_ge(q["m_num2"], b * 8 + t)
                    V.tensor_tensor_reduce(prod, c, ps[:, 4 * (b % 2) + 2 + h // 2, (h % 2) * DK:(h % 2 + 1) * DK], 1.0, 0.0,
                                           ALU.mult, ALU.add, num[:, t, b:b + 1]).then_inc(q["m_num2"], 1)
            dve.wait_ge(q["m_num2"], 8 * NS)
            for v in range(2):
                o = num[:].rearrange("p (h v) b -> p v h b", v=2)[:, v]
                link(V.tensor_tensor(o, o, by_head(2), ALU.mult))
            V.tensor_tensor(nsq[:], num[:], num[:], ALU.mult).then_inc(q["m_sqs"], 1)
            dve.wait_ge(q["m_root2"], 1)
            link(V.reciprocal(vd[:, 0:4, :], vd[:, 0:4, :]))
            for v in range(2):
                o = num[:].rearrange("p (h v) b -> p v h b", v=2)[:, v]
                link(V.tensor_tensor(o, o, vd[:, 0:4, :], ALU.mult))
            link(V.tensor_tensor(num[:], num[:], core.gcols[:, 16:24].rearrange("p (j o) -> p j o", o=1).to_broadcast([P, 8, NS]),
                                 ALU.mult))
            link(V.tensor_tensor(mixT[:, 0:8, SEQ:NT], num[:], pT[:, MO0:MO0 + 8, SEQ:NT], ALU.mult))


    core.landed_base -= NS // NCH


def out_project(core, w, mixT, oT):
    nc, ps = core.nc, core.ps
    wo = w["w_out"][0]
    with nc.Block() as block:
        @block.sync
        def _(sp):
            load_groups(core, sp, wo, 0, 4)

        @block.tensor
        def _(pe):
            project_groups(core, pe, mixT, 4)
            pe.wait_ge(core.proj_copied, 2 * (core.proj_groups + 4) + 2)
            turn_back(core, pe, oT)

        @block.scalar
        def _(act):
            base = core.proj_groups
            with act.Fori(0, 4) as g:
                act.wait_ge(core.proj_done, g + (base + 1))
                nc.scalar.activation(oT[:, bass.ds(g * 4, 2), :], ps[:, 0:2, 0:NT], ACT.Copy).then_inc(core.proj_copied, 1)

        @block.vector
        def _(dve):
            base = core.proj_groups
            with dve.Fori(0, 4) as g:
                dve.wait_ge(core.proj_done, g + (base + 1))
                nc.vector.tensor_copy(oT[:, bass.ds(g * 4 + 2, 2), :], ps[:, 2:4, 0:NT]).then_inc(core.proj_copied, 1)
            add_turned(core, dve)
    core.turned_banks += 12
    core.raw_groups += 4
    core.proj_groups += 4


def turn_back(core, pe, oT):
    nc, ps = core.nc, core.ps
    base, n = core.turned_banks, 0
    for t, (t0, rows) in enumerate(TILES):
        for j in range(4):
            if n >= 4:
                pe.wait_ge(core.added, base + n - 3)
            for i in range(4):
                last = nc.tensor.transpose(ps[0:rows, 4 + n % 4, i * P:(i + 1) * P], oT[:, 4 * j + i, t0:t0 + rows],
                                           core.ident[:])
            last.then_inc(core.turned, 1)
            n += 1


def add_turned(core, dve):
    nc, ps = core.nc, core.ps
    base, n = core.turned_banks, 0
    for t, (t0, rows) in enumerate(TILES):
        for j in range(4):
            dve.wait_ge(core.turned, base + n + 1)
            x = core.x_res[0:rows, t, j * 512:(j + 1) * 512]
            nc.vector.tensor_tensor(x, x, ps[0:rows, 4 + n % 4, :], ALU.add).then_inc(core.added, 1)
            n += 1


def router(core, w, xT, rt, ctx):
    nc, ps = core.nc, core.ps
    S = lambda name, shape, dt=F32: core.sb(name, shape, dt, ctx)
    NL = NG + NE
    wr = S("wr", [P, KD, NL])
    br = S("br", [1, NL])
    lg = S("lg", [P, 3, NL])
    a, b4 = S("ra", [P, 3, NG]), S("rb", [P, 3, NG])
    el, e1, e2 = S("el", [P, 3, NE]), S("e1", [P, 3, NE]), S("e2", [P, 3, NE])
    c = S("rc", [P, 10, 3])
    down4, down32 = S("down4", [P, NG]), S("down32", [P, NE])
    valid = S("valid", [P, 3])
    both = S("both", [P, 3, NE])
    names = "r_loaded r_const r_logits r_exp1 r_exp2 r_in1 r_in2 r_rank r_ranked".split()
    q = {n: core.sem(n) for n in names}
    with nc.Block() as block:
        @block.gpsimd
        def _(pool):
            link = chain(pool, core.pool_chain)
            link(nc.gpsimd.iota(down4[:], pattern=[[-1, NG]], base=NG, channel_multiplier=0, allow_small_or_imprecise_dtypes=True))
            link(nc.gpsimd.iota(down32[:], pattern=[[-1, NE]], base=NE, channel_multiplier=0, allow_small_or_imprecise_dtypes=True))
            link(nc.gpsimd.memset(valid[:], 1.0))
            link(nc.gpsimd.affine_select(out=valid[:, 2:3], in_=valid[:, 2:3], compare_op=ALU.is_gt, fill=0.0,
                                         base=NS, pattern=[[0, 1]], channel_multiplier=-1))
            link(nc.gpsimd.memset(lg[:, 2, :], 0.0))
            link(nc.gpsimd.iota(rt["slot"][:], pattern=[[1, SLOTS]], base=0, channel_multiplier=0, allow_small_or_imprecise_dtypes=True))
            link(nc.gpsimd.iota(rt["ids"][:, :, :, 0], pattern=[[P, 3], [0, NE]], base=1, channel_multiplier=1, allow_small_or_imprecise_dtypes=True))
            link(nc.gpsimd.iota(rt["ids"][:, :, :, 1], pattern=[[2 * P, 3], [0, NE]], base=1, channel_multiplier=2, allow_small_or_imprecise_dtypes=True))
            link(nc.gpsimd.iota(rt["level"][:], pattern=[[SLOTS, PASSES]], base=0, channel_multiplier=0, allow_small_or_imprecise_dtypes=True))
            pool.sem_inc(q["r_const"], 1)

        @block.sync
        def _(sp):
            sp.dma_start(wr[:, :, 0:NG], w["w_router_g"][0].rearrange("(k p) c -> p k c", p=P)).then_inc(q["r_loaded"], 16)
            sp.dma_start(wr[:, :, NG:NL], w["w_router_e"][0].rearrange("(k p) c -> p k c", p=P)).then_inc(q["r_loaded"], 16)
            sp.dma_start(br[:, 0:NG], w["b_router_g"]).then_inc(q["r_loaded"], 16)
            sp.dma_start(br[:, NG:NL], w["b_router_e"]).then_inc(q["r_loaded"], 16)

        @block.tensor
        def _(pe):
            pe.wait_ge(q["r_loaded"], 64)
            for t, (t0, n) in enumerate(TILES):
                for k in range(KD):
                    nc.tensor.matmul(ps[0:n, t, 0:NL], xT[:, k, t0:t0 + n], wr[:, k, :], start=(k == 0), stop=False)
                nc.tensor.matmul(ps[0:n, t, 0:NL], core.ones[0:1, 0:n], br[:], start=False, stop=True).then_inc(q["r_logits"], 1)
            pe.wait_ge(q["r_rank"], 1)
            for t in range(3):
                nc.tensor.matmul(ps[:, 3, t * NE:(t + 1) * NE], core.upper[:], both[:, t, :], start=True, stop=(t == 0))
                for s in range(t):
                    nc.tensor.matmul(ps[:, 3, t * NE:(t + 1) * NE], core.ones[:], both[:, s, :], start=False, stop=(s == t - 1))
            for t in range(3):
                last = nc.tensor.matmul(ps[:, 4, 0:NE], core.ones[:], both[:, t, :], start=(t == 0), stop=(t == 2))
            last.then_inc(q["r_ranked"], 1)

        @block.scalar
        def _(act):
            act.wait_ge(q["r_in1"], 1)
            nc.scalar.activation(a[:], a[:], ACT.Exp).then_inc(q["r_exp1"], 1)
            act.wait_ge(q["r_in2"], 1)
            nc.scalar.activation(c[:, 5, :], c[:, 5, :], ACT.Exp).then_inc(q["r_exp2"], 1)

        @block.vector
        def _(dve):
            link = chain(dve, core.dve_chain)
            V = nc.vector
            wide = lambda row, n: row.rearrange("p (t o) -> p t o", o=1).to_broadcast([P, 3, n])
            over = lambda row, n: row.rearrange("p (o e) -> p o e", o=1).to_broadcast([P, 3, n])
            dve.wait_ge(q["r_const"], 1)
            dve.wait_ge(q["r_logits"], 3)
            link(V.tensor_copy(lg[:, 0:2, :], ps[:, 0:2, 0:NL]))
            link(V.tensor_copy(lg[0:NS, 2, :], ps[0:NS, 2, 0:NL]))
            gl, le = lg[:, :, 0:NG], lg[:, :, NG:NL]

            def first_max(src, n, top, onehot, tmp, down):
                link(V.tensor_reduce(top, src, AX, ALU.max))
                link(V.tensor_tensor(tmp, src, wide(top, n), ALU.is_equal))
                link(V.tensor_tensor(tmp, tmp, over(down[:], n), ALU.mult))
                link(V.tensor_reduce(c[:, 9, :], tmp, AX, ALU.max))
                link(V.tensor_tensor(onehot, tmp, wide(c[:, 9, :], n), ALU.is_equal))

            first_max(gl, NG, c[:, 0, :], b4[:], a[:], down4)
            V.tensor_tensor(a[:], gl, wide(c[:, 0, :], NG), ALU.subtract).then_inc(q["r_in1"], 1)
            dve.wait_ge(q["r_exp1"], 1)
            link(V.tensor_reduce(c[:, 1, :], a[:], AX, ALU.add))
            link(V.reciprocal(c[:, 2, :], c[:, 1, :]))
            link(V.tensor_scalar(b4[:], b4[:], 1.0, BIG, ALU.subtract, ALU.mult))
            for t in range(3):
                link(V.tensor_tensor(el[:, t, :].rearrange("p (g e) -> p g e", g=NG), le[:, t, :].rearrange("p (g e) -> p g e", g=NG),
                                     b4[:, t, :].rearrange("p (g o) -> p g o", o=1).to_broadcast([P, NG, EPG]), ALU.add))
            first_max(el[:], NE, c[:, 3, :], e1[:], both[:], down32)
            link(V.scalar_tensor_tensor(el[:], e1[:], -2.0 * BIG, el[:], ALU.mult, ALU.add))
            first_max(el[:], NE, c[:, 4, :], e2[:], both[:], down32)
            V.tensor_tensor(c[:, 5, :], c[:, 4, :], c[:, 3, :], ALU.subtract).then_inc(q["r_in2"], 1)
            dve.wait_ge(q["r_exp2"], 1)
            link(V.tensor_scalar(c[:, 6, :], c[:, 5, :], 1.0, None, ALU.add))
            link(V.reciprocal(c[:, 7, :], c[:, 6, :]))
            link(V.tensor_tensor(rt["wt"][:, 0, :], c[:, 7, :], c[:, 2, :], ALU.mult))
            link(V.tensor_tensor(rt["wt"][:, 1, :], rt["wt"][:, 0, :], c[:, 5, :], ALU.mult))
            link(V.tensor_tensor(both[:], e1[:], e2[:], ALU.add))
            link(V.tensor_tensor(both[:], both[:], wide(valid[:], NE), ALU.mult))
            dve.sem_inc(q["r_rank"], 1)
            link(V.tensor_tensor(rt["ids"][:, :, :, 1], rt["ids"][:, :, :, 1], e2[:], ALU.add))
            dve.wait_ge(q["r_ranked"], 1)
            link(V.tensor_tensor(el[:], ps[:, 3, 0:3 * NE].rearrange("p (t e) -> p t e", t=3), both[:], ALU.mult))
            link(V.tensor_scalar(both[:], both[:], 1.0, 1.0e6, ALU.subtract, ALU.mult))
            link(V.tensor_tensor(rt["rank"][:], el[:], both[:], ALU.add))
            link(V.tensor_reduce(c[:, 8, 0:1], ps[:, 4, 0:NE], AX, ALU.max))
            link(V.tensor_tensor(rt["need"][:], c[:, 8, 0:1].to_broadcast([P, PASSES]), rt["level"][:], ALU.is_gt))


def experts(core, w, rt, rows, ydram, ctx):
    nc, ps, raw = core.nc, core.ps, core.raw
    S = lambda name, shape, dt=F32: core.sb(name, shape, dt, ctx)
    hi, lo = S("w_hi", [P, SPL, 2048], F32R), S("w_lo", [P, SPL, 2048], F32R)
    xs = S("x_split", [P, KD, 2 * SLOTS], F32R)
    xd = S("x_direct", [P, CK, SLOTS])
    hs = S("h_split", [P, 4, 2 * SLOTS], F32R)
    xe = S("xe", [SLOTS, D])
    gu = S("gu", [2 * SLOTS, 2, DE])
    sig, hid = S("sig", [P, 4, SLOTS]), S("hid", [P, 4, SLOTS])
    yl, ysum = S("yl", [SLOTS, D]), S("ysum", [SLOTS, D])
    fold = S("fold", [2 * SLOTS, SLOTS])
    hot = S("hot", [P, NE, SLOTS])
    rel = S("rel", [P, 3, NE])
    tabs = S("tabs", [SLOTS, NE, 2])
    gat, sca = S("gat", [SLOTS, NE + 1], I32), S("sca", [SLOTS, NE + 1], I32)
    gi, si = S("gi", [SLOTS, 1], I32), S("si", [SLOTS, 1], I32)
    flag = S("flag", [1, PASSES], I32)
    names = ("w_hi_ready w_lo_ready w_used direct_used rel_ready hot_ready hot_used tabs_step tabs_ready "
             "gather_idx gathered x_turned x_hi x_lo gu_copied gu_folded sig_ready h_step h_ready "
             "y_low y_sum scatter_idx y_stored pass_done pool_tick pe_tick").split()
    q = {n: core.sem(n) for n in names}
    landed = core.raw_landed
    lbase = [16 * (core.raw_groups - core.landed_base)] * NCH + [0] * (RAW - NCH)
    wg = w["w_gate"][0].rearrange("e (k p) c -> e p k c", p=P)
    wu = w["w_up"][0].rearrange("e (k p) c -> e p k c", p=P)
    wd = w["w_down"][0].rearrange("e (k p) c -> e p k c", p=P)
    XB, GB, YB = 3, 2, 4

    with nc.Block() as block:
        @block.gpsimd
        def _(pool):
            link = chain(pool, core.pool_chain)
            link(nc.gpsimd.memset(xe[:], 0.0))
            link(nc.gpsimd.tensor_copy(fold[0:SLOTS, :], core.ident[0:SLOTS, 0:SLOTS]))
            link(nc.gpsimd.tensor_copy(fold[SLOTS:2 * SLOTS, :], core.ident[SLOTS:2 * SLOTS, SLOTS:2 * SLOTS]))
            link(nc.gpsimd.memset(gat[:, NE:NE + 1], int(NONE)))
            link(nc.gpsimd.memset(sca[:, 0:1], int(NONE)))
            pool.sem_inc(q["pass_done"], 1)

        @block.vector
        def _(dve):
            link = chain(dve, core.dve_chain)
            link(nc.vector.tensor_copy(flag[:], rt["need"][0:1, :]))
            link(nc.vector.memset(ps[:, YB:YB + 4, :], 0.0))
            dve.sem_inc(q["x_lo"], 1)

        @block.tensor
        def _(pe):
            pe.sem_inc(q["w_used"], SPL)
            pe.sem_inc(q["x_turned"], 1)
            pe.sem_inc(q["hot_used"], 1)

        @block.sync
        def _(sp):
            sp.sem_inc(q["w_lo_ready"], LEAD)
            sp.sem_inc(q["direct_used"], 1)

    def passes(engine, body):
        with engine.Fori(0, PASSES) as p:
            need = engine.value_load(flag[0:1, bass.ds(p, 1)], min_val=0, max_val=1)
            with engine.If(need > 0):
                body(p)

    DIRECT = 1
    WHOLE = (0, 2, 3)

    def landing(m, i, n):
        at = m * NCH + i
        slot = at % RAW
        return slot, n * (16 * ECH // RAW) + (lbase[slot] + 16 * (at // RAW + 1))

    def slot_free(m, i, n):
        at = m * NCH + i - RAW
        back = at < 0
        m0, i0 = divmod(at % ECH, NCH)
        if i0 == DIRECT:
            return q["direct_used"], n * 3 + (m0 + 1 + 1 - 3 * back)
        return q["w_lo_ready"], n * (3 * SPL) + (m0 * SPL + WHOLE.index(i0) + 1 + LEAD - 3 * SPL * back)

    def split_count(m, r, n, ahead=0):
        return n * (3 * SPL) + (m * SPL + r + 1 + ahead)

    def skip(engine, sem, done, by):
        engine.wait_ge(sem, done)
        engine.sem_inc(sem, by)

    with nc.Block() as block:
        @block.sync
        def _(sp):
            def load(m, e, n):
                for i in range(NCH):
                    sp.wait_ge(*slot_free(m, i, n))
                    slot, _ = landing(m, i, n)
                    if m < 2:
                        src = (wg, wu)[m][bass.ds(e, 1), :, i * CK:(i + 1) * CK, :].rearrange("o p k c -> (o p) k c")
                        dst = raw[:, slot, :].rearrange("p (k c) -> p k c", k=CK)
                    else:
                        src, dst = wd[bass.ds(e, 1), :, i, :].rearrange("o p c -> (o p) c"), raw[:, slot, :]
                    sp.dma_start(dst, src).then_inc(landed[slot], 16)

            def body(p):
                n = p * (NE + 1)
                load(0, 0, n)
                load(1, 0, n)
                for i in range(NCH):
                    slot, value = landing(2, i, n)
                    skip(sp, landed[slot], p * (32 * (NE + 1)) + (lbase[slot] + 16), 16)
                with sp.Fori(1, NE) as e:
                    n = p * (NE + 1) + e
                    load(0, e, n)
                    load(1, e, n)
                    load(2, e - 1, n)
                n = p * (NE + 1) + NE
                for slot in range(RAW):
                    skip(sp, landed[slot], n * 32 + lbase[slot], 32 if slot < 2 * NCH - RAW else 16)
                sp.wait_ge(q["direct_used"], n * 3 + 1)
                load(2, NE - 1, n)
            passes(sp, body)

        @block.scalar
        def _(act):
            def high(m, n):
                for r, i in enumerate(WHOLE):
                    slot, value = landing(m, i, n)
                    act.wait_ge(landed[slot], value)
                    act.wait_ge(q["w_used"], split_count(m, r, n))
                    nc.scalar.activation(hi[:, r, :], raw[:, slot, :], ACT.Copy).then_inc(q["w_hi_ready"], 1)
                    yield r

            def x_high(ix):
                act.wait_ge(q["x_turned"], ix + 2)
                bank = ps[:, XB, :].rearrange("p (k s) -> p k s", k=KD)
                nc.scalar.activation(xd[:], bank[:, DIRECT * CK:(DIRECT + 1) * CK, :], ACT.Copy)
                nc.scalar.activation(xs[:, :, 0:SLOTS], bank, ACT.Copy).then_inc(q["x_hi"], 1)

            def half_copy(m):
                nc.scalar.activation(gu[:, m, :], ps[0:2 * SLOTS, m, :], ACT.Copy).then_inc(q["gu_copied"], 1)

            def sigmoid(it):
                act.wait_ge(q["gu_folded"], it + 1)
                nc.scalar.activation(sig[:], ps[:, GB, 0:4 * SLOTS].rearrange("p (k s) -> p k s", k=4), ACT.Sigmoid
                                     ).then_inc(q["sig_ready"], 1)

            def y_low():
                nc.scalar.activation(yl[:].rearrange("p (a c) -> p a c", a=4), ps[SLOTS:2 * SLOTS, YB:YB + 4, :], ACT.Copy
                                     ).then_inc(q["y_low"], 1)

            def step(n, before):
                for r in high(0, n):
                    if r == 1 and before is not None:
                        sigmoid(before)
                if before is not None:
                    y_low()
                for r in high(1, n):
                    pass
                half_copy(0)
                if before is not None:
                    for r in high(2, n):
                        pass
                else:
                    act.wait_ge(q["w_used"], split_count(1, SPL - 1, n, SPL))
                half_copy(1)
                x_high(n + 1)

            def body(p):
                n = p * (NE + 1)
                x_high(n)
                step(n, None)
                skip(act, q["w_hi_ready"], split_count(1, SPL - 1, n), SPL)
                with act.Fori(1, NE) as e:
                    n = p * (NE + 1) + e
                    step(n, p * NE + (e - 1))
                n = p * (NE + 1) + NE
                skip(act, q["w_hi_ready"], n * (3 * SPL), 2 * SPL)
                act.wait_ge(q["w_used"], n * (3 * SPL) + SPL)
                sigmoid(p * NE + (NE - 1))
                y_low()
                for r in high(2, n):
                    pass
                act.wait_ge(q["w_used"], split_count(2, SPL - 1, n, SPL))
                y_low()
            passes(act, body)

        @block.vector
        def _(dve):
            V = nc.vector

            def x_low(ix):
                dve.wait_ge(q["x_hi"], ix + 1)
                V.tensor_tensor(xs[:, :, SLOTS:2 * SLOTS], ps[:, XB, :].rearrange("p (k s) -> p k s", k=KD),
                                xs[:, :, 0:SLOTS].bitcast(F32), ALU.subtract).then_inc(q["x_lo"], 1)

            def y_add(iy):
                dve.wait_ge(q["y_low"], iy + 1)
                dve.wait_ge(q["y_stored"], iy * 16)
                V.tensor_tensor(ysum[:].rearrange("p (a c) -> p a c", a=4), ps[0:SLOTS, YB:YB + 4, :],
                                yl[:].rearrange("p (a c) -> p a c", a=4), ALU.add).then_inc(q["y_sum"], 1)

            def low(m, n):
                for r, i in enumerate(WHOLE):
                    dve.wait_ge(q["w_hi_ready"], split_count(m, r, n))
                    V.tensor_tensor(lo[:, r, :], raw[:, landing(m, i, n)[0], :], hi[:, r, :].bitcast(F32),
                                    ALU.subtract).then_inc(q["w_lo_ready"], 1)
                    yield r

            def hidden(n, it):
                g3 = ps[:, GB, 0:4 * SLOTS].rearrange("p (k s) -> p k s", k=4)
                u3 = ps[:, GB, 4 * SLOTS:8 * SLOTS].rearrange("p (k s) -> p k s", k=4)
                dve.wait_ge(q["sig_ready"], it + 1)
                dve.wait_ge(q["w_used"], n * (3 * SPL) + SPL)
                V.tensor_tensor(hid[:], g3, sig[:], ALU.mult).then_inc(q["h_step"], 1)
                dve.wait_ge(q["h_step"], it * 3 + 1)
                V.tensor_tensor(hid[:], u3, hid[:], ALU.mult).then_inc(q["h_step"], 1)
                dve.wait_ge(q["h_step"], it * 3 + 2)
                V.tensor_copy(hs[:, :, 0:SLOTS], hid[:]).then_inc(q["h_step"], 1)
                dve.wait_ge(q["h_step"], it * 3 + 3)
                V.tensor_tensor(hs[:, :, SLOTS:2 * SLOTS], hid[:], hs[:, :, 0:SLOTS].bitcast(F32), ALU.subtract
                                ).then_inc(q["h_ready"], 1)

            def step(n, before):
                for r in low(0, n):
                    if r == 1 and before is not None:
                        hidden(n, before)
                if before is not None:
                    y_add(n - 1)
                for r in low(1, n):
                    pass
                if before is not None:
                    for r in low(2, n):
                        pass
                x_low(n + 1)

            def body(p):
                dve.wait_ge(q["pass_done"], p + 1)
                V.tensor_scalar(rel[:], rt["rank"][:], rt["level"][:, bass.ds(p, 1)], None, ALU.subtract
                                ).then_inc(q["rel_ready"], 1)
                dve.wait_ge(q["rel_ready"], p + 1)
                for t in range(3):
                    dve.wait_ge(q["hot_used"], p * 3 + (t + 1))
                    V.tensor_tensor(hot[:], rt["slot"][:].rearrange("p (o s) -> p o s", o=1).to_broadcast([P, NE, SLOTS]),
                                    rel[:, t, :].rearrange("p (e o) -> p e o", o=1).to_broadcast([P, NE, SLOTS]),
                                    ALU.is_equal).then_inc(q["hot_ready"], 1)
                dve.wait_ge(q["hot_used"], p * 3 + 4)
                t2 = ps[0:SLOTS, GB, 0:2 * NE].rearrange("p (e i) -> p e i", i=2)
                V.tensor_scalar(tabs[:], t2, 0.0, NONE, ALU.is_equal, ALU.mult).then_inc(q["tabs_step"], 1)
                dve.wait_ge(q["tabs_step"], p + 1)
                V.scalar_tensor_tensor(gat[:, 0:NE], t2[:, :, 0], -1.0, tabs[:, :, 0], ALU.add, ALU.add
                                       ).then_inc(q["tabs_ready"], 1)
                V.scalar_tensor_tensor(sca[:, 1:NE + 1], t2[:, :, 1], -1.0, tabs[:, :, 1], ALU.add, ALU.add
                                       ).then_inc(q["tabs_ready"], 1)
                n = p * (NE + 1)
                x_low(n)
                step(n, None)
                skip(dve, q["w_lo_ready"], split_count(1, SPL - 1, n, LEAD), SPL)
                with dve.Fori(1, NE) as e:
                    step(p * (NE + 1) + e, p * NE + (e - 1))
                n = p * (NE + 1) + NE
                skip(dve, q["w_lo_ready"], n * (3 * SPL) + LEAD, 2 * SPL)
                hidden(n, p * NE + (NE - 1))
                y_add(n - 1)
                for r in low(2, n):
                    pass
                y_add(n)
            passes(dve, body)

        @block.tensor
        def _(pe):
            def x_turn(ix):
                pe.wait_ge(q["gathered"], ix * 16 + 16)
                pe.wait_ge(q["x_lo"], ix + 1)
                pe.sem_inc(q["pe_tick"], 1)
                for k in range(KD):
                    last = nc.tensor.transpose(ps[:, XB, k * SLOTS:(k + 1) * SLOTS], xe[:, k * P:(k + 1) * P],
                                               core.ident[0:SLOTS, 0:SLOTS])
                last.then_inc(q["x_turned"], 1)

            def project(n):
                pe.wait_ge(q["x_lo"], n + 2)
                for m in range(2):
                    for i in range(NCH):
                        slot, value = landing(m, i, n)
                        if i == DIRECT:
                            pe.wait_ge(landed[slot], value)
                            for k in range(CK):
                                last = nc.tensor.matmul(ps[0:SLOTS, m, :], xd[:, k, :], raw[:, slot, k * GW:(k + 1) * GW],
                                                        start=False, stop=False, skip_group_check=True)
                            last.then_inc(q["direct_used"], 1)
                            continue
                        r = WHOLE.index(i)
                        pe.wait_ge(q["w_lo_ready"], split_count(m, r, n, LEAD))
                        for k in range(CK):
                            for part in (hi, lo):
                                kk = i * CK + k
                                last = nc.tensor.matmul(ps[0:2 * SLOTS, m, :], xs[:, kk, :], part[:, r, k * GW:(k + 1) * GW],
                                                        start=(kk == 0 and part is hi), stop=(kk == KD - 1 and part is lo),
                                                        skip_group_check=True)
                        last.then_inc(q["w_used"], 1)

            def gates(it):
                for i in range(2):
                    pe.wait_ge(q["gu_copied"], it * 2 + (i + 1))
                    for j in range(4):
                        last = nc.tensor.matmul(ps[:, GB, (i * 4 + j) * SLOTS:(i * 4 + j + 1) * SLOTS],
                                                gu[:, i, j * P:(j + 1) * P], fold[:], start=True, stop=True)
                last.then_inc(q["gu_folded"], 1)

            def down(n, it):
                pe.wait_ge(q["h_ready"], it + 1)
                pe.wait_ge(q["y_sum"], n)
                for i in range(NCH):
                    slot, value = landing(2, i, n)
                    if i == DIRECT:
                        pe.wait_ge(landed[slot], value)
                        for a in range(4):
                            last = nc.tensor.matmul(ps[0:SLOTS, YB + a, :], hid[:, i, :], raw[:, slot, a * GW:(a + 1) * GW],
                                                    start=False, stop=False, skip_group_check=True)
                        last.then_inc(q["direct_used"], 1)
                    else:
                        r = WHOLE.index(i)
                        pe.wait_ge(q["w_lo_ready"], split_count(2, r, n, LEAD))
                        for part in (hi, lo):
                            for a in range(4):
                                last = nc.tensor.matmul(ps[0:2 * SLOTS, YB + a, :], hs[:, i, :], part[:, r, a * GW:(a + 1) * GW],
                                                        start=(i == 0 and part is hi), stop=(i == 3 and part is lo),
                                                        skip_group_check=True)
                        last.then_inc(q["w_used"], 1)
                    yield i

            def body(p):
                for t in range(3):
                    pe.wait_ge(q["hot_ready"], p * 3 + (t + 1))
                    for e in range(NE):
                        last = nc.tensor.matmul(ps[0:SLOTS, GB, 2 * e:2 * e + 2], hot[:, e, :], rt["ids"][:, t, e, :],
                                                start=(t == 0 and e == 0), stop=(t == 2), skip_group_check=True)
                    last.then_inc(q["hot_used"], 1)
                n = p * (NE + 1)
                x_turn(n)
                project(n)
                x_turn(n + 1)
                gates(p * NE)
                skip(pe, q["w_used"], split_count(1, SPL - 1, n, SPL), SPL)
                skip(pe, q["direct_used"], n * 3 + 3, 1)
                with pe.Fori(1, NE) as e:
                    n = p * (NE + 1) + e
                    it = p * NE + e
                    project(n)
                    x_turn(n + 1)
                    for i in down(n, it - 1):
                        if i == DIRECT:
                            gates(it)
                n = p * (NE + 1) + NE
                skip(pe, q["w_used"], n * (3 * SPL) + SPL, 2 * SPL)
                skip(pe, q["direct_used"], n * 3 + 1, 2)
                for i in down(n, p * NE + (NE - 1)):
                    pass
            passes(pe, body)

        @block.gpsimd
        def _(pool):
            def wait(sem, value):
                pool.wait_ge(sem, value)
                pool.sem_inc(q["pool_tick"], 1)

            def gather(column, ix):
                wait(q["x_turned"], ix + 1)
                nc.gpsimd.tensor_copy(gi[:], gat[:, column]).then_inc(q["gather_idx"], 1)
                wait(q["gather_idx"], ix + 1)
                pool.indirect_dma_start(out=xe[:], out_offset=None, in_=rows,
                                        in_offset=bass.IndirectOffsetOnAxis(ap=gi[:, 0:1], axis=0),
                                        bounds_check=NT - 1, oob_is_err=False).then_inc(q["gathered"], 16)

            def scatter(column, iy):
                wait(q["y_stored"], iy * 16)
                nc.gpsimd.tensor_copy(si[:], sca[:, column]).then_inc(q["scatter_idx"], 1)
                wait(q["scatter_idx"], iy + 1)
                wait(q["y_sum"], iy + 1)
                pool.indirect_dma_start(out=ydram, out_offset=bass.IndirectOffsetOnAxis(ap=si[:, 0:1], axis=0),
                                        in_=ysum[:], in_offset=None,
                                        bounds_check=2 * NT - 1, oob_is_err=False).then_inc(q["y_stored"], 16)

            def body(p):
                wait(q["tabs_ready"], p * 2 + 2)
                gather(slice(0, 1), p * (NE + 1))
                gather(slice(1, 2), p * (NE + 1) + 1)
                with pool.Fori(1, NE) as e:
                    n = p * (NE + 1) + e
                    gather(bass.ds(e + 1, 1), n + 1)
                    scatter(bass.ds(e - 1, 1), n - 1)
                scatter(slice(NE - 1, NE), p * (NE + 1) + (NE - 1))
                scatter(slice(NE, NE + 1), p * (NE + 1) + NE)
                wait(q["y_stored"], p * (16 * (NE + 1)) + 16 * (NE + 1))
                pool.sem_inc(q["pass_done"], 1)
            passes(pool, body)


def combine(core, rt, ydram, ctx):
    nc = core.nc
    yb = core.sb("yb", [P, 3, 2 * D], F32, ctx)
    landed = [core.sem(f"c_landed{t}") for t in range(3)]
    y2 = ydram.rearrange("(t i) d -> t (i d)", i=2)
    with nc.Block() as block:
        @block.sync
        def _(sp):
            for t, (t0, n) in enumerate(TILES):
                sp.dma_start(yb[0:n, t, :], y2[t0:t0 + n, :]).then_inc(landed[t], 16)

        @block.vector
        def _(dve):
            link = chain(dve, core.dve_chain)
            for t, (t0, n) in enumerate(TILES):
                dve.wait_ge(landed[t], 16)
                x = core.x_res[0:n, t, :]
                for i in range(2):
                    link(nc.vector.scalar_tensor_tensor(x, yb[0:n, t, i * D:(i + 1) * D], rt["wt"][0:n, i, t:t + 1], x,
                                                        ALU.mult, ALU.add))


def ple(core, w, xT, ctx):
    nc, ps = core.nc, core.ps
    S = lambda name, shape, dt=F32: core.sb(name, shape, dt, ctx)
    pin, pinT = S("pin", [P, 3, PLE]), S("pinT", [P, 2, NT])
    wp = S("wp", [P, 2, D])
    pp, gate = S("pp", [P, KD, NT]), S("ple_gate", [P, KD, NT])
    names = "e_loaded e_turned e_inT e_pp e_ppc e_mul".split()
    q = {n: core.sem(n) for n in names}
    with nc.Block() as block:
        @block.sync
        def _(sp):
            for t, (t0, n) in enumerate(TILES):
                src = w["p_prompt"][0, 0, t0:t0 + n, :] if t < 2 else w["p_sample"][0].rearrange("b s d -> (b s) d")
                sp.dma_start(pin[0:n, t, :], src).then_inc(q["e_loaded"], 16)
            sp.dma_start(wp[:], w["w_ple_proj"][0].rearrange("(k p) c -> p k c", p=P)).then_inc(q["e_loaded"], 16)
            load_groups(core, sp, w["w_ple_gate"][0], 0, 4)

        @block.tensor
        def _(pe):
            pe.wait_ge(q["e_loaded"], 64)
            for k in range(2):
                for t, (t0, n) in enumerate(TILES):
                    last = nc.tensor.transpose(ps[:, 4 + k, t0:t0 + n], pin[0:n, t, k * P:(k + 1) * P], core.ident[0:n, 0:n])
            last.then_inc(q["e_turned"], 1)
            pe.wait_ge(q["e_inT"], 1)
            for j in range(KD):
                if j >= 4:
                    pe.wait_ge(q["e_ppc"], j - 3)
                for k in range(2):
                    last = nc.tensor.matmul(ps[:, 4 + j % 4, 0:NT], wp[:, k, j * P:(j + 1) * P], pinT[:, k, :],
                                            start=(k == 0), stop=(k == 1))
                last.then_inc(q["e_pp"], 1)
            project_groups(core, pe, xT, 4)
            pe.wait_ge(q["e_mul"], 4)
            turn_back(core, pe, gate)

        @block.scalar
        def _(act):
            base = core.proj_groups
            with act.Fori(0, 4) as g:
                act.wait_ge(core.proj_done, g + (base + 1))
                nc.scalar.activation(gate[:, bass.ds(g * 4, 4), :], ps[:, 0:4, 0:NT], ACT.Sigmoid).then_inc(core.proj_copied, 2)

        @block.vector
        def _(dve):
            dve.wait_ge(q["e_turned"], 1)
            nc.vector.tensor_copy(pinT[:], ps[:, 4:6, 0:NT]).then_inc(q["e_inT"], 1)
            for j in range(KD):
                dve.wait_ge(q["e_pp"], j + 1)
                nc.vector.tensor_copy(pp[:, j, :], ps[:, 4 + j % 4, 0:NT]).then_inc(q["e_ppc"], 1)
            dve.wait_ge(q["e_ppc"], KD)
            base = core.proj_groups
            with dve.Fori(0, 4) as g:
                dve.wait_ge(core.proj_copied, g * 2 + (2 * base + 4))
                o = gate[:, bass.ds(g * 4, 4), :]
                nc.vector.tensor_tensor(o, o, pp[:, bass.ds(g * 4, 4), :], ALU.mult).then_inc(q["e_mul"], 1)
            add_turned(core, dve)
    core.raw_groups += 4
    core.proj_groups += 4


def final_norm(core, gain_row, out_p, out_s, ctx):
    nc = core.nc
    y = core.sb("y", [P, 3, D], F32, ctx)
    ss = core.sb("f_ss", [P, 3], F32, ctx)
    u = core.norm_runs
    ss_clear, squares, mean_ready, root_ready, rows_ready = core.norm_sems[:5]
    stored = core.sem("f_stored")
    with nc.Block() as block:
        @block.scalar
        def _(act):
            act.wait_ge(ss_clear, u + 1)
            for t, (_, n) in enumerate(TILES):
                nc.scalar.activation(y[0:n, t, :], core.x_res[0:n, t, :], ACT.Square,
                                     accum_out=ss[0:n, t:t + 1]).then_inc(squares, 1)
            act.wait_ge(mean_ready, u + 1)
            nc.scalar.activation(ss[:], ss[:], ACT.Sqrt).then_inc(root_ready, 1)

        @block.vector
        def _(dve):
            link = chain(dve, core.dve_chain)
            nc.vector.memset(ss[:], 1.0).then_inc(ss_clear, 1)
            dve.wait_ge(squares, u * 3 + 3)
            nc.vector.tensor_scalar(ss[:], ss[:], 1.0 / D, EPS, ALU.mult, ALU.add).then_inc(mean_ready, 1)
            dve.wait_ge(root_ready, u + 1)
            link(nc.vector.reciprocal(ss[:], ss[:]))
            for t, (_, n) in enumerate(TILES):
                nc.vector.scalar_tensor_tensor(y[0:n, t, :], core.x_res[0:n, t, :], ss[0:n, t:t + 1], gain_row[0:n, :],
                                               ALU.mult, ALU.mult).then_inc(rows_ready, 1)

        @block.sync
        def _(sp):
            for t, (t0, n) in enumerate(TILES):
                sp.wait_ge(rows_ready, u * 3 + t + 1)
                dst = out_p[0, t0:t0 + n, :] if t < 2 else out_s.rearrange("b s d -> (b s) d")
                sp.dma_start(dst, y[0:n, t, :]).then_inc(stored, 16)
            sp.wait_ge(stored, 48)


def load_row(core, dst, src, name):
    landed = core.sem(name)
    with core.nc.Block() as block:
        @block.sync
        def _(sp):
            sp.dma_start(dst, src.to_broadcast([P, D])).then_inc(landed, 16)
            sp.wait_ge(landed, 16)


def build(nc, w, out):
    with ExitStack() as ctx:
        core = Core(nc, ctx)
        core.x_res = core.sb("x_res", [P, 3, D])
        core.raw = core.sb("raw", [P, RAW, 2048])
        core.x_landed = core.sem("x_landed")
        core.gcols_turned = core.sem("gcols_turned")
        core.gcols_ready = core.sem("gcols_ready")
        rows = nc.dram_tensor("ffn_rows", (NT, D), F32, kind="Internal").ap()
        ydram = nc.dram_tensor("expert_rows", (2 * NT, D), F32, kind="Internal").ap()
        constants(core, w)

        with ExitStack() as mix:
            pT = core.sb("pT", [P, NPT, NT], F32, mix)
            gates = core.sb("gates", [MH, 2, NT], F32, mix)
            with ExitStack() as s:
                hT = core.sb("hT", [P, KD, NT], F32, s)
                core.wg8 = core.sb("wg8", [P, KD, 2 * MH], F32, s)
                with ExitStack() as s2:
                    xn = core.sb("xn", [P, 3, D], F32, s2)
                    norm_stage(core, xn, hT, s2, gain_cols=core.gcols[:, 0:16])
                mix_project(core, w, hT, pT, gates)
            mixT = core.sb("mixT", [P, KD, NT], F32, mix)
            with ExitStack() as s:
                attention(core, w, out, pT, mixT, s)
            with ExitStack() as s:
                mlstm(core, w, out, pT, mixT, gates, s)
            with ExitStack() as s:
                oT = core.sb("oT", [P, KD, NT], F32, s)
                out_project(core, w, mixT, oT)

        with ExitStack() as moe:
            rt = {"slot": core.sb("slot", [P, SLOTS], F32), "ids": core.sb("ids", [P, 3, NE, 2], F32),
                  "level": core.sb("level", [P, PASSES], F32), "wt": core.sb("wt_tok", [P, 2, 3], F32),
                  "rank": core.sb("rank", [P, 3, NE], F32), "need": core.sb("need", [P, PASSES], F32)}
            with ExitStack() as s:
                grow = core.sb("g_ffn_row", [P, D], F32, s)
                load_row(core, grow[:], w["g_ffn"], "g_ffn_landed")
                xn = core.sb("xn2", [P, 3, D], F32, s)
                xT = core.sb("xT2", [P, KD, NT], F32, s)
                norm_stage(core, xn, xT, s, gain_row=grow, rows_out=rows)
                router(core, w, xT, rt, s)
            with ExitStack() as s:
                experts(core, w, rt, rows, ydram, s)
            with ExitStack() as s:
                combine(core, rt, ydram, s)

        with ExitStack() as s:
            xn = core.sb("xn3", [P, 3, D], F32, s)
            xT = core.sb("xT3", [P, KD, NT], F32, s)
            norm_stage(core, xn, xT, s, gain_cols=core.gcols[:, 40:56])
            core.raw_landed = [core.sem(f"ple_landed{i}") for i in range(NCH)]
            core.landed_base = core.raw_groups
            ple(core, w, xT, s)
        with ExitStack() as s:
            grow = core.sb("g_final_row", [P, D], F32, s)
            load_row(core, grow[:], w["g_final"].rearrange("(o d) -> o d", o=1), "g_final_landed")
            final_norm(core, grow, out["y_prompt"], out["y_sample"], s)


_INS = ("x_prompt x_sample p_prompt p_sample state_mlstm_C state_mlstm_n state_mlstm_m state_swa_k state_swa_v "
        "g_mix w_in b_igate b_fgate g_mh attn_sinks w_out g_ffn w_router_g b_router_g w_router_e b_router_e "
        "w_gate w_up w_down g_ple w_ple_gate w_ple_proj g_final").split()
_STATE = {"C": (MH, DK, DK), "n": (MH, DK), "m": (MH,), "k": (WIN, KV, HD), "v": (WIN, KV, HD)}
_OUTS = {"y_prompt": (1, SEQ, D), "y_sample": (NS, 1, D),
         **{f"prompt_{n}": (1, 1, *s) for n, s in _STATE.items()},
         **{f"sample_{n}": (1, NS, *s) for n, s in _STATE.items()}}


def kernel(**inputs):
    import concourse.bacc as bacc
    from concourse.bass_utils import run_bass_kernel_spmd

    nc = bacc.Bacc("TRN2", target_bir_lowering=False, num_devices=1)
    arrays, w, out = {}, {}, {}
    for name in _INS:
        a = np.ascontiguousarray(inputs[name])
        arrays[f"in_{name}"] = a
        w[name] = nc.dram_tensor(f"in_{name}", a.shape, mybir.dt.from_np(a.dtype), kind="ExternalInput").ap()
    for name, shape in _OUTS.items():
        out[name] = nc.dram_tensor(f"out_{name}", shape, F32, kind="ExternalOutput").ap()
    build(nc, w, out)
    r = run_bass_kernel_spmd(nc, [arrays], core_ids=[0])
    return tuple(r.results[0][f"out_{name}"] for name in _OUTS)
```

```python
from contextlib import ExitStack

import numpy as np

import concourse.bass as bass
from concourse import mybir

F32 = mybir.dt.float32
F32R = mybir.dt.float32r
I32 = mybir.dt.int32
ALU = mybir.AluOpType
ACT = mybir.ActivationFunctionType
AX = mybir.AxisListType.X

P = 128
D = 2048
KD = D // P
SEQ, NS = 256, 8
NT = SEQ + NS
TILES = ((0, P), (P, P), (SEQ, NS))
MH, DK = 4, 256
AH, KV, HD = 16, 4, 64
WIN = 128
NG, NE, EPG = 4, 32, 8
DE = 512
PLE = 256
EPS = 1e-6
A_GROUPS = 3
GW = 512
CK = 4
NCH = KD // CK
SLOTS = 32
PASSES = -(-NT // SLOTS)
RAW = 6
LEAD = 6
SPL = 3
ECH = 3 * NCH
NONE = 4096.0
BIG = 1.0e30

AQ0, AK0, AV0 = 0, 8, 10
MQ0, MK0, MV0, MO0 = 12, 20, 28, 36
NPT = 44
C_MQ, C_GATES, C_AQ = 0, 4096, 4104


class Counted:

    def __init__(self, sem):
        self.sem, self.n = sem, 0

    def inc(self, ins, by=1):
        ins.then_inc(self.sem, by)
        self.n += by
        return self.n


def chain(engine, counted):

    def link(ins):
        engine.wait_ge(counted.sem, counted.inc(ins))

    return link


class Core:

    def __init__(self, nc, ctx):
        self.nc, self.ctx = nc, ctx
        self.ps = ctx.enter_context(nc.psum_tensor("ps", [P, 8, 512], F32))
        self.act_chain = Counted(self.sem("act_chain"))
        self.dve_chain = Counted(self.sem("dve_chain"))
        self.pool_chain = Counted(self.sem("pool_chain"))
        self.raw_landed = [self.sem(f"raw_landed{i}") for i in range(RAW)]
        self.raw_free = self.sem("raw_free")
        self.raw_groups = 0
        self.landed_base = 0
        self.proj_done = self.sem("proj_done")
        self.proj_copied = self.sem("proj_copied")
        self.proj_groups = 0
        self.norm_runs = 0
        self.scaled_runs = 0
        self.scale_ready = self.sem("scale_ready")
        self.turned, self.added = self.sem("turned"), self.sem("added")
        self.turned_banks = 0
        self.norm_sems = [self.sem(f"norm_{n}") for n in
                          "ss_clear squares mean root rows turned stored copied0 copied1".split()]

    def sem(self, name):
        return self.ctx.enter_context(self.nc.semaphore(name))

    def sb(self, name, shape, dt=F32, ctx=None):
        return (ctx or self.ctx).enter_context(self.nc.sbuf_tensor(name, shape, dt))


def weight_group(w, col):
    return w.rearrange("(k p) c -> p k c", p=P)[:, :, col]


def load_ahead(core, sp, w, first_col, chunks=range(NCH)):
    for c in chunks:
        src = weight_group(w, slice(first_col, first_col + GW))[:, c * CK:(c + 1) * CK, :]
        dst = core.raw[:, c, :].rearrange("p (k c) -> p k c", k=CK)
        sp.dma_start(dst, src).then_inc(core.raw_landed[c], 16)


def load_groups(core, sp, w, first_col, count, ahead=0):
    base = core.raw_groups + ahead
    first_col, count = first_col + ahead * GW, count - ahead
    with sp.Fori(0, count) as g:
        for c in range(NCH):
            sp.wait_ge(core.raw_free, g * NCH + (base * NCH + c + 1))
            src = weight_group(w, bass.ds(g * GW + first_col, GW))[:, c * CK:(c + 1) * CK, :]
            dst = core.raw[:, c, :].rearrange("p (k c) -> p k c", k=CK)
            sp.dma_start(dst, src).then_inc(core.raw_landed[c], 16)


def project_groups(core, pe, xT, count):
    nc, ps = core.nc, core.ps
    base, done = core.raw_groups, core.proj_groups
    with pe.Fori(0, count) as g:
        pe.wait_ge(core.proj_copied, g * 2 + (done * 2 + 2))
        for c in range(NCH):
            pe.wait_ge(core.raw_landed[c], g * 16 + ((base - core.landed_base) * 16 + 16))
            for k in range(CK):
                for j in range(4):
                    last = nc.tensor.matmul(ps[:, j, 0:NT], core.raw[:, c, k * GW + j * P:k * GW + (j + 1) * P],
                                            xT[:, c * CK + k, :], start=(c == 0 and k == 0),
                                            stop=(c == NCH - 1 and k == CK - 1))
            last.then_inc(core.raw_free, 1)
        pe.wait_ge(core.raw_free, g * NCH + (base * NCH + 2 * NCH))
        pe.sem_inc(core.proj_done, 1)


def project_chunk(core, pe, xT, groups, done, u, c):
    nc, ps = core.nc, core.ps
    if c == 0:
        pe.wait_ge(core.proj_copied, 2 * (done + u) + 2)
    pe.wait_ge(core.raw_landed[c], 16 * (groups - core.landed_base + u + 1))
    for k in range(CK):
        for j in range(4):
            last = nc.tensor.matmul(ps[:, j, 0:NT], core.raw[:, c, k * GW + j * P:k * GW + (j + 1) * P],
                                    xT[:, c * CK + k, :], start=(c == 0 and k == 0), stop=(c == NCH - 1 and k == CK - 1))
    last.then_inc(core.raw_free, 1)
    if c == NCH - 1:
        pe.wait_ge(core.raw_free, NCH * (groups + u + 2))
        pe.sem_inc(core.proj_done, 1)


def constants(core, w):
    nc = core.nc
    core.ident = core.sb("ident", [P, P])
    core.ones = core.sb("ones", [P, P])
    core.upper = core.sb("upper", [P, P])
    core.gcols = core.sb("gcols", [P, 56])
    core.eps = core.sb("eps", [P, 1])
    core.grows = core.sb("grows", [56, P])
    core.consts_ready = core.sem("consts_ready")
    core.grows_landed = core.sem("grows_landed")

    with nc.Block() as block:
        @block.gpsimd
        def _(pool):
            link = chain(pool, core.pool_chain)
            link(nc.gpsimd.memset(core.wg8[:], 0.0))
            link(nc.gpsimd.memset(core.ident[:], 0.0))
            link(nc.gpsimd.memset(core.ones[:], 1.0))
            link(nc.gpsimd.memset(core.eps[:], EPS))
            link(nc.gpsimd.affine_select(out=core.ident[:], in_=core.ident[:], compare_op=ALU.not_equal,
                                         fill=1.0, base=0, pattern=[[-1, P]], channel_multiplier=1))
            link(nc.gpsimd.affine_select(out=core.upper[:], in_=core.ones[:], compare_op=ALU.is_gt,
                                         fill=0.0, base=0, pattern=[[1, P]], channel_multiplier=-1))
            pool.sem_inc(core.consts_ready, 1)

        @block.sync
        def _(sp):
            for t, (t0, n) in enumerate(TILES):
                src = w["x_prompt"][0, t0:t0 + n, :] if t < 2 else w["x_sample"].rearrange("b s d -> (b s) d")
                sp.dma_start(core.x_res[0:n, t, :], src).then_inc(core.x_landed, 16)
            at = 0
            for name, n in (("g_mix", 16), ("g_mh", 8), ("g_ffn", 16), ("g_ple", 16)):
                sp.dma_start(core.grows[at:at + n, :], w[name].rearrange("l (k p) -> (l k) p", p=P)
                             ).then_inc(core.grows_landed, 16)
                at += n
            sp.sem_inc(core.raw_free, NCH)
            sp.wait_ge(core.consts_ready, 1)
            for b in range(2):
                c = C_GATES + b * MH
                sp.dma_start(core.wg8[:, :, 32 * b:32 * b + MH],
                             w["w_in"][0].rearrange("(k p) c -> p k c", p=P)[:, :, c:c + MH]).then_inc(core.gates_landed, 16)
            load_ahead(core, sp, w["w_in"][0], C_AQ)
            sp.wait_ge(core.x_landed, 48)

        @block.vector
        def _(dve):
            dve.wait_ge(core.gcols_turned, 1)
            nc.vector.tensor_copy(core.gcols[:], core.ps[:, 0, 0:56]).then_inc(core.gcols_ready, 1)
            dve.sem_inc(core.proj_copied, 2)

        @block.tensor
        def _(pe):
            pe.wait_ge(core.consts_ready, 1)
            pe.wait_ge(core.grows_landed, 64)
            nc.tensor.transpose(core.ps[:, 0, 0:56], core.grows[:], core.ident[0:56, 0:56]
                                ).then_inc(core.gcols_turned, 1)


def norm_stage(core, xn, xT, ctx, gain_cols=None, gain_row=None, rows_out=None):
    nc, ps = core.nc, core.ps
    ss = core.sb(f"norm{core.norm_runs}_ss", [P, 3], F32, ctx)
    u = core.norm_runs
    core.norm_runs += 1
    ss_clear, squares, mean_ready, root_ready, rows_ready, turned, stored = core.norm_sems[:7]
    copied = core.norm_sems[7:9]
    scale_ready = core.scale_ready

    def take(engine, k):
        engine.wait_ge(turned, u * KD + k + 1)
        src, dst = ps[:, k % 8, 0:NT], xT[:, k, :]
        if k % 2 == 0:
            scale = gain_cols[:, k:k + 1] if gain_cols is not None else 1.0
            nc.scalar.activation(dst, src, ACT.Copy, scale=scale).then_inc(copied[0], 1)
        elif gain_cols is not None:
            nc.vector.tensor_scalar(dst, src, gain_cols[:, k:k + 1], None, ALU.mult).then_inc(copied[1], 1)
        else:
            nc.vector.tensor_copy(dst, src).then_inc(copied[1], 1)

    with nc.Block() as block:
        @block.scalar
        def _(act):
            sum_squares(core, act, xn, ss, u)
            if gain_row is None:
                t, n = 2, TILES[2][1]
                act.wait_ge(scale_ready, core.scaled_runs + 1)
                nc.scalar.activation(xn[0:n, t, :], core.x_res[0:n, t, :], ACT.Copy, scale=ss[0:n, t:t + 1]
                                     ).then_inc(rows_ready, 1)
            for k in range(0, KD, 2):
                take(act, k)

        @block.vector
        def _(dve):
            link = chain(dve, core.dve_chain)
            inverse_root(core, dve, link, xn, ss, u)
            if gain_row is None:
                dve.sem_inc(scale_ready, 1)
            if gain_row is not None:
                dve.wait_ge(core.gain_landed, 16)
            for t, (_, n) in enumerate(TILES):
                if gain_row is None and t == 2:
                    continue
                if gain_row is None:
                    nc.vector.tensor_scalar(xn[0:n, t, :], core.x_res[0:n, t, :], ss[0:n, t:t + 1], None,
                                            ALU.mult).then_inc(rows_ready, 1)
                else:
                    nc.vector.scalar_tensor_tensor(xn[0:n, t, :], core.x_res[0:n, t, :], ss[0:n, t:t + 1],
                                                   gain_row[0:n, :], ALU.mult, ALU.mult).then_inc(rows_ready, 1)
            for k in range(1, KD, 2):
                take(dve, k)

        @block.tensor
        def _(pe):
            pe.wait_ge(rows_ready, u * 3 + 3)
            for k in range(KD):
                if k >= 8:
                    pe.wait_ge(copied[k % 2], u * (KD // 2) + (k - 8) // 2 + 1)
                for t, (t0, n) in enumerate(TILES):
                    last = nc.tensor.transpose(ps[:, k % 8, t0:t0 + n], xn[0:n, t, k * P:(k + 1) * P],
                                               core.ident[0:n, 0:n])
                last.then_inc(turned, 1)

        if rows_out is not None:
            @block.sync
            def _(sp):
                sp.wait_ge(rows_ready, u * 3 + 3)
                for t, (t0, n) in enumerate(TILES):
                    sp.dma_start(rows_out[t0:t0 + n, :], xn[0:n, t, :]).then_inc(stored, 16)
                sp.wait_ge(stored, 48)
    if gain_row is None:
        core.scaled_runs += 1


def sum_squares(core, act, scratch, ss, u):
    ss_clear, squares, mean_ready, root_ready = core.norm_sems[:4]
    act.wait_ge(ss_clear, u + 1)
    for t in (0, 2):
        n = TILES[t][1]
        core.nc.scalar.activation(scratch[0:n, t, :], core.x_res[0:n, t, :], ACT.Square,
                                  accum_out=ss[0:n, t:t + 1]).then_inc(squares, 1)
    act.wait_ge(mean_ready, u + 1)
    core.nc.scalar.activation(ss[:], ss[:], ACT.Sqrt).then_inc(root_ready, 1)


def inverse_root(core, dve, link, scratch, ss, u):
    nc = core.nc
    ss_clear, squares, mean_ready, root_ready = core.norm_sems[:4]
    link(nc.vector.memset(ss[:], 1.0))
    dve.sem_inc(ss_clear, 1)
    x = core.x_res[:, 1, :]
    link(nc.vector.tensor_tensor_reduce(scratch[:, 1, :], x, x, 1.0, 0.0, ALU.mult, ALU.add, ss[:, 1:2]))
    dve.wait_ge(squares, u * 2 + 2)
    nc.vector.tensor_scalar(ss[:], ss[:], 1.0 / D, EPS, ALU.mult, ALU.add).then_inc(mean_ready, 1)
    dve.wait_ge(root_ready, u + 1)
    link(nc.vector.reciprocal(ss[:], ss[:]))


def mix_project(core, w, hT, pT, gates):
    nc, ps = core.nc, core.ps
    wi = w["w_in"][0]
    wg8 = core.wg8
    gates_landed = core.gates_landed
    gates_done = core.sem("gates_done")
    gates_copied = core.sem("gates_copied")
    done = core.proj_groups

    with nc.Block() as block:
        @block.sync
        def _(sp):
            load_groups(core, sp, wi, C_AQ, A_GROUPS, ahead=1)

        @block.tensor
        def _(pe):
            pe.wait_ge(gates_landed, 32)
            for k in range(KD):
                last = nc.tensor.matmul(ps[0:32 + MH, 4, 0:NT], wg8[:, k, :], hT[:, k, :],
                                        start=(k == 0), stop=(k == KD - 1))
            last.then_inc(gates_done, 1)
            project_groups(core, pe, hT, A_GROUPS)

        @block.scalar
        def _(act):
            with act.Fori(0, A_GROUPS) as g:
                act.wait_ge(core.proj_done, g + (done + 1))
                nc.scalar.activation(pT[:, bass.ds(g * 4 + AQ0, 2), :], ps[:, 0:2, 0:NT], ACT.Copy
                                     ).then_inc(core.proj_copied, 1)

        @block.vector
        def _(dve):
            dve.wait_ge(gates_done, 1)
            for b in range(2):
                nc.vector.tensor_copy(gates[:, b, :], ps[32 * b:32 * b + MH, 4, 0:NT]).then_inc(gates_copied, 1)
            with dve.Fori(0, A_GROUPS) as g:
                dve.wait_ge(core.proj_done, g + (done + 1))
                nc.vector.tensor_copy(pT[:, bass.ds(g * 4 + (AQ0 + 2), 2), :], ps[:, 2:4, 0:NT]
                                      ).then_inc(core.proj_copied, 1)
    core.raw_groups += A_GROUPS
    core.proj_groups += A_GROUPS


def attention(core, w, out, hT, pT, mixT, ctx):
    nc, ps = core.nc, core.ps
    S = lambda name, shape, dt=F32: core.sb(name, shape, dt, ctx)
    kswp = S("kswp", [P, 2, NT])
    avtok = S("avtok", [P, 2, 256])
    aktok = S("aktok", [P, 256])
    new_kv = S("new_kv", [NS, 2, 256])
    mask = S("mask", [P, 256])
    sinks = S("sinks", [P, AH])
    sink16 = S("sink16", [AH, 1])
    spread = S("spread", [AH, P])
    sm = S("sm", [P, 2, 4, 256])
    small = S("small", [P, 2, 6, 4])
    prT = S("prT", [P, 8, P])
    kv = S("kv", [P, 2, NS, 256])
    kT = core.raw[:, NCH:RAW, :].rearrange("p a (n c) -> p a n c", c=P)
    groups, done = core.raw_groups, core.proj_groups
    UNITS, GROUPS = 2 * KV, 8
    sT = S("sT", [P, P])
    sq = S("sq", [P, P])
    st = S("st", [P, 8])

    names = ("a_const a_swap a_rows a_rowsT a_sinks a_win a_new a_stored a_scores a_shift a_exp "
             "a_prob a_turn a_turned a_pv a_mixed s_keysT s_kcopy s_scores s_sT s_turn s_prob s_back "
             "s_pT s_pv a_bias a_bias2 s_straight").split()
    q = {n: core.sem(n) for n in names}

    def span(b):
        return 128 * (b + 1)

    with nc.Block() as block:
        @block.gpsimd
        def _(pool):
            link = chain(pool, core.pool_chain)
            link(nc.gpsimd.memset(mask[:], 0.0))
            link(nc.gpsimd.affine_select(out=mask[:], in_=mask[:], compare_op=ALU.is_ge, fill=-BIG,
                                         base=P, pattern=[[-1, 256]], channel_multiplier=1))
            link(nc.gpsimd.affine_select(out=mask[:], in_=mask[:], compare_op=ALU.is_gt, fill=-BIG,
                                         base=0, pattern=[[1, 256]], channel_multiplier=-1))
            link(nc.gpsimd.memset(spread[:], 0.0))
            link(nc.gpsimd.affine_select(out=spread[:].rearrange("p (b h) -> p b h", b=NS),
                                         in_=spread[:].rearrange("p (b h) -> p b h", b=NS),
                                         compare_op=ALU.not_equal, fill=1.0, base=0,
                                         pattern=[[0, NS], [1, AH]], channel_multiplier=-1))
            pool.sem_inc(q["a_const"], 1)

        @block.sync
        def _(sp):
            sp.dma_start(sinks[:], w["attn_sinks"].to_broadcast([P, AH])).then_inc(q["a_sinks"], 16)
            sp.dma_start(sink16[:], w["attn_sinks"].rearrange("l h -> h l")).then_inc(q["a_sinks"], 16)
            load_groups(core, sp, w["w_in"][0], C_MQ, 1)
            for i, name in enumerate(("state_swa_k", "state_swa_v")):
                rows = w[name][0].rearrange("b s h d -> s b (h d)")
                for a, b in ((0, 112), (112, 127)):
                    sp.dma_start(kv[a:b, i, :, :], rows[a + 1:b + 1]).then_inc(q["a_win"], 16)
            sp.wait_ge(q["a_rows"], 2)
            for i in range(2):
                sp.dma_start(kv[127:128, i, :, :], new_kv[:, i, :]).then_inc(q["a_new"], 16)
            sp.dma_start(out["prompt_k"][0, 0].rearrange("s h d -> s (h d)"), aktok[:]).then_inc(q["a_stored"], 16)
            sp.dma_start(out["prompt_v"][0, 0].rearrange("s h d -> s (h d)"), avtok[:, 1, :]).then_inc(q["a_stored"], 16)
            sp.wait_ge(q["a_win"], 64)
            sp.wait_ge(q["a_new"], 32)
            for i, name in enumerate(("sample_k", "sample_v")):
                sp.dma_start(out[name][0].rearrange("b s h d -> s b (h d)"), kv[:, i, :, :]).then_inc(q["a_stored"], 16)
            core.raw_groups += 1
            load_groups(core, sp, w["w_in"][0], C_MQ + GW, GROUPS - 1)
            core.raw_groups = groups
            sp.wait_ge(q["a_stored"], 64)

        @block.tensor
        def _(pe):
            def project(n):
                project_chunk(core, pe, hT, groups, done, n // NCH, n % NCH)

            for i in range(2):
                for b in range(2):
                    nc.tensor.transpose(ps[:, 7, b * 256 + i * P:b * 256 + (i + 1) * P],
                                        pT[:, AV0 + i, b * P:(b + 1) * P], core.ident[:])
                nc.tensor.transpose(ps[:, 6, i * P:(i + 1) * P], pT[:, AK0 + i, P:SEQ], core.ident[:])
                nc.tensor.transpose(ps[0:NS, 6, 256 + i * P:256 + (i + 1) * P], pT[:, AK0 + i, SEQ:NT], core.ident[:])
                last = nc.tensor.transpose(ps[0:NS, 5, i * P:(i + 1) * P], pT[:, AV0 + i, SEQ:NT], core.ident[:])
            last.then_inc(q["a_rowsT"], 1)
            pe.wait_ge(q["a_swap"], 2)
            pe.wait_ge(q["a_rows"], 2)

            def scores(u):
                g, b = divmod(u, 2)
                if u >= 1:
                    pe.wait_ge(q["a_shift"], 2 * u)
                for i in range(4):
                    h = 4 * g + i
                    lo = (h % 2) * HD
                    keys = pT[lo:lo + HD, AK0 + g // 2, 0:span(b)] if h % 2 == g % 2 else kswp[lo:lo + HD, g // 2, 0:span(b)]
                    last = nc.tensor.matmul(ps[:, 4 + i % 2, (i // 2) * 256:(i // 2) * 256 + span(b)],
                                            pT[lo:lo + HD, AQ0 + h // 2, b * P:(b + 1) * P], keys,
                                            start=True, stop=True)
                last.then_inc(q["a_scores"], 1)

            def turn(u):
                b = u % 2
                pe.wait_ge(q["a_prob"], u + 1)
                if u >= 1:
                    pe.wait_ge(q["a_mixed"], u)
                for i in range(4):
                    for kb in range(b + 1):
                        n = i * 2 + kb
                        last = nc.tensor.transpose(ps[:, 6 + n // 4, (n % 4) * P:(n % 4 + 1) * P],
                                                   sm[:, u % 2, i, kb * P:(kb + 1) * P], core.ident[:])
                last.then_inc(q["a_turn"], 1)

            def values(u):
                g, b = divmod(u, 2)
                pe.wait_ge(q["a_turned"], u + 1)
                for i in range(4):
                    lo = (i % 2) * HD
                    for kb in range(b + 1):
                        last = nc.tensor.matmul(ps[lo:lo + HD, 6, (i // 2) * P:(i // 2 + 1) * P],
                                                avtok[:, kb, g * HD:(g + 1) * HD], prT[:, i * 2 + kb, :],
                                                start=(kb == 0), stop=(kb == b))
                last.then_inc(q["a_pv"], 1)

            for u in range(UNITS):
                scores(u)
                project(2 * u)
                turn(u)
                project(2 * u + 1)
                values(u)
            chunk = 2 * UNITS

            pe.wait_ge(q["a_win"], 64)
            pe.wait_ge(q["a_new"], 32)
            pe.wait_ge(q["a_mixed"], UNITS)
            for n in range(2 * NS):
                last = nc.tensor.transpose(ps[:, 4 + n // 4, (n % 4) * P:(n % 4 + 1) * P],
                                           kv[:, 0, n // 2, (n % 2) * P:(n % 2 + 1) * P], core.ident[:])
                if n % 4 == 3:
                    last.then_inc(q["s_keysT"], 1)
            project(chunk)
            pe.wait_ge(q["a_const"], 1)
            pe.wait_ge(q["a_sinks"], 32)
            pe.wait_ge(q["s_kcopy"], 8)
            nc.tensor.matmul(ps[:, 7, 256:257], spread[:], sink16[:], start=True, stop=True)
            for b in range(NS):
                for g in range(KV):
                    for par in range(2):
                        lo = par * HD
                        keys = kT[lo:lo + HD, int(par != g % 2), 2 * b + g // 2, :]
                        c = b * (AH // 2) + 2 * g
                        last = nc.tensor.matmul(ps[:, 4 + par, c:c + 2], keys,
                                                pT[lo:lo + HD, AQ0 + 2 * g:AQ0 + 2 * g + 2, SEQ + b],
                                                start=True, stop=True)
            last.then_inc(q["s_scores"], 1)
            project(chunk + 1)
            pe.wait_ge(q["s_sT"], 1)
            nc.tensor.transpose(ps[:, 7, 0:P], sT[:], core.ident[:]).then_inc(q["s_turn"], 1)
            project(chunk + 2)
            pe.wait_ge(q["s_prob"], 1)
            nc.tensor.transpose(ps[:, 7, 128:256], sq[:], core.ident[:]).then_inc(q["s_back"], 1)
            project(chunk + 3)
            pe.wait_ge(q["s_pT"], 1)
            for b in range(NS):
                for g in range(KV):
                    last = nc.tensor.matmul(ps[0:HD, 6, b * AH + 4 * g:b * AH + 4 * g + 4],
                                            kv[:, 1, b, g * HD:(g + 1) * HD], sT[:, b * AH + 4 * g:b * AH + 4 * g + 4],
                                            start=True, stop=True)
            last.then_inc(q["s_pv"], 1)
            for n in range(chunk + 4, GROUPS * NCH):
                project(n)

        @block.scalar
        def _(act):
            act.wait_ge(q["a_rowsT"], 1)
            nc.scalar.activation(avtok[:], ps[:, 7, :].rearrange("p (b c) -> p b c", b=2), ACT.Copy
                                 ).then_inc(q["a_rows"], 1)

            def turned(u):
                b = u % 2
                act.wait_ge(q["a_turn"], u + 1)
                if u >= 1:
                    act.wait_ge(q["a_pv"], u)
                src = ps[:, 6:8, :].rearrange("p a (i k c) -> p (a i) k c", k=2, c=P)[:, :, 0:b + 1, :]
                dst = prT[:].rearrange("p (i k) c -> p i k c", k=2)[:, :, 0:b + 1, :]
                nc.scalar.activation(dst, src, ACT.Copy).then_inc(q["a_turned"], 1)

            def mixed(u):
                g, b = divmod(u, 2)
                act.wait_ge(q["a_pv"], u + 1)
                nc.scalar.activation(mixT[:, 8 + 2 * g:10 + 2 * g, b * P:(b + 1) * P],
                                     ps[:, 6, 0:256].rearrange("p (i c) -> p i c", i=2), ACT.Copy
                                     ).then_inc(q["a_mixed"], 1)

            def projected(g):
                act.wait_ge(core.proj_done, done + g + 1)
                nc.scalar.activation(pT[:, MQ0 + 4 * g:MQ0 + 4 * g + 2, :], ps[:, 0:2, 0:NT], ACT.Copy
                                     ).then_inc(core.proj_copied, 1)

            for u in range(8):
                b = u % 2
                act.wait_ge(q["a_bias"], u + 1)
                for i in range(4):
                    nc.scalar.activation(sm[:, u % 2, i, 0:span(b)], sm[:, u % 2, i, 0:span(b)], ACT.Exp,
                                         bias=small[:, u % 2, 1, i:i + 1], accum_out=small[:, u % 2, 3, i:i + 1])
                nc.scalar.activation(small[:, u % 2, 2, :], small[:, u % 2, 2, :], ACT.Exp).then_inc(q["a_exp"], 1)
                turned(u)
                if u % 2:
                    projected(u // 2)
                mixed(u)
            link = chain(act, core.act_chain)
            for n in range(4):
                act.wait_ge(q["s_keysT"], n + 1)
                src = ps[:, 4 + n, :].rearrange("p (i c) -> p i c", i=4)
                nc.scalar.activation(kT[:, 0, 4 * n:4 * n + 4, :], src, ACT.Copy).then_inc(q["s_straight"], 1)
                nc.scalar.activation(kT[0:HD, 1, 4 * n:4 * n + 4, :], src[HD:P], ACT.Copy).then_inc(q["s_kcopy"], 1)
            act.wait_ge(q["s_scores"], 1)
            nc.scalar.activation(sT[:].rearrange("p (c a) -> p a c", a=2), ps[:, 4:6, 0:P // 2], ACT.Copy,
                                 scale=HD ** -0.5).then_inc(q["s_sT"], 1)
            act.wait_ge(q["a_bias2"], 1)
            link(nc.scalar.activation(sq[:], ps[:, 7, 0:P], ACT.Exp, bias=st[:, 1:2], accum_out=st[:, 3:4]))
            nc.scalar.activation(st[:, 2:3], st[:, 2:3], ACT.Exp).then_inc(q["a_exp"], 1)
            act.wait_ge(q["s_back"], 1)
            nc.scalar.activation(sT[:], ps[:, 7, 128:256], ACT.Copy).then_inc(q["s_pT"], 1)
            projected(UNITS // 2)
            act.wait_ge(q["s_pv"], 1)
            for par in range(2):
                src = ps[0:HD, 6, 0:P].rearrange("p (b j q) -> p q j b", b=NS, q=2)[:, par]
                link(nc.scalar.activation(mixT[par * HD:(par + 1) * HD, 8:16, SEQ:NT], src, ACT.Copy))
            for g in range(UNITS // 2 + 1, GROUPS):
                projected(g)

        @block.vector
        def _(dve):
            link = chain(dve, core.dve_chain)
            nc.vector.tensor_copy(kswp[0:HD], pT[HD:P, AK0:AK0 + 2, :]).then_inc(q["a_swap"], 1)
            nc.vector.tensor_copy(kswp[HD:P], pT[0:HD, AK0:AK0 + 2, :]).then_inc(q["a_swap"], 1)
            dve.wait_ge(q["a_rowsT"], 1)
            link(nc.vector.tensor_copy(aktok[:], ps[:, 6, 0:256]))
            link(nc.vector.tensor_copy(new_kv[:, 0, :], ps[0:NS, 6, 256:512]))
            nc.vector.tensor_copy(new_kv[:, 1, :], ps[0:NS, 5, 0:256]).then_inc(q["a_rows"], 1)
            dve.wait_ge(q["a_const"], 1)
            dve.wait_ge(q["a_sinks"], 32)

            def projected(g):
                dve.wait_ge(core.proj_done, done + g + 1)
                nc.vector.tensor_copy(pT[:, MQ0 + 4 * g + 2:MQ0 + 4 * g + 4, :], ps[:, 2:4, 0:NT]
                                      ).then_inc(core.proj_copied, 1)

            for u in range(8):
                g, b = divmod(u, 2)
                s, m = sm[:, u % 2, :, 0:span(b)], small[:, u % 2]
                dve.wait_ge(q["a_scores"], u + 1)
                if u >= 2:
                    dve.wait_ge(q["a_turn"], u - 1)
                msk = mask[:, 256 - span(b):256].rearrange("p (o c) -> p o c", o=1).to_broadcast([P, 2, span(b)])
                for a in range(2):
                    src = ps[:, 4 + a, :].rearrange("p (i c) -> p i c", i=2)[:, :, 0:span(b)]
                    nc.vector.scalar_tensor_tensor(sm[:, u % 2, a::2, 0:span(b)], src, HD ** -0.5, msk, ALU.mult, ALU.add
                                                   ).then_inc(q["a_shift"], 1)
                dve.wait_ge(q["a_shift"], 2 * u + 2)
                link(nc.vector.tensor_reduce(m[:, 0, :], s, AX, ALU.max))
                link(nc.vector.tensor_tensor(m[:, 0, :], m[:, 0, :], sinks[:, 4 * g:4 * g + 4], ALU.max))
                link(nc.vector.tensor_tensor(m[:, 2, :], sinks[:, 4 * g:4 * g + 4], m[:, 0, :], ALU.subtract))
                nc.vector.tensor_scalar(m[:, 1, :], m[:, 0, :], -1.0, None, ALU.mult).then_inc(q["a_bias"], 1)
                dve.wait_ge(q["a_exp"], u + 1)
                link(nc.vector.tensor_tensor(m[:, 4, :], m[:, 3, :], m[:, 2, :], ALU.add))
                link(nc.vector.reciprocal(m[:, 5, :], m[:, 4, :]))
                nc.vector.tensor_tensor(s, s, m[:, 5, :].rearrange("p (i o) -> p i o", o=1).to_broadcast([P, 4, span(b)]),
                                        ALU.mult).then_inc(q["a_prob"], 1)
                if u % 2:
                    projected(u // 2)
            for n in range(4):
                dve.wait_ge(q["s_straight"], n + 1)
                nc.vector.tensor_copy(kT[HD:P, 1, 4 * n:4 * n + 4, :], kT[0:HD, 0, 4 * n:4 * n + 4, :]).then_inc(q["s_kcopy"], 1)
            dve.wait_ge(q["s_turn"], 1)
            link(nc.vector.tensor_reduce(st[:, 0:1], ps[:, 7, 0:P], AX, ALU.max))
            link(nc.vector.tensor_tensor(st[:, 0:1], st[:, 0:1], ps[:, 7, 256:257], ALU.max))
            link(nc.vector.tensor_tensor(st[:, 2:3], ps[:, 7, 256:257], st[:, 0:1], ALU.subtract))
            nc.vector.tensor_scalar(st[:, 1:2], st[:, 0:1], -1.0, None, ALU.mult).then_inc(q["a_bias2"], 1)
            dve.wait_ge(q["a_exp"], 9)
            link(nc.vector.tensor_tensor(st[:, 4:5], st[:, 3:4], st[:, 2:3], ALU.add))
            link(nc.vector.reciprocal(st[:, 5:6], st[:, 4:5]))
            nc.vector.tensor_scalar(sq[:], sq[:], st[:, 5:6], None, ALU.mult).then_inc(q["s_prob"], 1)
            for g in range(UNITS // 2, GROUPS):
                projected(g)
    core.raw_groups += GROUPS
    core.proj_groups += GROUPS


def mlstm(core, w, out, pT, mixT, gates, ctx):
    nc, ps = core.nc, core.ps
    S = lambda name, shape, dt=F32: core.sb(name, shape, dt, ctx)
    ktok = core.raw[:, NCH + 1, :].rearrange("p (b c) -> p b c", b=2)
    vaug = S("vaug", [P, 2, MH, DK + 1])
    skq = S("skq", [NS, 2, 4 * DK])
    bi, bf = S("bi", [MH, 1]), S("bf", [MH, 1])
    lf = S("lf", [MH, NT])
    t1, t2 = S("t1", [MH, NT]), S("t2", [MH, NT])
    fsum, amax = S("fsum", [MH, SEQ]), S("amax", [MH, SEQ])
    arow = S("arow", [MH, 3, SEQ])
    cols = S("cols", [P, 3, 2, MH])
    mend = S("mend", [MH, 2])
    sel = S("sel", [NS, NS, P])
    causal = S("causal", [P, 256])
    et = S("et", [P, 2, 384])
    wt = S("wt", [P, 2, 384])
    hh = core.raw[:, NCH, :].rearrange("p (b h k) -> p b h k", b=2, h=MH)
    vw = S("vw", [P, 2, DK])
    col = S("col", [P, 6, 8])
    cout = S("cout", [P, 2, 2, DK])
    nout = S("nout", [1, MH, DK])
    sg = S("sg", [NS, 10, MH])
    n0, n1 = S("n0", [NS, MH, DK]), S("n1", [NS, MH, DK])
    diag = S("diag", [NS, 3, NS, MH])
    tab = S("tab", [P, 3, NS, MH])
    vd = S("vd", [P, 8, NS])
    num = S("num", [P, 8, NS])
    nsq = S("nsq", [P, 8, NS])
    cst = core.raw[:, 0:NCH, :]
    landed_before = 16 * (core.raw_groups - core.landed_base)
    junk = wt[:, 0, 0:DK]
    prods = [x[:].rearrange("p a c -> p (a c)")[:, i * DK:(i + 1) * DK] for x in (et, wt) for i in range(3)]

    names = ("m_small m_const m_rowsT m_rows m_lf1 m_lf2 m_arow m_colsT m_cols m_en m_mb m_e1 m_e2 m_st m_wt "
             "m_num m_den m_root m_hh m_hT m_mix m_vw m_c m_cout m_cst0 m_cst1 m_nn m_sig m_sT m_sg1 "
             "m_sg2 m_diag m_tabT m_tab m_kq m_cdec m_cnew m_num2 m_sqs m_ssum m_root2 "
             "m_stored m_cstored m_nrec m_sg3 m_nq").split()
    q = {n: core.sem(n) for n in names}

    jobs = [(MK0, 0, t) for t in range(3)] + [(MK0, 4, t) for t in range(3)]
    jobs += [(MV0, 0, t) for t in range(2)] + [(MV0, 4, t) for t in range(2)]
    jobs += [(MQ0, 0, 2), (MQ0, 4, 2)]

    with nc.Block() as block:
        @block.gpsimd
        def _(pool):
            link = chain(pool, core.pool_chain)
            link(nc.gpsimd.memset(vaug[:, :, :, DK:DK + 1], 1.0))
            link(nc.gpsimd.memset(sel[:], 0.0))
            link(nc.gpsimd.affine_select(out=sel[:], in_=sel[:], compare_op=ALU.not_equal, fill=1.0,
                                         base=0, pattern=[[1, NS], [0, P]], channel_multiplier=-1))
            link(nc.gpsimd.memset(causal[:], 0.0))
            link(nc.gpsimd.affine_select(out=causal[:], in_=causal[:], compare_op=ALU.is_ge, fill=-BIG,
                                         base=0, pattern=[[1, 256]], channel_multiplier=-1))
            pool.sem_inc(q["m_const"], 1)
            wide = lambda i: sg[:, i, :].rearrange("p (h o) -> p h o", o=1).to_broadcast([NS, MH, DK])
            kk, qq = (skq[:, i, :].rearrange("p (h k) -> p h k", h=MH) for i in range(2))
            pool.wait_ge(q["m_small"], 64)
            pool.wait_ge(q["m_sg3"], 1)
            pool.wait_ge(q["m_rows"], len(jobs))
            link(nc.gpsimd.tensor_tensor(n0[:], n0[:], wide(6), ALU.mult))
            link(nc.gpsimd.tensor_tensor(n1[:], kk, wide(7), ALU.mult))
            link(nc.gpsimd.tensor_tensor(n1[:], n1[:], n0[:], ALU.add))
            pool.sem_inc(q["m_nrec"], 1)
            nc.gpsimd.tensor_tensor(n0[:], n1[:], qq, ALU.mult).then_inc(q["m_nq"], 1)

        @block.sync
        def _(sp):
            sp.dma_start(bi[:], w["b_igate"].rearrange("l h -> h l")).then_inc(q["m_small"], 16)
            sp.dma_start(bf[:], w["b_fgate"].rearrange("l h -> h l")).then_inc(q["m_small"], 16)
            sp.dma_start(sg[:, 0, :], w["state_mlstm_m"][0]).then_inc(q["m_small"], 16)
            sp.dma_start(n0[:], w["state_mlstm_n"][0]).then_inc(q["m_small"], 16)

            def state(ap, b):
                return ap[0, b].rearrange("h (v p) k -> p (h v) k", p=P)

            def slot(b):
                return cst[:, b % NCH, :].rearrange("p (t k) -> p t k", k=DK)

            def load(b):
                sp.dma_start(slot(b), state(w["state_mlstm_C"], b)).then_inc(core.raw_landed[b % NCH], 16)

            for b in range(NCH):
                load(b)
            for h in range(MH):
                sp.wait_ge(q["m_cout"], h + 1)
                sp.dma_start(out["prompt_C"][0, 0, h].rearrange("(v p) k -> p v k", p=P), cout[:, h % 2]
                             ).then_inc(q[f"m_cst{h % 2}"], 16)
            sp.wait_ge(q["m_nn"], 2)
            sp.dma_start(out["prompt_n"][0], nout[:]).then_inc(q["m_stored"], 16)
            sp.dma_start(out["prompt_m"].rearrange("l b h -> h (l b)"), mend[:, 1:2]).then_inc(q["m_stored"], 16)
            sp.wait_ge(q["m_nrec"], 1)
            sp.dma_start(out["sample_n"][0], n1[:]).then_inc(q["m_stored"], 16)
            sp.dma_start(out["sample_m"][0], sg[:, 5, :]).then_inc(q["m_stored"], 16)
            for b in range(NS):
                if b >= 1 and b - 1 + NCH < NS:
                    sp.wait_ge(q["m_cstored"], 16 * b)
                    sp.wait_ge(q["m_num2"], 8 * b)
                    load(b - 1 + NCH)
                elif b >= 1:
                    sp.wait_ge(q["m_cstored"], 16 * b)
                    sp.wait_ge(q["m_num2"], 8 * b)
                    load_ahead(core, sp, w["w_out"][0], 0, (b - 1 + NCH - NS,))
                sp.wait_ge(q["m_cnew"], 8 * (b + 1))
                sp.dma_start(state(out["sample_C"], b), slot(b)).then_inc(q["m_cstored"], 16)
            for i in range(2):
                sp.wait_ge(q[f"m_cst{i}"], 16 * (MH // 2))
            sp.wait_ge(q["m_stored"], 64)
            sp.wait_ge(q["m_cstored"], 16 * NS)
            sp.wait_ge(q["m_num2"], 8 * NS)
            load_ahead(core, sp, w["w_out"][0], 0, (NCH - 1,))

        @block.tensor
        def _(pe):
            for n, (tile, off, t) in enumerate(jobs):
                t0, rows = TILES[t]
                if n >= 4:
                    pe.wait_ge(q["m_rows"], n - 3)
                for i in range(4):
                    last = nc.tensor.transpose(ps[0:rows, n % 4, i * P:(i + 1) * P],
                                               pT[:, tile + off + i, t0:t0 + rows], core.ident[:])
                last.then_inc(q["m_rowsT"], 1)
            pe.wait_ge(q["m_arow"], 3)
            for kind in range(3):
                for b in range(2):
                    c = (kind * 2 + b) * MH
                    last = nc.tensor.transpose(ps[:, 4, c:c + MH], arow[:, kind, b * P:(b + 1) * P],
                                               core.ident[0:MH, 0:MH])
            last.then_inc(q["m_colsT"], 1)
            nc.tensor.transpose(ps[0:NS, 5, 0:MH], t1[:, SEQ:NT], core.ident[0:MH, 0:MH])
            nc.tensor.transpose(ps[0:NS, 5, MH:2 * MH], lf[:, SEQ:NT], core.ident[0:MH, 0:MH]).then_inc(q["m_sT"], 1)
            pe.wait_ge(q["m_const"], 1)
            pe.wait_ge(q["m_rows"], len(jobs))

            def scores(h):
                if h >= 2:
                    pe.wait_ge(q["m_e1"], h - 1)
                nc.tensor.matmul(ps[:, h % 2, 0:SEQ], sel[0:MH, h, :], amax[:], start=True, stop=True
                                 ).then_inc(q["m_mb"], 1)
                if h >= 2:
                    pe.wait_ge(q["m_wt"], h - 1)
                for s in range(2):
                    o = ps[:, 2 + h % 2, 0:256] if s == 0 else ps[:, 2 + h % 2, 256:384]
                    for j in range(2):
                        last = nc.tensor.matmul(o, pT[:, MK0 + 2 * h + j, s * P:(s + 1) * P],
                                                pT[:, MQ0 + 2 * h + j, s * P:SEQ], start=(j == 0), stop=(j == 1))
                last.then_inc(q["m_st"], 1)

            def values(h):
                pe.wait_ge(q["m_wt"], h + 1)
                if h >= 1:
                    pe.wait_ge(q["m_den"], 2 * h)
                for t in range(2):
                    for s in range(t + 1):
                        lhs = wt[:, h % 2, t * P:(t + 1) * P] if s == 0 else wt[:, h % 2, 256:384]
                        last = nc.tensor.matmul(ps[:, 6 + t, 0:DK + 1], lhs, vaug[:, s, h, :],
                                                start=(s == 0), stop=(s == t))
                last.then_inc(q["m_num"], 1)

            scores(0)
            for h in range(MH):
                if h + 1 < MH:
                    scores(h + 1)
                values(h)
            pe.wait_ge(q["m_cols"], 1)
            pe.wait_ge(q["m_sg1"], 1)
            for h in range(MH):
                if h >= 2:
                    pe.wait_ge(q["m_cout"], h - 1)
                for b in range(2):
                    pe.wait_ge(q["m_vw"], 2 * h + b + 1)
                    for v in range(2):
                        last = nc.tensor.matmul(ps[:, 4 + h % 2, v * DK:(v + 1) * DK], vw[:, b, v * P:(v + 1) * P],
                                                ktok[:, b, h * DK:(h + 1) * DK], start=(b == 0 and v == 0),
                                                stop=(b == 1), skip_group_check=True)
                    if b == 1:
                        last.then_inc(q["m_c"], 1)
                for b in range(2):
                    last = nc.tensor.matmul(ps[0:1, 2 + h // 2, (h % 2) * DK:(h % 2 + 1) * DK], cols[:, 2, b, h:h + 1],
                                            ktok[:, b, h * DK:(h + 1) * DK], start=(b == 0), stop=(b == 1))
                if h % 2:
                    last.then_inc(q["m_hT"], 1)
            def spread_rows(b):
                for kq in range(2):
                    for i in range(2):
                        last = nc.tensor.matmul(ps[:, 4 * (b % 2) + 2 * kq + i, :], sel[:, b, :],
                                                skq[:, kq, i * 512:(i + 1) * 512], start=True, stop=True)
                last.then_inc(q["m_kq"], 1)

            pe.wait_ge(q["m_nn"], 2)
            spread_rows(0)
            pe.wait_ge(q["m_diag"], 1)
            pe.wait_ge(q["m_cout"], MH)
            nc.tensor.matmul(ps[:, 4, 0:96], core.ones[0:NS, :], diag[:].rearrange("p a b h -> p (a b h)"),
                             start=True, stop=True).then_inc(q["m_tabT"], 1)
            pe.wait_ge(q["m_hh"], 1)
            for j in range(8):
                if j >= 2:
                    pe.wait_ge(q["m_mix"], j - 1)
                for b in range(2):
                    last = nc.tensor.transpose(ps[:, 6 + j % 2, b * P:(b + 1) * P],
                                               hh[:, b, j // 2, (j % 2) * P:(j % 2 + 1) * P], core.ident[:])
                last.then_inc(q["m_hT"], 1)
            for b in range(1, NS):
                if b == 1:
                    pe.wait_ge(q["m_mix"], 8)
                    pe.wait_ge(q["m_tab"], 1)
                if b >= 2:
                    pe.wait_ge(q["m_num2"], 8 * (b - 1))
                spread_rows(b)
            pe.wait_ge(q["m_sqs"], 1)
            v4 = nsq[:].rearrange("p (h v) b -> p v h b", v=2)
            for v in range(2):
                last = nc.tensor.matmul(ps[:, 5, 0:32], core.ones[:], v4[:, v], start=(v == 0), stop=(v == 1))
            last.then_inc(q["m_ssum"], 1)

        @block.scalar
        def _(act):
            link = chain(act, core.act_chain)
            for n, (tile, off, t) in enumerate(jobs):
                act.wait_ge(q["m_rowsT"], n + 1)
                rows = TILES[t][1]
                src = ps[0:rows, n % 4, :]
                if t == 2:
                    dst = skq[:, int(tile == MQ0), off * P:off * P + 512]
                elif tile == MK0:
                    dst = ktok[:, t, off * P:off * P + 512]
                else:
                    dst = vaug[:, t, off // 2:off // 2 + 2, 0:DK]
                    src = src.rearrange("p (h c) -> p h c", h=2)
                nc.scalar.activation(dst, src, ACT.Copy).then_inc(q["m_rows"], 1)
                if n == 5:
                    act.wait_ge(q["m_lf1"], 1)
                    link(nc.scalar.activation(t2[:], t2[:], ACT.Exp, scale=-1.0))
                    nc.scalar.activation(t2[:], t2[:], ACT.Ln, bias=1.0).then_inc(q["m_lf2"], 1)
            act.wait_ge(q["m_arow"], 2)
            nc.scalar.activation(arow[:, 2, :], arow[:, 2, :], ACT.Exp).then_inc(q["m_en"], 1)
            act.wait_ge(q["m_cols"], 1)
            nc.scalar.activation(col[:, 0, :], cols[:, 1].rearrange("p b h -> p (b h)"), ACT.Exp).then_inc(q["m_en"], 1)
            for h in range(MH):
                act.wait_ge(q["m_e1"], h + 1)
                for s in range(2):
                    o = et[:, h % 2, 0:256] if s == 0 else et[:, h % 2, 256:384]
                    ins = nc.scalar.activation(o, o, ACT.Exp, bias=cols[:, 0, s, h:h + 1])
                ins.then_inc(q["m_e2"], 1)
                if h == 0:
                    act.wait_ge(q["m_sg1"], 1)
                    nc.scalar.activation(sg[:, 6:9, :], sg[:, 6:9, :], ACT.Exp).then_inc(q["m_sg2"], 1)
            act.wait_ge(q["m_den"], 8)
            for b in range(2):
                for h in range(MH):
                    link(nc.scalar.activation(junk, hh[:, b, h, :], ACT.Square, accum_out=col[:, 3, b * MH + h:b * MH + h + 1]))
            nc.scalar.activation(col[:, 4, :], col[:, 3, :], ACT.Sqrt, scale=1.0 / DK, bias=core.eps[:]).then_inc(q["m_root"], 1)
            for j in range(2):
                act.wait_ge(q["m_hT"], j + 1)
                link(nc.scalar.activation(nout[:, 2 * j:2 * j + 2, :], ps[0:1, 2 + j, :].rearrange("p (h c) -> p h c", h=2),
                                     ACT.Copy))
                act.sem_inc(q["m_nn"], 1)
            nc.scalar.activation(pT[:, MO0:MO0 + 8, :], pT[:, MO0:MO0 + 8, :], ACT.Sigmoid).then_inc(q["m_sig"], 1)
            act.wait_ge(q["m_tab"], 1)
            for b in range(NS):
                act.wait_ge(core.raw_landed[b % NCH], landed_before + 16 * (b // NCH + 1))
                for h in range(MH):
                    c = cst[:, b % NCH, h * 512:(h + 1) * 512]
                    nc.scalar.activation(c, c, ACT.Copy, scale=tab[:, 0, b, h:h + 1]).then_inc(q["m_cdec"], 1)
            act.wait_ge(q["m_ssum"], 1)
            nc.scalar.activation(vd[:, 0:4, :], ps[:, 5, 0:32].rearrange("p (h b) -> p h b", h=MH), ACT.Sqrt,
                                 scale=1.0 / DK, bias=core.eps[:]).then_inc(q["m_root2"], 1)

        @block.vector
        def _(dve):
            link = chain(dve, core.dve_chain)
            V = nc.vector
            dve.wait_ge(q["m_small"], 64)
            link(V.tensor_scalar(t1[:], gates[:, 1, :], bf[:], -1.0, ALU.add, ALU.mult))
            V.scalar_tensor_tensor(t2[:], t1[:], -1.0, t1[:], ALU.mult, ALU.max).then_inc(q["m_lf1"], 1)
            dve.wait_ge(q["m_lf2"], 1)
            link(V.scalar_tensor_tensor(lf[:], t1[:], 0.0, t2[:], ALU.max, ALU.add))
            link(V.tensor_scalar(lf[:], lf[:], -1.0, None, ALU.mult))
            link(V.tensor_scalar(t1[:], gates[:, 0, :], bi[:], None, ALU.add))
            dve.wait_ge(q["m_const"], 1)
            link(V.tensor_tensor_scan(fsum[:], core.ones[0:MH, 0:1].to_broadcast([MH, SEQ]), lf[:, 0:SEQ], 0.0, ALU.mult, ALU.add))
            link(V.tensor_tensor(arow[:, 0, :], t1[:, 0:SEQ], fsum[:], ALU.subtract))
            link(V.tensor_tensor_scan(amax[:], arow[:, 0, :], arow[:, 0, :], 0.0, ALU.max, ALU.max))
            V.scalar_tensor_tensor(arow[:, 1, :], fsum[:], -1.0, amax[:], ALU.mult, ALU.subtract).then_inc(q["m_arow"], 1)
            link(V.tensor_copy(mend[:, 0:1], amax[:, SEQ - 1:SEQ]))
            link(V.tensor_tensor(mend[:, 1:2], mend[:, 0:1], fsum[:, SEQ - 1:SEQ], ALU.add))
            V.tensor_scalar(arow[:, 2, :], arow[:, 0, :], mend[:, 0:1], None, ALU.subtract).then_inc(q["m_arow"], 1)
            dve.wait_ge(q["m_en"], 1)
            V.tensor_scalar(arow[:, 2, :], arow[:, 2, :], DK ** -0.5, None, ALU.mult).then_inc(q["m_arow"], 1)
            dve.wait_ge(q["m_colsT"], 1)
            V.tensor_copy(cols[:].rearrange("p a b h -> p (a b h)"), ps[:, 4, 0:24]).then_inc(q["m_cols"], 1)
            dve.wait_ge(q["m_sT"], 1)
            link(V.tensor_copy(sg[:, 1:3, :], ps[0:NS, 5, 0:8].rearrange("p (a h) -> p a h", a=2)))
            link(V.tensor_tensor(sg[:, 3, :], sg[:, 1, :], sg[:, 2, :], ALU.subtract))
            link(V.tensor_tensor(sg[:, 4, :], sg[:, 0, :], sg[:, 3, :], ALU.max))
            link(V.tensor_tensor(sg[:, 5, :], sg[:, 2, :], sg[:, 4, :], ALU.add))
            link(V.tensor_tensor(sg[:, 6, :], sg[:, 0, :], sg[:, 4, :], ALU.subtract))
            link(V.tensor_tensor(sg[:, 7, :], sg[:, 3, :], sg[:, 4, :], ALU.subtract))
            V.tensor_scalar(sg[:, 8, :], sg[:, 5, :], -1.0, None, ALU.mult).then_inc(q["m_sg1"], 1)
            for h in range(MH):
                dve.wait_ge(q["m_mb"], h + 1)
                if h >= 2:
                    dve.wait_ge(q["m_wt"], h - 1)
                link(V.scalar_tensor_tensor(et[:, h % 2, 0:256], ps[:, h % 2, 0:256], -1.0, causal[:], ALU.mult, ALU.add))
                V.scalar_tensor_tensor(et[:, h % 2, 256:384], ps[:, h % 2, P:256], -1.0, causal[:, 0:P],
                                       ALU.mult, ALU.add).then_inc(q["m_e1"], 1)
                dve.wait_ge(q["m_e2"], h + 1)
                dve.wait_ge(q["m_st"], h + 1)
                if h >= 2:
                    dve.wait_ge(q["m_num"], h - 1)
                V.scalar_tensor_tensor(wt[:, h % 2], ps[:, 2 + h % 2, 0:384], DK ** -0.5, et[:, h % 2],
                                       ALU.mult, ALU.mult).then_inc(q["m_wt"], 1)
                dve.wait_ge(q["m_num"], h + 1)
                dve.wait_ge(q["m_en"], 2)
                for b in range(2):
                    i = b * MH + h
                    den, rec = col[:, 1, i:i + 1], col[:, 2, i:i + 1]
                    link(V.tensor_copy(rec, ps[:, 6 + b, DK:DK + 1]))
                    link(V.scalar_tensor_tensor(den, rec, -1.0, rec, ALU.mult, ALU.max))
                    link(V.tensor_tensor(den, den, col[:, 0, i:i + 1], ALU.max))
                    link(V.reciprocal(rec, den))
                    link(V.tensor_scalar(hh[:, b, h, :], ps[:, 6 + b, 0:DK], rec, None, ALU.mult))
                    dve.sem_inc(q["m_den"], 1)
                if h == 0:
                    dve.wait_ge(q["m_sg2"], 1)
                    V.tensor_scalar(sg[:, 7, :], sg[:, 7, :], DK ** -0.5, None, ALU.mult).then_inc(q["m_sg3"], 1)
            for h in range(MH):
                for b in range(2):
                    if h >= 1:
                        dve.wait_ge(q["m_c"], h)
                    V.tensor_scalar(vw[:, b, :], vaug[:, b, h, 0:DK], cols[:, 2, b, h:h + 1], None, ALU.mult
                                    ).then_inc(q["m_vw"], 1)
                if h >= 2:
                    dve.wait_ge(q[f"m_cst{h % 2}"], 16 * (h // 2))
                dve.wait_ge(q["m_c"], h + 1)
                V.tensor_copy(cout[:, h % 2], ps[:, 4 + h % 2, :].rearrange("p (v k) -> p v k", v=2)).then_inc(q["m_cout"], 1)
            dve.wait_ge(q["m_root"], 1)
            link(V.reciprocal(col[:, 5, :], col[:, 4, :]))
            for b in range(2):
                for h in range(MH):
                    link(V.tensor_scalar(hh[:, b, h, :], hh[:, b, h, :], col[:, 5, b * MH + h:b * MH + h + 1], None, ALU.mult))
            dve.sem_inc(q["m_hh"], 1)
            dve.wait_ge(q["m_nq"], 1)
            link(V.tensor_reduce(sg[:, 9, :], n0[:], AX, ALU.add))
            link(V.scalar_tensor_tensor(sg[:, 9, :], sg[:, 9, :], -1.0, sg[:, 9, :], ALU.mult, ALU.max))
            link(V.tensor_tensor(sg[:, 9, :], sg[:, 9, :], sg[:, 8, :], ALU.max))
            link(V.reciprocal(sg[:, 9, :], sg[:, 9, :]))
            eye = core.ident[0:NS, 0:NS].rearrange("p (b o) -> p b o", o=1).to_broadcast([NS, NS, MH])
            for i, row in enumerate((6, 7, 9)):
                link(V.tensor_tensor(diag[:, i], eye, sg[:, row, :].rearrange("p (o h) -> p o h", o=1).to_broadcast([NS, NS, MH]),
                                     ALU.mult))
            dve.sem_inc(q["m_diag"], 1)
            dve.wait_ge(q["m_tabT"], 1)
            V.tensor_copy(tab[:].rearrange("p a b h -> p (a b h)"), ps[:, 4, 0:96]).then_inc(q["m_tab"], 1)
            dve.wait_ge(q["m_tab"], 1)
            by_head = lambda i: tab[:, i].rearrange("p b h -> p h b")
            for v in range(2):
                link(V.tensor_tensor(vd[:].rearrange("p (h v) b -> p v h b", v=2)[:, v],
                                     pT[:, MV0:MV0 + 8, SEQ:NT].rearrange("p (h v) b -> p v h b", v=2)[:, v],
                                     by_head(1), ALU.mult))
            dve.wait_ge(q["m_sig"], 1)
            for j in range(8):
                dve.wait_ge(q["m_hT"], 2 + j + 1)
                V.scalar_tensor_tensor(mixT[:, j, 0:SEQ], ps[:, 6 + j % 2, 0:SEQ], core.gcols[:, 16 + j:17 + j],
                                       pT[:, MO0 + j, 0:SEQ], ALU.mult, ALU.mult).then_inc(q["m_mix"], 1)
            for b in range(NS):
                dve.wait_ge(q["m_kq"], b + 1)
                for t in range(8):
                    h = t // 2
                    c = cst[:, b % NCH, t * DK:(t + 1) * DK]
                    if t % 2 == 0:
                        dve.wait_ge(q["m_cdec"], b * MH + h + 1)
                    V.scalar_tensor_tensor(c, ps[:, 4 * (b % 2) + h // 2, (h % 2) * DK:(h % 2 + 1) * DK], vd[:, t, b:b + 1], c,
                                           ALU.mult, ALU.add).then_inc(q["m_cnew"], 1)
                for t in range(8):
                    h = t // 2
                    c = cst[:, b % NCH, t * DK:(t + 1) * DK]
                    dve.wait_ge(q["m_cnew"], b * 8 + t + 1)
                    n = b * 8 + t
                    if n >= len(prods):
                        dve.wait_ge(q["m_num2"], n + 1 - len(prods))
                    V.tensor_tensor_reduce(prods[n % len(prods)], c, ps[:, 4 * (b % 2) + 2 + h // 2, (h % 2) * DK:(h % 2 + 1) * DK], 1.0, 0.0,
                                           ALU.mult, ALU.add, num[:, t, b:b + 1]).then_inc(q["m_num2"], 1)
            dve.wait_ge(q["m_num2"], 8 * NS)
            for v in range(2):
                o = num[:].rearrange("p (h v) b -> p v h b", v=2)[:, v]
                link(V.tensor_tensor(o, o, by_head(2), ALU.mult))
            V.tensor_tensor(nsq[:], num[:], num[:], ALU.mult).then_inc(q["m_sqs"], 1)
            dve.wait_ge(q["m_root2"], 1)
            link(V.reciprocal(vd[:, 0:4, :], vd[:, 0:4, :]))
            for v in range(2):
                o = num[:].rearrange("p (h v) b -> p v h b", v=2)[:, v]
                link(V.tensor_tensor(o, o, vd[:, 0:4, :], ALU.mult))
            link(V.tensor_tensor(num[:], num[:], core.gcols[:, 16:24].rearrange("p (j o) -> p j o", o=1).to_broadcast([P, 8, NS]),
                                 ALU.mult))
            link(V.tensor_tensor(mixT[:, 0:8, SEQ:NT], num[:], pT[:, MO0:MO0 + 8, SEQ:NT], ALU.mult))


    core.landed_base -= NS // NCH


def out_project(core, w, mixT, oT):
    nc, ps = core.nc, core.ps
    wo = w["w_out"][0]
    done = core.proj_groups
    with nc.Block() as block:
        @block.sync
        def _(sp):
            sp.dma_start(core.gain_row[:], w["g_ffn"].to_broadcast([P, D])).then_inc(core.gain_landed, 16)
            load_groups(core, sp, wo, 0, 4, ahead=1)

        @block.tensor
        def _(pe):
            project_and_turn(core, pe, mixT, oT, core.proj_copied, lambda g: 2 * (done + g) + 4)

        @block.scalar
        def _(act):
            for g in range(4):
                act.wait_ge(core.proj_done, done + g + 1)
                nc.scalar.activation(oT[:, 4 * g:4 * g + 2, :], ps[:, 0:2, 0:NT], ACT.Copy).then_inc(core.proj_copied, 1)

        @block.vector
        def _(dve):
            for g in range(4):
                if g:
                    add_turned(core, dve, g - 1)
                dve.wait_ge(core.proj_done, done + g + 1)
                nc.vector.tensor_copy(oT[:, 4 * g + 2:4 * g + 4, :], ps[:, 2:4, 0:NT]).then_inc(core.proj_copied, 1)
            add_turned(core, dve, 3)
    core.turned_banks += 12
    core.raw_groups += 4
    core.proj_groups += 4


def project_and_turn(core, pe, xT, oT, ready, value):
    nc, ps = core.nc, core.ps

    def turn(g):
        pe.wait_ge(ready, value(g))
        for t, (t0, rows) in enumerate(TILES):
            n = 3 * g + t
            if n >= 4:
                pe.wait_ge(core.added, core.turned_banks + n - 3)
            for i in range(4):
                last = nc.tensor.transpose(ps[0:rows, 4 + n % 4, i * P:(i + 1) * P], oT[:, 4 * g + i, t0:t0 + rows],
                                           core.ident[:])
            last.then_inc(core.turned, 1)

    for g in range(4):
        for c in range(NCH):
            project_chunk(core, pe, xT, core.raw_groups, core.proj_groups, g, c)
            if g and c == 0:
                turn(g - 1)
    turn(3)


def add_turned(core, dve, g):
    nc, ps = core.nc, core.ps
    for t, (_, rows) in enumerate(TILES):
        n = 3 * g + t
        dve.wait_ge(core.turned, core.turned_banks + n + 1)
        x = core.x_res[0:rows, t, g * GW:(g + 1) * GW]
        nc.vector.tensor_tensor(x, x, ps[0:rows, 4 + n % 4, :], ALU.add).then_inc(core.added, 1)


def expert_chunk(core, w, m, i, e, slot):
    rows = w[("w_gate", "w_up", "w_down")[m]][0].rearrange("e (k p) c -> e p k c", p=P)
    if m < 2:
        src = rows[bass.ds(e, 1), :, i * CK:(i + 1) * CK, :].rearrange("o p k c -> (o p) k c")
        return src, core.raw[:, slot, :].rearrange("p (k c) -> p k c", k=CK)
    return rows[bass.ds(e, 1), :, i, :].rearrange("o p c -> (o p) c"), core.raw[:, slot, :]


def router(core, w, xT, rt, ctx):
    nc, ps = core.nc, core.ps
    S = lambda name, shape, dt=F32: core.sb(name, shape, dt, ctx)
    NL = NG + NE
    wr = S("wr", [P, KD, NL])
    br = S("br", [1, NL])
    lg = S("lg", [P, 3, NL])
    a, b4 = S("ra", [P, 3, NG]), S("rb", [P, 3, NG])
    el, e1, e2 = S("el", [P, 3, NE]), S("e1", [P, 3, NE]), S("e2", [P, 3, NE])
    c = S("rc", [P, 10, 3])
    down4, down32 = S("down4", [P, NG]), S("down32", [P, NE])
    valid = S("valid", [P, 3])
    both = S("both", [P, 3, NE])
    names = "r_loaded r_const r_logits r_exp1 r_exp2 r_in1 r_in2 r_rank r_ranked".split()
    q = {n: core.sem(n) for n in names}
    with nc.Block() as block:
        @block.gpsimd
        def _(pool):
            link = chain(pool, core.pool_chain)
            link(nc.gpsimd.iota(down4[:], pattern=[[-1, NG]], base=NG, channel_multiplier=0, allow_small_or_imprecise_dtypes=True))
            link(nc.gpsimd.iota(down32[:], pattern=[[-1, NE]], base=NE, channel_multiplier=0, allow_small_or_imprecise_dtypes=True))
            link(nc.gpsimd.memset(valid[:], 1.0))
            link(nc.gpsimd.affine_select(out=valid[:, 2:3], in_=valid[:, 2:3], compare_op=ALU.is_gt, fill=0.0,
                                         base=NS, pattern=[[0, 1]], channel_multiplier=-1))
            link(nc.gpsimd.memset(lg[:, 2, :], 0.0))
            link(nc.gpsimd.iota(rt["slot"][:], pattern=[[1, SLOTS]], base=0, channel_multiplier=0, allow_small_or_imprecise_dtypes=True))
            link(nc.gpsimd.iota(rt["ids"][:, :, :, 0], pattern=[[P, 3], [0, NE]], base=1, channel_multiplier=1, allow_small_or_imprecise_dtypes=True))
            link(nc.gpsimd.iota(rt["ids"][:, :, :, 1], pattern=[[2 * P, 3], [0, NE]], base=1, channel_multiplier=2, allow_small_or_imprecise_dtypes=True))
            link(nc.gpsimd.iota(rt["level"][:], pattern=[[SLOTS, PASSES]], base=0, channel_multiplier=0, allow_small_or_imprecise_dtypes=True))
            pool.sem_inc(q["r_const"], 1)

        @block.sync
        def _(sp):
            sp.dma_start(wr[:, :, 0:NG], w["w_router_g"][0].rearrange("(k p) c -> p k c", p=P)).then_inc(q["r_loaded"], 16)
            sp.dma_start(wr[:, :, NG:NL], w["w_router_e"][0].rearrange("(k p) c -> p k c", p=P)).then_inc(q["r_loaded"], 16)
            sp.dma_start(br[:, 0:NG], w["b_router_g"]).then_inc(q["r_loaded"], 16)
            sp.dma_start(br[:, NG:NL], w["b_router_e"]).then_inc(q["r_loaded"], 16)
            for t, (t0, n) in enumerate(TILES):
                src = w["p_prompt"][0, 0, t0:t0 + n, :] if t < 2 else w["p_sample"][0].rearrange("b s d -> (b s) d")
                sp.dma_start(core.pin[0:n, t, :], src).then_inc(core.ple_loaded, 16)
            sp.dma_start(core.wp[:], w["w_ple_proj"][0].rearrange("(k p) c -> p k c", p=P)).then_inc(core.ple_loaded, 16)
            for at in range(RAW):
                src, dst = expert_chunk(core, w, at // NCH, at % NCH, 0, at)
                sp.dma_start(dst, src).then_inc(core.raw_landed[at], 16)

        @block.tensor
        def _(pe):
            pe.wait_ge(q["r_loaded"], 64)
            for t, (t0, n) in enumerate(TILES):
                for k in range(KD):
                    nc.tensor.matmul(ps[0:n, t, 0:NL], xT[:, k, t0:t0 + n], wr[:, k, :], start=(k == 0), stop=False)
                nc.tensor.matmul(ps[0:n, t, 0:NL], core.ones[0:1, 0:n], br[:], start=False, stop=True).then_inc(q["r_logits"], 1)
            pe.wait_ge(q["r_rank"], 1)
            for t in range(3):
                nc.tensor.matmul(ps[:, 3, t * NE:(t + 1) * NE], core.upper[:], both[:, t, :], start=True, stop=(t == 0))
                for s in range(t):
                    nc.tensor.matmul(ps[:, 3, t * NE:(t + 1) * NE], core.ones[:], both[:, s, :], start=False, stop=(s == t - 1))
            for t in range(3):
                last = nc.tensor.matmul(ps[:, 4, 0:NE], core.ones[:], both[:, t, :], start=(t == 0), stop=(t == 2))
            last.then_inc(q["r_ranked"], 1)

        @block.scalar
        def _(act):
            act.wait_ge(q["r_in1"], 1)
            nc.scalar.activation(a[:], a[:], ACT.Exp).then_inc(q["r_exp1"], 1)
            act.wait_ge(q["r_in2"], 1)
            nc.scalar.activation(c[:, 5, :], c[:, 5, :], ACT.Exp).then_inc(q["r_exp2"], 1)

        @block.vector
        def _(dve):
            link = chain(dve, core.dve_chain)
            V = nc.vector
            wide = lambda row, n: row.rearrange("p (t o) -> p t o", o=1).to_broadcast([P, 3, n])
            over = lambda row, n: row.rearrange("p (o e) -> p o e", o=1).to_broadcast([P, 3, n])
            dve.wait_ge(q["r_const"], 1)
            dve.wait_ge(q["r_logits"], 3)
            link(V.tensor_copy(lg[:, 0:2, :], ps[:, 0:2, 0:NL]))
            link(V.tensor_copy(lg[0:NS, 2, :], ps[0:NS, 2, 0:NL]))
            gl, le = lg[:, :, 0:NG], lg[:, :, NG:NL]

            def first_max(src, n, top, onehot, tmp, down):
                link(V.tensor_reduce(top, src, AX, ALU.max))
                link(V.tensor_tensor(tmp, src, wide(top, n), ALU.is_equal))
                link(V.tensor_tensor(tmp, tmp, over(down[:], n), ALU.mult))
                link(V.tensor_reduce(c[:, 9, :], tmp, AX, ALU.max))
                link(V.tensor_tensor(onehot, tmp, wide(c[:, 9, :], n), ALU.is_equal))

            first_max(gl, NG, c[:, 0, :], b4[:], a[:], down4)
            V.tensor_tensor(a[:], gl, wide(c[:, 0, :], NG), ALU.subtract).then_inc(q["r_in1"], 1)
            dve.wait_ge(q["r_exp1"], 1)
            link(V.tensor_reduce(c[:, 1, :], a[:], AX, ALU.add))
            link(V.reciprocal(c[:, 2, :], c[:, 1, :]))
            link(V.tensor_scalar(b4[:], b4[:], 1.0, BIG, ALU.subtract, ALU.mult))
            for t in range(3):
                link(V.tensor_tensor(el[:, t, :].rearrange("p (g e) -> p g e", g=NG), le[:, t, :].rearrange("p (g e) -> p g e", g=NG),
                                     b4[:, t, :].rearrange("p (g o) -> p g o", o=1).to_broadcast([P, NG, EPG]), ALU.add))
            first_max(el[:], NE, c[:, 3, :], e1[:], both[:], down32)
            link(V.scalar_tensor_tensor(el[:], e1[:], -2.0 * BIG, el[:], ALU.mult, ALU.add))
            first_max(el[:], NE, c[:, 4, :], e2[:], both[:], down32)
            V.tensor_tensor(c[:, 5, :], c[:, 4, :], c[:, 3, :], ALU.subtract).then_inc(q["r_in2"], 1)
            dve.wait_ge(q["r_exp2"], 1)
            link(V.tensor_scalar(c[:, 6, :], c[:, 5, :], 1.0, None, ALU.add))
            link(V.reciprocal(c[:, 7, :], c[:, 6, :]))
            link(V.tensor_tensor(rt["wt"][:, 0, :], c[:, 7, :], c[:, 2, :], ALU.mult))
            link(V.tensor_tensor(rt["wt"][:, 1, :], rt["wt"][:, 0, :], c[:, 5, :], ALU.mult))
            link(V.tensor_tensor(both[:], e1[:], e2[:], ALU.add))
            link(V.tensor_tensor(both[:], both[:], wide(valid[:], NE), ALU.mult))
            dve.sem_inc(q["r_rank"], 1)
            link(V.tensor_tensor(rt["ids"][:, :, :, 1], rt["ids"][:, :, :, 1], e2[:], ALU.add))
            dve.wait_ge(q["r_ranked"], 1)
            link(V.tensor_tensor(el[:], ps[:, 3, 0:3 * NE].rearrange("p (t e) -> p t e", t=3), both[:], ALU.mult))
            link(V.tensor_scalar(both[:], both[:], 1.0, 1.0e6, ALU.subtract, ALU.mult))
            link(V.tensor_tensor(rt["rank"][:], el[:], both[:], ALU.add))
            link(V.tensor_reduce(c[:, 8, 0:1], ps[:, 4, 0:NE], AX, ALU.max))
            link(V.tensor_tensor(rt["need"][:], c[:, 8, 0:1].to_broadcast([P, PASSES]), rt["level"][:], ALU.is_gt))


def experts(core, w, rt, rows, ydram, ctx):
    nc, ps, raw = core.nc, core.ps, core.raw
    S = lambda name, shape, dt=F32: core.sb(name, shape, dt, ctx)
    hi, lo = S("w_hi", [P, SPL, 2048], F32R), S("w_lo", [P, SPL, 2048], F32R)
    xs = S("x_split", [P, KD, 2 * SLOTS], F32R)
    xd = S("x_direct", [P, CK, SLOTS])
    hs = S("h_split", [P, 4, 2 * SLOTS], F32R)
    xe = S("xe", [SLOTS, D])
    gu = S("gu", [2 * SLOTS, 2, DE])
    sig, hid = S("sig", [P, 4, SLOTS]), S("hid", [P, 4, SLOTS])
    yl, ysum = S("yl", [SLOTS, D]), S("ysum", [SLOTS, D])
    fold = S("fold", [2 * SLOTS, SLOTS])
    hot = S("hot", [P, NE, SLOTS])
    rel = S("rel", [P, 3, NE])
    tabs = S("tabs", [SLOTS, NE, 2])
    gat, sca = S("gat", [SLOTS, NE + 1], I32), S("sca", [SLOTS, NE + 1], I32)
    gi, si = S("gi", [SLOTS, 1], I32), S("si", [SLOTS, 1], I32)
    flag = S("flag", [1, PASSES], I32)
    names = ("w_hi_ready w_lo_ready w_used direct_used rel_ready hot_ready hot_used tabs_step tabs_ready "
             "gather_idx gathered x_turned x_hi x_lo gu_copied gu_folded sig_ready h_step h_ready "
             "y_low y_sum scatter_idx y_stored pass_done pool_tick pe_tick").split()
    q = {n: core.sem(n) for n in names}
    landed = core.raw_landed
    lbase = [16 * (core.raw_groups - core.landed_base)] * NCH + [0] * (RAW - NCH)
    XB, GB, YB = 3, 2, 4

    with nc.Block() as block:
        @block.gpsimd
        def _(pool):
            link = chain(pool, core.pool_chain)
            link(nc.gpsimd.memset(xe[:], 0.0))
            link(nc.gpsimd.tensor_copy(fold[0:SLOTS, :], core.ident[0:SLOTS, 0:SLOTS]))
            link(nc.gpsimd.tensor_copy(fold[SLOTS:2 * SLOTS, :], core.ident[SLOTS:2 * SLOTS, SLOTS:2 * SLOTS]))
            link(nc.gpsimd.memset(gat[:, NE:NE + 1], int(NONE)))
            link(nc.gpsimd.memset(sca[:, 0:1], int(NONE)))
            pool.sem_inc(q["pass_done"], 1)

        @block.vector
        def _(dve):
            link = chain(dve, core.dve_chain)
            link(nc.vector.tensor_copy(flag[:], rt["need"][0:1, :]))
            link(nc.vector.memset(ps[:, YB:YB + 4, :], 0.0))
            dve.sem_inc(q["x_lo"], 1)

        @block.tensor
        def _(pe):
            pe.sem_inc(q["w_used"], SPL)
            pe.sem_inc(q["x_turned"], 1)
            pe.sem_inc(q["hot_used"], 1)

        @block.sync
        def _(sp):
            sp.sem_inc(q["w_lo_ready"], LEAD)
            sp.sem_inc(q["direct_used"], 1)

    def passes(engine, body):
        with engine.Fori(0, PASSES) as p:
            need = engine.value_load(flag[0:1, bass.ds(p, 1)], min_val=0, max_val=1)
            with engine.If(need > 0):
                body(p)

    DIRECT = 1
    WHOLE = (0, 2, 3)

    def landing(m, i, n):
        at = m * NCH + i
        slot = at % RAW
        return slot, n * (16 * ECH // RAW) + (lbase[slot] + 16 * (at // RAW + 1))

    def slot_free(m, i, n):
        at = m * NCH + i - RAW
        back = at < 0
        m0, i0 = divmod(at % ECH, NCH)
        if i0 == DIRECT:
            return q["direct_used"], n * 3 + (m0 + 1 + 1 - 3 * back)
        return q["w_lo_ready"], n * (3 * SPL) + (m0 * SPL + WHOLE.index(i0) + 1 + LEAD - 3 * SPL * back)

    def split_count(m, r, n, ahead=0):
        return n * (3 * SPL) + (m * SPL + r + 1 + ahead)

    def skip(engine, sem, done, by):
        engine.wait_ge(sem, done)
        engine.sem_inc(sem, by)

    with nc.Block() as block:
        @block.sync
        def _(sp):
            def load(m, e, n, chunks=range(NCH)):
                for i in chunks:
                    sp.wait_ge(*slot_free(m, i, n))
                    slot, _ = landing(m, i, n)
                    src, dst = expert_chunk(core, w, m, i, e, slot)
                    sp.dma_start(dst, src).then_inc(landed[slot], 16)

            def body(p):
                n = p * (NE + 1)
                with sp.If(p > 0):
                    load(0, 0, n)
                    load(1, 0, n, range(RAW - NCH))
                load(1, 0, n, range(RAW - NCH, NCH))
                for i in range(NCH):
                    slot, value = landing(2, i, n)
                    skip(sp, landed[slot], p * (32 * (NE + 1)) + (lbase[slot] + 16), 16)
                with sp.Fori(1, NE) as e:
                    n = p * (NE + 1) + e
                    load(0, e, n)
                    load(1, e, n)
                    load(2, e - 1, n)
                n = p * (NE + 1) + NE
                for slot in range(RAW):
                    skip(sp, landed[slot], n * 32 + lbase[slot], 32 if slot < 2 * NCH - RAW else 16)
                sp.wait_ge(q["direct_used"], n * 3 + 1)
                load(2, NE - 1, n)
            passes(sp, body)

        @block.scalar
        def _(act):
            def high(m, n):
                for r, i in enumerate(WHOLE):
                    slot, value = landing(m, i, n)
                    act.wait_ge(landed[slot], value)
                    act.wait_ge(q["w_used"], split_count(m, r, n))
                    nc.scalar.activation(hi[:, r, :], raw[:, slot, :], ACT.Copy).then_inc(q["w_hi_ready"], 1)
                    yield r

            def x_high(ix):
                act.wait_ge(q["x_turned"], ix + 2)
                bank = ps[:, XB, :].rearrange("p (k s) -> p k s", k=KD)
                nc.scalar.activation(xd[:], bank[:, DIRECT * CK:(DIRECT + 1) * CK, :], ACT.Copy)
                nc.scalar.activation(xs[:, :, 0:SLOTS], bank, ACT.Copy).then_inc(q["x_hi"], 1)

            def half_copy(m):
                nc.scalar.activation(gu[:, m, :], ps[0:2 * SLOTS, m, :], ACT.Copy).then_inc(q["gu_copied"], 1)

            def sigmoid(it):
                act.wait_ge(q["gu_folded"], it + 1)
                nc.scalar.activation(sig[:], ps[:, GB, 0:4 * SLOTS].rearrange("p (k s) -> p k s", k=4), ACT.Sigmoid
                                     ).then_inc(q["sig_ready"], 1)

            def y_low():
                nc.scalar.activation(yl[:].rearrange("p (a c) -> p a c", a=4), ps[SLOTS:2 * SLOTS, YB:YB + 4, :], ACT.Copy
                                     ).then_inc(q["y_low"], 1)

            def step(n, before):
                for r in high(0, n):
                    if r == 1 and before is not None:
                        sigmoid(before)
                if before is not None:
                    y_low()
                for r in high(1, n):
                    pass
                half_copy(0)
                if before is not None:
                    for r in high(2, n):
                        pass
                else:
                    act.wait_ge(q["w_used"], split_count(1, SPL - 1, n, SPL))
                half_copy(1)
                x_high(n + 1)

            def body(p):
                n = p * (NE + 1)
                x_high(n)
                step(n, None)
                skip(act, q["w_hi_ready"], split_count(1, SPL - 1, n), SPL)
                with act.Fori(1, NE) as e:
                    n = p * (NE + 1) + e
                    step(n, p * NE + (e - 1))
                n = p * (NE + 1) + NE
                skip(act, q["w_hi_ready"], n * (3 * SPL), 2 * SPL)
                act.wait_ge(q["w_used"], n * (3 * SPL) + SPL)
                sigmoid(p * NE + (NE - 1))
                y_low()
                for r in high(2, n):
                    pass
                act.wait_ge(q["w_used"], split_count(2, SPL - 1, n, SPL))
                y_low()
            passes(act, body)

        @block.vector
        def _(dve):
            V = nc.vector

            def x_low(ix):
                dve.wait_ge(q["x_hi"], ix + 1)
                V.tensor_tensor(xs[:, :, SLOTS:2 * SLOTS], ps[:, XB, :].rearrange("p (k s) -> p k s", k=KD),
                                xs[:, :, 0:SLOTS].bitcast(F32), ALU.subtract).then_inc(q["x_lo"], 1)

            def y_add(iy):
                dve.wait_ge(q["y_low"], iy + 1)
                dve.wait_ge(q["y_stored"], iy * 16)
                V.tensor_tensor(ysum[:].rearrange("p (a c) -> p a c", a=4), ps[0:SLOTS, YB:YB + 4, :],
                                yl[:].rearrange("p (a c) -> p a c", a=4), ALU.add).then_inc(q["y_sum"], 1)

            def low(m, n):
                for r, i in enumerate(WHOLE):
                    dve.wait_ge(q["w_hi_ready"], split_count(m, r, n))
                    V.tensor_tensor(lo[:, r, :], raw[:, landing(m, i, n)[0], :], hi[:, r, :].bitcast(F32),
                                    ALU.subtract).then_inc(q["w_lo_ready"], 1)
                    yield r

            def hidden(n, it):
                g3 = ps[:, GB, 0:4 * SLOTS].rearrange("p (k s) -> p k s", k=4)
                u3 = ps[:, GB, 4 * SLOTS:8 * SLOTS].rearrange("p (k s) -> p k s", k=4)
                dve.wait_ge(q["sig_ready"], it + 1)
                dve.wait_ge(q["w_used"], n * (3 * SPL) + SPL)
                V.tensor_tensor(hid[:], g3, sig[:], ALU.mult).then_inc(q["h_step"], 1)
                dve.wait_ge(q["h_step"], it * 3 + 1)
                V.tensor_tensor(hid[:], u3, hid[:], ALU.mult).then_inc(q["h_step"], 1)
                dve.wait_ge(q["h_step"], it * 3 + 2)
                V.tensor_copy(hs[:, :, 0:SLOTS], hid[:]).then_inc(q["h_step"], 1)
                dve.wait_ge(q["h_step"], it * 3 + 3)
                V.tensor_tensor(hs[:, :, SLOTS:2 * SLOTS], hid[:], hs[:, :, 0:SLOTS].bitcast(F32), ALU.subtract
                                ).then_inc(q["h_ready"], 1)

            def step(n, before):
                for r in low(0, n):
                    if r == 1 and before is not None:
                        hidden(n, before)
                if before is not None:
                    y_add(n - 1)
                for r in low(1, n):
                    pass
                if before is not None:
                    for r in low(2, n):
                        pass
                x_low(n + 1)

            def body(p):
                dve.wait_ge(q["pass_done"], p + 1)
                V.tensor_scalar(rel[:], rt["rank"][:], rt["level"][:, bass.ds(p, 1)], None, ALU.subtract
                                ).then_inc(q["rel_ready"], 1)
                dve.wait_ge(q["rel_ready"], p + 1)
                for t in range(3):
                    dve.wait_ge(q["hot_used"], p * 3 + (t + 1))
                    V.tensor_tensor(hot[:], rt["slot"][:].rearrange("p (o s) -> p o s", o=1).to_broadcast([P, NE, SLOTS]),
                                    rel[:, t, :].rearrange("p (e o) -> p e o", o=1).to_broadcast([P, NE, SLOTS]),
                                    ALU.is_equal).then_inc(q["hot_ready"], 1)
                dve.wait_ge(q["hot_used"], p * 3 + 4)
                t2 = ps[0:SLOTS, GB, 0:2 * NE].rearrange("p (e i) -> p e i", i=2)
                V.tensor_scalar(tabs[:], t2, 0.0, NONE, ALU.is_equal, ALU.mult).then_inc(q["tabs_step"], 1)
                dve.wait_ge(q["tabs_step"], p + 1)
                V.scalar_tensor_tensor(gat[:, 0:NE], t2[:, :, 0], -1.0, tabs[:, :, 0], ALU.add, ALU.add
                                       ).then_inc(q["tabs_ready"], 1)
                V.scalar_tensor_tensor(sca[:, 1:NE + 1], t2[:, :, 1], -1.0, tabs[:, :, 1], ALU.add, ALU.add
                                       ).then_inc(q["tabs_ready"], 1)
                n = p * (NE + 1)
                x_low(n)
                step(n, None)
                skip(dve, q["w_lo_ready"], split_count(1, SPL - 1, n, LEAD), SPL)
                with dve.Fori(1, NE) as e:
                    step(p * (NE + 1) + e, p * NE + (e - 1))
                n = p * (NE + 1) + NE
                skip(dve, q["w_lo_ready"], n * (3 * SPL) + LEAD, 2 * SPL)
                hidden(n, p * NE + (NE - 1))
                y_add(n - 1)
                for r in low(2, n):
                    pass
                y_add(n)
            passes(dve, body)

        @block.tensor
        def _(pe):
            def x_turn(ix):
                pe.wait_ge(q["gathered"], ix * 16 + 16)
                pe.wait_ge(q["x_lo"], ix + 1)
                pe.sem_inc(q["pe_tick"], 1)
                for k in range(KD):
                    last = nc.tensor.transpose(ps[:, XB, k * SLOTS:(k + 1) * SLOTS], xe[:, k * P:(k + 1) * P],
                                               core.ident[0:SLOTS, 0:SLOTS])
                last.then_inc(q["x_turned"], 1)

            def project(n):
                pe.wait_ge(q["x_lo"], n + 2)
                for m in range(2):
                    for i in range(NCH):
                        slot, value = landing(m, i, n)
                        if i == DIRECT:
                            pe.wait_ge(landed[slot], value)
                            for k in range(CK):
                                last = nc.tensor.matmul(ps[0:SLOTS, m, :], xd[:, k, :], raw[:, slot, k * GW:(k + 1) * GW],
                                                        start=False, stop=False, skip_group_check=True)
                            last.then_inc(q["direct_used"], 1)
                            continue
                        r = WHOLE.index(i)
                        pe.wait_ge(q["w_lo_ready"], split_count(m, r, n, LEAD))
                        for k in range(CK):
                            for part in (hi, lo):
                                kk = i * CK + k
                                last = nc.tensor.matmul(ps[0:2 * SLOTS, m, :], xs[:, kk, :], part[:, r, k * GW:(k + 1) * GW],
                                                        start=(kk == 0 and part is hi), stop=(kk == KD - 1 and part is lo),
                                                        skip_group_check=True)
                        last.then_inc(q["w_used"], 1)

            def gates(it):
                for i in range(2):
                    pe.wait_ge(q["gu_copied"], it * 2 + (i + 1))
                    for j in range(4):
                        last = nc.tensor.matmul(ps[:, GB, (i * 4 + j) * SLOTS:(i * 4 + j + 1) * SLOTS],
                                                gu[:, i, j * P:(j + 1) * P], fold[:], start=True, stop=True)
                last.then_inc(q["gu_folded"], 1)

            def down(n, it):
                pe.wait_ge(q["h_ready"], it + 1)
                pe.wait_ge(q["y_sum"], n)
                for i in range(NCH):
                    slot, value = landing(2, i, n)
                    if i == DIRECT:
                        pe.wait_ge(landed[slot], value)
                        for a in range(4):
                            last = nc.tensor.matmul(ps[0:SLOTS, YB + a, :], hid[:, i, :], raw[:, slot, a * GW:(a + 1) * GW],
                                                    start=False, stop=False, skip_group_check=True)
                        last.then_inc(q["direct_used"], 1)
                    else:
                        r = WHOLE.index(i)
                        pe.wait_ge(q["w_lo_ready"], split_count(2, r, n, LEAD))
                        for part in (hi, lo):
                            for a in range(4):
                                last = nc.tensor.matmul(ps[0:2 * SLOTS, YB + a, :], hs[:, i, :], part[:, r, a * GW:(a + 1) * GW],
                                                        start=(i == 0 and part is hi), stop=(i == 3 and part is lo),
                                                        skip_group_check=True)
                        last.then_inc(q["w_used"], 1)
                    yield i

            def body(p):
                for t in range(3):
                    pe.wait_ge(q["hot_ready"], p * 3 + (t + 1))
                    for e in range(NE):
                        last = nc.tensor.matmul(ps[0:SLOTS, GB, 2 * e:2 * e + 2], hot[:, e, :], rt["ids"][:, t, e, :],
                                                start=(t == 0 and e == 0), stop=(t == 2), skip_group_check=True)
                    last.then_inc(q["hot_used"], 1)
                n = p * (NE + 1)
                x_turn(n)
                project(n)
                x_turn(n + 1)
                gates(p * NE)
                skip(pe, q["w_used"], split_count(1, SPL - 1, n, SPL), SPL)
                skip(pe, q["direct_used"], n * 3 + 3, 1)
                with pe.Fori(1, NE) as e:
                    n = p * (NE + 1) + e
                    it = p * NE + e
                    project(n)
                    x_turn(n + 1)
                    for i in down(n, it - 1):
                        if i == DIRECT:
                            gates(it)
                n = p * (NE + 1) + NE
                skip(pe, q["w_used"], n * (3 * SPL) + SPL, 2 * SPL)
                skip(pe, q["direct_used"], n * 3 + 1, 2)
                for i in down(n, p * NE + (NE - 1)):
                    pass
            passes(pe, body)

        @block.gpsimd
        def _(pool):
            def wait(sem, value):
                pool.wait_ge(sem, value)
                pool.sem_inc(q["pool_tick"], 1)

            def gather(column, ix):
                wait(q["x_turned"], ix + 1)
                nc.gpsimd.tensor_copy(gi[:], gat[:, column]).then_inc(q["gather_idx"], 1)
                wait(q["gather_idx"], ix + 1)
                pool.indirect_dma_start(out=xe[:], out_offset=None, in_=rows,
                                        in_offset=bass.IndirectOffsetOnAxis(ap=gi[:, 0:1], axis=0),
                                        bounds_check=NT - 1, oob_is_err=False).then_inc(q["gathered"], 16)

            def scatter(column, iy):
                wait(q["y_stored"], iy * 16)
                nc.gpsimd.tensor_copy(si[:], sca[:, column]).then_inc(q["scatter_idx"], 1)
                wait(q["scatter_idx"], iy + 1)
                wait(q["y_sum"], iy + 1)
                pool.indirect_dma_start(out=ydram, out_offset=bass.IndirectOffsetOnAxis(ap=si[:, 0:1], axis=0),
                                        in_=ysum[:], in_offset=None,
                                        bounds_check=2 * NT - 1, oob_is_err=False).then_inc(q["y_stored"], 16)

            def body(p):
                wait(q["tabs_ready"], p * 2 + 2)
                gather(slice(0, 1), p * (NE + 1))
                gather(slice(1, 2), p * (NE + 1) + 1)
                with pool.Fori(1, NE) as e:
                    n = p * (NE + 1) + e
                    gather(bass.ds(e + 1, 1), n + 1)
                    scatter(bass.ds(e - 1, 1), n - 1)
                scatter(slice(NE - 1, NE), p * (NE + 1) + (NE - 1))
                scatter(slice(NE, NE + 1), p * (NE + 1) + NE)
                wait(q["y_stored"], p * (16 * (NE + 1)) + 16 * (NE + 1))
                pool.sem_inc(q["pass_done"], 1)
            passes(pool, body)


def combine(core, w, rt, ydram, pp, ctx):
    nc, ps = core.nc, core.ps
    S = lambda name, shape, dt=F32: core.sb(name, shape, dt, ctx)
    pin, wp, loaded = core.pin, core.wp, core.ple_loaded
    pinT = S("pinT", [P, 2, NT])
    q = {n: core.sem(n) for n in "e_turned e_inT e_pp e_ppc".split()}
    yb = core.sb("yb", [P, 3, 2 * D], F32, ctx)
    landed = [core.sem(f"c_landed{t}") for t in range(3)]
    y2 = ydram.rearrange("(t i) d -> t (i d)", i=2)
    with nc.Block() as block:
        @block.sync
        def _(sp):
            for t, (t0, n) in enumerate(TILES):
                sp.dma_start(yb[0:n, t, :], y2[t0:t0 + n, :]).then_inc(landed[t], 16)
            load_ahead(core, sp, w["w_ple_gate"][0], 0)

        @block.tensor
        def _(pe):
            pe.wait_ge(loaded, 64)
            for k in range(2):
                for t, (t0, n) in enumerate(TILES):
                    last = nc.tensor.transpose(ps[:, 4 + k, t0:t0 + n], pin[0:n, t, k * P:(k + 1) * P], core.ident[0:n, 0:n])
            last.then_inc(q["e_turned"], 1)
            pe.wait_ge(q["e_inT"], 1)
            for j in range(KD):
                if j >= 4:
                    pe.wait_ge(q["e_ppc"], j - 3)
                for k in range(2):
                    last = nc.tensor.matmul(ps[:, 4 + j % 4, 0:NT], wp[:, k, j * P:(j + 1) * P], pinT[:, k, :],
                                            start=(k == 0), stop=(k == 1))
                last.then_inc(q["e_pp"], 1)

        @block.scalar
        def _(act):
            act.wait_ge(q["e_turned"], 1)
            nc.scalar.activation(pinT[:], ps[:, 4:6, 0:NT], ACT.Copy).then_inc(q["e_inT"], 1)
            for j in range(KD):
                act.wait_ge(q["e_pp"], j + 1)
                nc.scalar.activation(pp[:, j, :], ps[:, 4 + j % 4, 0:NT], ACT.Copy).then_inc(q["e_ppc"], 1)

        @block.vector
        def _(dve):
            link = chain(dve, core.dve_chain)
            for t, (t0, n) in enumerate(TILES):
                dve.wait_ge(landed[t], 16)
                x = core.x_res[0:n, t, :]
                for i in range(2):
                    link(nc.vector.scalar_tensor_tensor(x, yb[0:n, t, i * D:(i + 1) * D], rt["wt"][0:n, i, t:t + 1], x,
                                                        ALU.mult, ALU.add))


def ple(core, w, xT, pp, ctx):
    nc, ps = core.nc, core.ps
    gate = core.sb("ple_gate", [P, KD, NT], F32, ctx)
    gated = core.sem("e_mul")
    done = core.proj_groups
    with nc.Block() as block:
        @block.sync
        def _(sp):
            load_groups(core, sp, w["w_ple_gate"][0], 0, 4, ahead=1)
            sp.dma_start(core.gain_row[:], w["g_final"].rearrange("(o d) -> o d", o=1).to_broadcast([P, D])
                         ).then_inc(core.gain_landed, 16)

        @block.tensor
        def _(pe):
            project_and_turn(core, pe, xT, gate, gated, lambda g: g + 1)

        @block.scalar
        def _(act):
            for g in range(4):
                act.wait_ge(core.proj_done, done + g + 1)
                nc.scalar.activation(gate[:, 4 * g:4 * g + 4, :], ps[:, 0:4, 0:NT], ACT.Sigmoid
                                     ).then_inc(core.proj_copied, 2)

        @block.vector
        def _(dve):
            for g in range(4):
                if g:
                    add_turned(core, dve, g - 1)
                dve.wait_ge(core.proj_copied, 2 * (done + g) + 4)
                o = gate[:, 4 * g:4 * g + 4, :]
                nc.vector.tensor_tensor(o, o, pp[:, 4 * g:4 * g + 4, :], ALU.mult).then_inc(gated, 1)
            add_turned(core, dve, 3)
    core.raw_groups += 4
    core.proj_groups += 4


def final_norm(core, gain_row, out_p, out_s, ctx):
    nc = core.nc
    y = core.sb("y", [P, 3, D], F32, ctx)
    ss = core.sb("f_ss", [P, 3], F32, ctx)
    u = core.norm_runs
    rows_ready = core.norm_sems[4]
    stored = core.sem("f_stored")
    with nc.Block() as block:
        @block.scalar
        def _(act):
            sum_squares(core, act, y, ss, u)

        @block.vector
        def _(dve):
            link = chain(dve, core.dve_chain)
            inverse_root(core, dve, link, y, ss, u)
            dve.wait_ge(core.gain_landed, 32)
            for t, (_, n) in enumerate(TILES):
                nc.vector.scalar_tensor_tensor(y[0:n, t, :], core.x_res[0:n, t, :], ss[0:n, t:t + 1], gain_row[0:n, :],
                                               ALU.mult, ALU.mult).then_inc(rows_ready, 1)

        @block.sync
        def _(sp):
            for t, (t0, n) in enumerate(TILES):
                sp.wait_ge(rows_ready, u * 3 + t + 1)
                dst = out_p[0, t0:t0 + n, :] if t < 2 else out_s.rearrange("b s d -> (b s) d")
                sp.dma_start(dst, y[0:n, t, :]).then_inc(stored, 16)
            sp.wait_ge(stored, 48)


def build(nc, w, out):
    with ExitStack() as ctx:
        core = Core(nc, ctx)
        core.x_res = core.sb("x_res", [P, 3, D])
        core.raw = core.sb("raw", [P, RAW, 2048])
        core.wg8 = core.sb("wg8", [P, KD, 32 + MH])
        core.x_landed = core.sem("x_landed")
        core.gates_landed = core.sem("gates_landed")
        core.gain_row = core.sb("gain_row", [P, D])
        core.gain_landed = core.sem("gain_landed")
        core.gcols_turned = core.sem("gcols_turned")
        core.gcols_ready = core.sem("gcols_ready")
        rows = nc.dram_tensor("ffn_rows", (NT, D), F32, kind="Internal").ap()
        ydram = nc.dram_tensor("expert_rows", (2 * NT, D), F32, kind="Internal").ap()
        constants(core, w)

        with ExitStack() as mix:
            pT = core.sb("pT", [P, NPT, NT], F32, mix)
            gates = core.sb("gates", [MH, 2, NT], F32, mix)
            mixT = core.sb("mixT", [P, KD, NT], F32, mix)
            with ExitStack() as s:
                hT = core.sb("hT", [P, KD, NT], F32, s)
                with ExitStack() as s2:
                    xn = core.sb("xn", [P, 3, D], F32, s2)
                    norm_stage(core, xn, hT, s2, gain_cols=core.gcols[:, 0:16])
                mix_project(core, w, hT, pT, gates)
                attention(core, w, out, hT, pT, mixT, s)
            with ExitStack() as s:
                mlstm(core, w, out, pT, mixT, gates, s)
            with ExitStack() as s:
                oT = core.sb("oT", [P, KD, NT], F32, s)
                out_project(core, w, mixT, oT)

        rt = {"slot": core.sb("slot", [P, SLOTS], F32), "ids": core.sb("ids", [P, 3, NE, 2], F32),
              "level": core.sb("level", [P, PASSES], F32), "wt": core.sb("wt_tok", [P, 2, 3], F32),
              "rank": core.sb("rank", [P, 3, NE], F32), "need": core.sb("need", [P, PASSES], F32)}
        core.pin, core.wp = core.sb("pin", [P, 3, PLE]), core.sb("wp", [P, 2, D])
        core.ple_loaded = core.sem("ple_inputs_loaded")
        with ExitStack() as s:
            xn = core.sb("xn2", [P, 3, D], F32, s)
            xT = core.sb("xT2", [P, KD, NT], F32, s)
            norm_stage(core, xn, xT, s, gain_row=core.gain_row, rows_out=rows)
            router(core, w, xT, rt, s)
        with ExitStack() as s:
            experts(core, w, rt, rows, ydram, s)
        with ExitStack() as s:
            pp = core.sb("pp", [P, KD, NT], F32, s)
            core.raw_landed = [core.sem(f"ple_landed{i}") for i in range(NCH)]
            core.landed_base = core.raw_groups
            with ExitStack() as s2:
                combine(core, w, rt, ydram, pp, s2)
            xn = core.sb("xn3", [P, 3, D], F32, s)
            xT = core.sb("xT3", [P, KD, NT], F32, s)
            norm_stage(core, xn, xT, s, gain_cols=core.gcols[:, 40:56])
            ple(core, w, xT, pp, s)
        with ExitStack() as s:
            final_norm(core, core.gain_row, out["y_prompt"], out["y_sample"], s)


_INS = ("x_prompt x_sample p_prompt p_sample state_mlstm_C state_mlstm_n state_mlstm_m state_swa_k state_swa_v "
        "g_mix w_in b_igate b_fgate g_mh attn_sinks w_out g_ffn w_router_g b_router_g w_router_e b_router_e "
        "w_gate w_up w_down g_ple w_ple_gate w_ple_proj g_final").split()
_STATE = {"C": (MH, DK, DK), "n": (MH, DK), "m": (MH,), "k": (WIN, KV, HD), "v": (WIN, KV, HD)}
_OUTS = {"y_prompt": (1, SEQ, D), "y_sample": (NS, 1, D),
         **{f"prompt_{n}": (1, 1, *s) for n, s in _STATE.items()},
         **{f"sample_{n}": (1, NS, *s) for n, s in _STATE.items()}}


def kernel(**inputs):
    import concourse.bacc as bacc
    from concourse.bass_utils import run_bass_kernel_spmd

    nc = bacc.Bacc("TRN2", target_bir_lowering=False, num_devices=1)
    arrays, w, out = {}, {}, {}
    for name in _INS:
        a = np.ascontiguousarray(inputs[name])
        arrays[f"in_{name}"] = a
        w[name] = nc.dram_tensor(f"in_{name}", a.shape, mybir.dt.from_np(a.dtype), kind="ExternalInput").ap()
    for name, shape in _OUTS.items():
        out[name] = nc.dram_tensor(f"out_{name}", shape, F32, kind="ExternalOutput").ap()
    build(nc, w, out)
    r = run_bass_kernel_spmd(nc, [arrays], core_ids=[0])
    return tuple(r.results[0][f"out_{name}"] for name in _OUTS)
```
